# Optimizing a Trainium2 kernel written in Bass

```python
import math
import jax, jax.numpy as jnp
from jax import lax
import numpy as np

D_MODEL = 1024
BATCH = 1
SEQ = 1024
DEPTH = 1

SSM_EXPAND = 2
SSM_D_INNER = SSM_EXPAND * D_MODEL
SSM_HEAD_DIM = 64
SSM_N_HEADS = SSM_D_INNER // SSM_HEAD_DIM
SSM_N_GROUPS = 8
SSM_D_STATE = 128
SSM_CONV = 5
SSM_CHUNK = 128
SSM_CONV_DIM = SSM_D_INNER + 2 * SSM_N_GROUPS * SSM_D_STATE
MLA_N_HEADS = 16
MLA_Q_RANK = 256
MLA_KV_RANK = 256
MLA_NOPE = 64
MLA_ROPE = 32
MLA_V = 64
MLA_QK = MLA_NOPE + MLA_ROPE
ROPE_BASE = 10000.0
ATTN_BLOCK = 128
D_FF = 4 * D_MODEL
N_BRANCHES = 2
EPS = 1e-6
IN_SPLITS = (SSM_D_INNER, SSM_CONV_DIM, 2 * SSM_N_HEADS, MLA_Q_RANK, MLA_KV_RANK, MLA_ROPE, N_BRANCHES * D_MODEL)
D_IN_PROJ = sum(IN_SPLITS)

kernel_name = "hybrid_bissd_mla_gated_sqrelu"

def rms_norm(x, w):
    xf = x.astype(jnp.float32)
    y = xf * lax.rsqrt(jnp.mean(xf * xf, axis=-1, keepdims=True) + EPS)
    return (y * w.astype(jnp.float32)).astype(x.dtype)

def split_cols(t, sizes):
    idx = [int(i) for i in np.cumsum(sizes)[:-1]]
    return jnp.split(t, idx, axis=-1)

def centred_depthwise_conv(x, w, b):
    y = lax.conv_general_dilated(
        x, w[:, None, :].astype(x.dtype), window_strides=(1,),
        padding=[(SSM_CONV // 2, SSM_CONV // 2)],
        dimension_numbers=("NWC", "WIO", "NWC"),
        feature_group_count=x.shape[-1])
    return y + b.astype(x.dtype)

def ssd_chunked(x, dt, a_coef, B, C):
    b, s, nh, p = x.shape
    g, n = B.shape[2], B.shape[3]
    hg = nh // g
    L = SSM_CHUNK
    c = s // L
    xs = (x * dt[..., None]).reshape(b, c, L, g, hg, p)
    la_cum = jnp.cumsum((dt * a_coef).reshape(b, c, L, g, hg), axis=2)
    Bc = B.reshape(b, c, L, g, n)
    Cc = C.reshape(b, c, L, g, n)
    lower = jnp.tril(jnp.ones((L, L), dtype=bool))[None, None, :, :, None, None]
    seg = la_cum[:, :, :, None] - la_cum[:, :, None, :]
    decay_ls = jnp.exp(jnp.where(lower, seg, -jnp.inf))
    cb = jnp.einsum('bclgn,bcsgn->bclsg', Cc, Bc)
    y_diag = jnp.einsum('bclsgh,bcsghp->bclghp', cb[..., None] * decay_ls, xs)
    decay_end = jnp.exp(la_cum[:, :, -1:] - la_cum)
    chunk_states = jnp.einsum('bcsgn,bcsghp->bcghpn', Bc, xs * decay_end[..., None])
    chunk_decay = jnp.exp(la_cum[:, :, -1])

    def step(state, inp):
        st, dec = inp
        return state * dec[..., None, None] + st, state

    init = jnp.zeros((b, g, hg, p, n), jnp.float32)
    _, prev = lax.scan(step, init, (jnp.moveaxis(chunk_states, 1, 0), jnp.moveaxis(chunk_decay, 1, 0)))
    prev = jnp.moveaxis(prev, 0, 1)
    y_off = jnp.einsum('bclgn,bcghpn->bclghp', Cc, prev) * jnp.exp(la_cum)[..., None]
    return (y_diag + y_off).reshape(b, s, nh, p)

def apply_rope(t, cos, sin):
    tf = t.astype(jnp.float32)
    t1, t2 = jnp.split(tf, 2, axis=-1)
    out = jnp.concatenate([t1 * cos - t2 * sin, t1 * sin + t2 * cos], axis=-1)
    return out.astype(t.dtype)

def block_attention(q, k, v):
    b, s, nh, dq = q.shape
    nb = s // ATTN_BLOCK
    qb = q.reshape(b, nb, ATTN_BLOCK, nh, dq).transpose(1, 0, 2, 3, 4)
    scale = dq ** -0.5

    def one_block(qblk):
        scores = jnp.einsum('bqhd,bkhd->bhqk', qblk, k).astype(jnp.float32) * scale
        probs = jax.nn.softmax(scores, axis=-1).astype(v.dtype)
        return jnp.einsum('bhqk,bkhd->bqhd', probs, v)

    out = lax.map(one_block, qb)
    return out.transpose(1, 0, 2, 3, 4).reshape(b, s, nh, v.shape[-1])

def setup_inputs(seed: int = 0) -> dict:
    key = jax.random.key(seed)
    ks = iter(jax.random.split(key, 40))
    f32 = jnp.float32
    Ly = DEPTH

    def nrm(shape, fan_in):
        return jax.random.normal(next(ks), shape, f32) * fan_in ** -0.5

    def gain(shape):
        return 1.0 + 0.05 * jax.random.normal(next(ks), shape, f32)

    def dt_bias(shape):
        dt0 = jnp.exp(jax.random.uniform(next(ks), shape, f32, minval=math.log(1e-3), maxval=math.log(1e-1)))
        return dt0 + jnp.log(-jnp.expm1(-dt0))

    def a_log(shape):
        return jnp.log(jax.random.uniform(next(ks), shape, f32, minval=1.0, maxval=16.0))

    x = jax.random.normal(next(ks), (BATCH, SEQ, D_MODEL), f32)
    positions = (jnp.arange(SEQ, dtype=jnp.int32)[None, :]
                 + jax.random.randint(next(ks), (BATCH, 1), 0, 4096, dtype=jnp.int32))
    return {
        "x": x,
        "positions": positions,
        "norm_mix_pre": gain((Ly, D_MODEL)),
        "w_in": nrm((Ly, D_MODEL, D_IN_PROJ), D_MODEL),
        "conv_w": nrm((Ly, SSM_CONV, SSM_CONV_DIM), SSM_CONV),
        "conv_b": 0.02 * jax.random.normal(next(ks), (Ly, SSM_CONV_DIM), f32),
        "dt_bias_fwd": dt_bias((Ly, SSM_N_HEADS)),
        "dt_bias_bwd": dt_bias((Ly, SSM_N_HEADS)),
        "a_log_fwd": a_log((Ly, SSM_N_HEADS)),
        "a_log_bwd": a_log((Ly, SSM_N_HEADS)),
        "d_skip": 1.0 + 0.1 * jax.random.normal(next(ks), (Ly, SSM_N_HEADS), f32),
        "ssm_norm_w": gain((Ly, SSM_D_INNER)),
        "w_ssm_out": nrm((Ly, SSM_D_INNER, D_MODEL), SSM_D_INNER),
        "q_a_norm": gain((Ly, MLA_Q_RANK)),
        "w_q_b": nrm((Ly, MLA_Q_RANK, MLA_N_HEADS * MLA_QK), MLA_Q_RANK),
        "kv_a_norm": gain((Ly, MLA_KV_RANK)),
        "w_kv_b": nrm((Ly, MLA_KV_RANK, MLA_N_HEADS * (MLA_NOPE + MLA_V)), MLA_KV_RANK),
        "w_mla_out": nrm((Ly, MLA_N_HEADS * MLA_V, D_MODEL), MLA_N_HEADS * MLA_V),
        "gate_b": 0.1 * jax.random.normal(next(ks), (Ly, N_BRANCHES * D_MODEL), f32),
        "w_out": nrm((Ly, D_MODEL, D_MODEL), D_MODEL),
        "norm_mix_post": gain((Ly, D_MODEL)),
        "norm_mlp_pre": gain((Ly, D_MODEL)),
        "w_up": nrm((Ly, D_MODEL, D_FF), D_MODEL),
        "w_down": nrm((Ly, D_FF, D_MODEL), D_FF),
        "norm_mlp_post": gain((Ly, D_MODEL)),
    }

def reference(x, positions, norm_mix_pre, w_in, conv_w, conv_b, dt_bias_fwd, dt_bias_bwd,
              a_log_fwd, a_log_bwd, d_skip, ssm_norm_w, w_ssm_out, q_a_norm, w_q_b,
              kv_a_norm, w_kv_b, w_mla_out, gate_b, w_out, norm_mix_post, norm_mlp_pre,
              w_up, w_down, norm_mlp_post):
    b, s, _ = x.shape
    f32 = jnp.float32
    inv_freq = ROPE_BASE ** (-jnp.arange(0, MLA_ROPE, 2, dtype=f32) / MLA_ROPE)
    ang = positions.astype(f32)[..., None] * inv_freq
    cos, sin = jnp.cos(ang), jnp.sin(ang)

    def flip(t):
        return jnp.flip(t, axis=1)

    for l in range(DEPTH):
        h = rms_norm(x, norm_mix_pre[l])
        proj = h @ w_in[l].astype(h.dtype)
        z, xbc, dt_raw, q_lat, kv_lat, k_rope, gate_lin = split_cols(proj, IN_SPLITS)

        xbc = jax.nn.silu(centred_depthwise_conv(xbc, conv_w[l], conv_b[l]))
        xs, Bm, Cm = split_cols(xbc, (SSM_D_INNER, SSM_N_GROUPS * SSM_D_STATE, SSM_N_GROUPS * SSM_D_STATE))
        xh = xs.reshape(b, s, SSM_N_HEADS, SSM_HEAD_DIM).astype(f32)
        Bm = Bm.reshape(b, s, SSM_N_GROUPS, SSM_D_STATE).astype(f32)
        Cm = Cm.reshape(b, s, SSM_N_GROUPS, SSM_D_STATE).astype(f32)
        dt_raw = dt_raw.astype(f32)
        dt_f = jax.nn.softplus(dt_raw[..., :SSM_N_HEADS] + dt_bias_fwd[l].astype(f32))
        dt_b = jax.nn.softplus(dt_raw[..., SSM_N_HEADS:] + dt_bias_bwd[l].astype(f32))
        a_f = -jnp.exp(a_log_fwd[l].astype(f32))
        a_b = -jnp.exp(a_log_bwd[l].astype(f32))
        y_f = ssd_chunked(xh, dt_f, a_f, Bm, Cm)
        y_b = flip(ssd_chunked(flip(xh), flip(dt_b), a_b, flip(Bm), flip(Cm)))
        y = y_f + y_b + d_skip[l].astype(f32)[:, None] * xh
        y = y.reshape(b, s, SSM_D_INNER) * jax.nn.silu(z.astype(f32))
        yg = y.reshape(b, s, SSM_N_GROUPS, SSM_D_INNER // SSM_N_GROUPS)
        yg = yg * lax.rsqrt(jnp.mean(yg * yg, axis=-1, keepdims=True) + EPS)
        y = (yg.reshape(b, s, SSM_D_INNER) * ssm_norm_w[l].astype(f32)).astype(x.dtype)
        y_ssm = y @ w_ssm_out[l].astype(y.dtype)

        q = (rms_norm(q_lat, q_a_norm[l]) @ w_q_b[l].astype(h.dtype)).reshape(b, s, MLA_N_HEADS, MLA_QK)
        q_nope, q_pe = jnp.split(q, [MLA_NOPE], axis=-1)
        kv = (rms_norm(kv_lat, kv_a_norm[l]) @ w_kv_b[l].astype(h.dtype)).reshape(b, s, MLA_N_HEADS, MLA_NOPE + MLA_V)
        k_nope, v = jnp.split(kv, [MLA_NOPE], axis=-1)
        q_pe = apply_rope(q_pe, cos[:, :, None, :], sin[:, :, None, :])
        k_pe = apply_rope(k_rope, cos, sin)
        q_full = jnp.concatenate([q_nope, q_pe], axis=-1)
        k_full = jnp.concatenate([k_nope, jnp.broadcast_to(k_pe[:, :, None, :], (b, s, MLA_N_HEADS, MLA_ROPE))], axis=-1)
        attn = block_attention(q_full, k_full, v).reshape(b, s, MLA_N_HEADS * MLA_V)
        y_mla = attn @ w_mla_out[l].astype(attn.dtype)

        gates = jax.nn.sigmoid(gate_lin + gate_b[l].astype(gate_lin.dtype))
        g_ssm, g_mla = jnp.split(gates, N_BRANCHES, axis=-1)
        mixed = (g_ssm * y_ssm + g_mla * y_mla) @ w_out[l].astype(x.dtype)
        x = x + rms_norm(mixed, norm_mix_post[l])

        hm = rms_norm(x, norm_mlp_pre[l])
        ff = jnp.square(jax.nn.relu(hm @ w_up[l].astype(hm.dtype))) @ w_down[l].astype(hm.dtype)
        x = x + rms_norm(ff, norm_mlp_post[l])
    return x


_drawn_inputs = setup_inputs


def setup_inputs(seed=0):
    import zlib

    import numpy as np

    out = dict(_drawn_inputs(seed))
    spreads = {}
    factors = {'q_a_norm': 8.0,
     'kv_a_norm': 8.0,
     'conv_b': 8.0,
     'dt_bias_fwd': 22.264,
     'dt_bias_bwd': 26.448,
     'a_log_fwd': 22.976,
     'a_log_bwd': 23.568,
     'd_skip': 8.0,
     'ssm_norm_w': 8.0}
    for name, (base, spread) in spreads.items():
        noise = np.random.default_rng([zlib.crc32(name.encode()), seed]).standard_normal(out[name].shape)
        drawn = base * np.exp(spread * noise) if base else spread * noise
        out[name] = __import__('jax').numpy.asarray(drawn.astype(out[name].dtype))
    for name, factor in factors.items():
        out[name] = (out[name] * factor).astype(out[name].dtype)
    return out
```

```python
import math
from contextlib import ExitStack

import numpy as np

import concourse.bass as bass
from concourse import mybir

F32 = mybir.dt.float32
F32R = mybir.dt.float32r
I32 = mybir.dt.int32
ACT = mybir.ActivationFunctionType
ALU = mybir.AluOpType
AX = mybir.AxisListType

P = 128
SEQ = 1024
D_MODEL = 1024
HALF = 512
NHALF = SEQ // HALF
TT = SEQ // P
KT = D_MODEL // P
EPS = 1e-6

D_INNER = 2048
HEADS = 32
HD = 64
GROUPS = 8
HPG = HEADS // GROUPS
GW = HPG * HD
N_STATE = 128
TAPS = 5
QR = 256
KVR = 256
ROPE = 32
NOPE = 64
VD = 64
A_HEADS = 16
QK = NOPE + ROPE
D_FF = 4096
SM_SCALE = float(QK) ** -0.5

ROUND = 1.5 * 2.0 ** 23
TWO_PI_1 = 6.28125
TWO_PI_2 = math.floor((2 * math.pi - TWO_PI_1) * 2 ** 20) / 2 ** 20
TWO_PI_3 = 2 * math.pi - TWO_PI_1 - TWO_PI_2
PI_F32 = 3.1415925

COL_Z = 0
COL_X = D_INNER
COL_B = COL_X + D_INNER
COL_C = COL_B + GROUPS * N_STATE
COL_DT = COL_C + GROUPS * N_STATE
COL_Q = COL_DT + 2 * HEADS
COL_KV = COL_Q + QR
COL_ROPE = COL_KV + KVR
COL_GATE = COL_ROPE + ROPE
D_IN = COL_GATE + 2 * D_MODEL

V_CONVW = 0
V_CONVB = V_CONVW + 32 * TAPS
V_GATEB = V_CONVB + 32
V_QN = V_GATEB + 16
V_KVN = V_QN + 2
V_DTB = V_KVN + 2
V_ALOG = V_DTB + 1
V_FREQ = V_ALOG + 1
V_SIGN = V_FREQ + 1
V_N = V_SIGN + 1

TOK_B = 0
TOK_X = GROUPS * N_STATE
TOK_Z = TOK_X + D_INNER
TOK_W = TOK_Z + D_INNER

U_LAT = 0
U_DT = 4
U_ROPE = 5
U_GATE = 6
U_C = U_GATE + 16
U_B = U_C + 8
U_X = U_B + 8
U_Z = U_X + 16
U_END = U_Z + 16


def unit_matmuls(pe, psum, w_hi, w_lo, act_hi, act_lo, kt=KT, start=True, stop=True):
    for k in range(kt):
        for n, (w, a) in enumerate(((w_hi, act_hi), (w_hi, act_lo), (w_lo, act_hi))):
            for h in range(NHALF):
                last = pe.matmul(psum[:, h * HALF:(h + 1) * HALF], w[:, k, :], a[:, k, h * HALF:(h + 1) * HALF],
                                 start=start and k == 0 and n == 0, stop=stop and k == kt - 1 and n == 2)
    return last


def pairs(engine, lo, hi, body):
    body(lo, True)
    if hi - lo > 1:
        with engine.Fori(lo + 1, hi) as i:
            body(i, False)


def stage_norm_in(nc, ap, keep, sem):
    with ExitStack() as ctx:
        def sb(name, shape, dt=F32):
            return ctx.enter_context(nc.sbuf_tensor(name, shape, dt))
        x_in = sb("n1_x", [P, 2, D_MODEL])
        squares = sb("n1_sq", [P, D_MODEL])
        wb = sb("n1_w", [P, D_MODEL])
        h = sb("n1_h", [P, 2, D_MODEL])
        sums = sb("n1_sums", [P, TT])
        means = sb("n1_means", [P, TT])
        roots = sb("n1_roots", [P, TT])
        rstd = sb("n1_rstd", [P, TT])
        pos = sb("rope_pos", [P, SEQ], I32)
        angle = sb("rope_angle", [P, SEQ])
        turns = sb("rope_turns", [P, SEQ])
        sin_full = sb("rope_sin", [P, SEQ])
        sin_half = sb("rope_half", [P, SEQ])
        turned = [ctx.enter_context(nc.psum_tensor(f"n1_turned{i}", [P, D_MODEL], F32)) for i in range(2)]
        x_loaded = [sem(f"n1_x_loaded{i}") for i in range(2)]
        vec_loaded, pos_loaded, ident_steps = sem("vectors_loaded"), sem("positions_loaded"), sem("ident_steps")
        sums_done, means_done, roots_done, rstd_done = sem("n1_sums"), sem("n1_means"), sem("n1_roots"), sem("n1_rstd")
        h_done, turned_done, hi_done, lo_done = sem("n1_h"), sem("n1_turned"), sem("n1_hi"), sem("n1_lo")
        rope_step, sines_done = sem("rope_steps"), sem("rope_sines")
        hT_hi, hT_lo, ident, vec, trig = keep["hT_hi"], keep["hT_lo"], keep["ident"], keep["vec"], keep["trig"]
        block = ctx.enter_context(nc.Block())

        @block.sync
        def _(sp):
            for t in range(2):
                sp.dma_start(x_in[:, t, :], ap["x"][t * P:(t + 1) * P, :]).then_inc(x_loaded[t], 16)
            sp.dma_start(wb[:], ap["norm_mix_pre"].partition_broadcast(P)).then_inc(vec_loaded, 16)
            sp.dma_start(vec[:], ap["vec"]).then_inc(vec_loaded, 16)
            sp.dma_start(pos[:], ap["positions"].partition_broadcast(P)).then_inc(pos_loaded, 16)
            with sp.Fori(1, TT // 2) as i:
                for u in range(2):
                    sp.wait_ge(h_done, 2 * i + u - 1)
                    sp.dma_start(x_in[:, u, :], ap["x"][bass.ds((2 * i + u) * P, P), :]).then_inc(x_loaded[u], 16)

        @block.gpsimd
        def _(pool):
            nc.gpsimd.memset(ident[:], 0.0).then_inc(ident_steps, 1)
            pool.wait_ge(ident_steps, 1)
            nc.gpsimd.affine_select(out=ident[:], in_=ident[:], compare_op=ALU.not_equal, fill=1.0, base=0,
                                    pattern=[[-1, P]], channel_multiplier=1).then_inc(ident_steps, 1)

        @block.scalar
        def _(act):
            def body(i, first):
                for u in range(2):
                    t = 2 * i + u
                    act.wait_ge(x_loaded[u], 16 * i + 16)
                    nc.scalar.activation(squares[:], x_in[:, u, :], ACT.Square,
                                         accum_out=sums[:, bass.ds(t, 1)]).then_inc(sums_done, 1)
                    act.wait_ge(means_done, t + 1)
                    nc.scalar.activation(roots[:, bass.ds(t, 1)], means[:, bass.ds(t, 1)], ACT.Sqrt).then_inc(roots_done, 1)
                    act.wait_ge(turned_done, t + 1)
                    nc.scalar.activation(hT_hi[:, :, bass.ds(t * P, P)], turned[u][:].rearrange("p (k t) -> p k t", k=KT),
                                         ACT.Copy).then_inc(hi_done, 1)
            pairs(act, 0, TT // 2, body)
            act.wait_ge(rope_step, 8)
            nc.scalar.activation(sin_full[:], angle[:], ACT.Sin).then_inc(sines_done, 1)
            act.wait_ge(rope_step, 9)
            nc.scalar.activation(sin_half[:], turns[:], ACT.Sin).then_inc(sines_done, 1)

        @block.vector
        def _(dve):
            dve.wait_ge(vec_loaded, 32)

            def body(i, first):
                for u in range(2):
                    t = 2 * i + u
                    dve.wait_ge(sums_done, t + 1)
                    nc.vector.tensor_scalar(means[:, bass.ds(t, 1)], sums[:, bass.ds(t, 1)], 1.0 / D_MODEL, EPS,
                                            ALU.mult, ALU.add).then_inc(means_done, 1)
                    dve.wait_ge(roots_done, t + 1)
                    nc.vector.reciprocal(rstd[:, bass.ds(t, 1)], roots[:, bass.ds(t, 1)]).then_inc(rstd_done, 1)
                    dve.wait_ge(rstd_done, t + 1)
                    dve.wait_ge(x_loaded[u], 16 * i + 16)
                    if not first:
                        dve.wait_ge(turned_done, t - 1)
                    nc.vector.scalar_tensor_tensor(out=h[:, u, :], in0=x_in[:, u, :], scalar=rstd[:, bass.ds(t, 1)],
                                                   in1=wb[:], op0=ALU.mult, op1=ALU.mult).then_inc(h_done, 1)
                    dve.wait_ge(hi_done, t + 1)
                    nc.vector.tensor_tensor(hT_lo[:, :, bass.ds(t * P, P)], turned[u][:].rearrange("p (k t) -> p k t", k=KT),
                                            hT_hi[:, :, bass.ds(t * P, P)].bitcast(F32), ALU.subtract).then_inc(lo_done, 1)
            pairs(dve, 0, TT // 2, body)
            dve.wait_ge(pos_loaded, 16)
            nc.vector.tensor_copy(sin_half[:], pos[:]).then_inc(rope_step, 1)
            dve.wait_ge(rope_step, 1)
            nc.vector.tensor_scalar(angle[:], sin_half[:], vec[:, V_FREQ:V_FREQ + 1], None, ALU.mult).then_inc(rope_step, 1)
            dve.wait_ge(rope_step, 2)
            nc.vector.tensor_scalar(turns[:], angle[:], 1.0 / (2 * math.pi), ROUND, ALU.mult, ALU.add).then_inc(rope_step, 1)
            dve.wait_ge(rope_step, 3)
            nc.vector.tensor_scalar(turns[:], turns[:], ROUND, None, ALU.subtract).then_inc(rope_step, 1)
            for n, part in enumerate((TWO_PI_1, TWO_PI_2, TWO_PI_3)):
                dve.wait_ge(rope_step, 4 + n)
                nc.vector.scalar_tensor_tensor(out=angle[:], in0=turns[:], scalar=-part, in1=angle[:],
                                               op0=ALU.mult, op1=ALU.add).then_inc(rope_step, 1)
            dve.wait_ge(rope_step, 7)
            nc.vector.tensor_scalar(angle[:], angle[:], PI_F32, -PI_F32, ALU.min, ALU.max).then_inc(rope_step, 1)
            dve.wait_ge(rope_step, 8)
            nc.vector.tensor_scalar(turns[:], angle[:], 0.5, None, ALU.mult).then_inc(rope_step, 1)
            dve.wait_ge(sines_done, 2)
            nc.vector.tensor_tensor(sin_half[:], sin_half[:], sin_half[:], ALU.mult).then_inc(rope_step, 1)
            dve.wait_ge(rope_step, 10)
            for q in (1, 3):
                s = slice(32 * q, 32 * q + 32)
                nc.vector.tensor_scalar(trig[s, :], sin_full[s, :], vec[s, V_SIGN:V_SIGN + 1], None, ALU.mult).then_inc(rope_step, 1)
            for q in (0, 2):
                s = slice(32 * q, 32 * q + 32)
                nc.vector.tensor_scalar(trig[s, :], sin_half[s, :], -2.0, 1.0, ALU.mult, ALU.add).then_inc(rope_step, 1)

        @block.tensor
        def _(pe):
            pe.wait_ge(ident_steps, 2)

            def body(i, first):
                for u in range(2):
                    t = 2 * i + u
                    pe.wait_ge(h_done, t + 1)
                    if not first:
                        pe.wait_ge(lo_done, t - 1)
                    for k in range(KT):
                        last = pe.transpose(turned[u][:, k * P:(k + 1) * P], h[:, u, k * P:(k + 1) * P], ident[:])
                    last.then_inc(turned_done, 1)
            pairs(pe, 0, TT // 2, body)


LOG1P_TERMS = 8


def stage_in_proj(nc, ap, keep, sem):
    with ExitStack() as ctx:
        def sb(name, shape, dt=F32):
            return ctx.enter_context(nc.sbuf_tensor(name, shape, dt))
        w_raw = [sb(f"w_raw{s}", [P, KT, P]) for s in range(2)]
        w_hi = [sb(f"w_hi{s}", [P, KT, P], F32R) for s in range(2)]
        w_lo = [sb(f"w_lo{s}", [P, KT, P], F32R) for s in range(2)]
        pad = [sb(f"conv_in{s}", [P, SEQ + TAPS - 1]) for s in range(2)]
        acc = [sb(f"conv_sum{s}", [P, SEQ]) for s in range(2)]
        feat = [sb(f"feature_major{s}", [P, SEQ]) for s in range(2)]
        tok = [sb(f"token_major{s}", [P, TT, P]) for s in range(2)]
        v, e, z, z2, q = (sb(f"dt_{n}", [2 * HEADS, SEQ]) for n in "vezsq")
        ends = sb("chunk_ends", [2 * HEADS, TT])
        a_exp = sb("a_exp", [2 * HEADS, 1])
        psum = [ctx.enter_context(nc.psum_tensor(f"proj{s}", [P, SEQ], F32)) for s in range(2)]
        turned = [ctx.enter_context(nc.psum_tensor(f"turned{s}", [P, SEQ], F32)) for s in range(2)]
        w_loaded = [sem(f"w_loaded{s}") for s in range(2)]
        hi_done, lo_done, mm_done, psum_free = sem("w_hi_done"), sem("w_lo_done"), sem("proj_done"), sem("proj_read")
        pad_zeroed, conv_step, feat_done = sem("conv_pads_zeroed"), sem("conv_steps"), sem("feature_major_done")
        turned_done, tok_done = sem("turned"), sem("token_major_done")
        feat_stored = [sem(f"feature_major_stored{s}") for s in range(2)]
        tok_stored = [sem(f"token_major_stored{s}") for s in range(2)]
        dt_in, dt_step, la_stored = sem("dt_inputs"), sem("dt_steps"), sem("decays_stored")
        small_turned, rope_k = sem("dt_turned"), sem("rope_key_steps")
        hT_hi, hT_lo, ident, vec, trig = keep["hT_hi"], keep["hT_lo"], keep["ident"], keep["vec"], keep["trig"]
        lat, kpe, kraw = keep["lat"], keep["kpe"], keep["kraw"]
        krot, chain = acc[0], acc[1]
        dt_tok, la_tok = keep["dt_tok"], keep["la_tok"]
        dt_last = 4 + LOG1P_TERMS + 11
        block = ctx.enter_context(nc.Block())

        def column(n, first_unit, first_column):
            return bass.ds((n - first_unit) * P + first_column, P)

        @block.sync
        def _(sp):
            def load(n, s, cols, wait=True):
                if wait:
                    sp.wait_ge(lo_done, n - 1)
                sp.dma_start(w_raw[s][:], ap["w_in"][:, cols].rearrange("(k p) c -> p k c", p=P)).then_inc(w_loaded[s], 16)

            for n in range(U_ROPE):
                load(n, n % 2, bass.ds(COL_Q + n * P if n < U_DT else COL_DT, P), wait=n >= 2)
            sp.wait_ge(lo_done, U_ROPE - 1)
            sp.dma_start(w_raw[1][:], ap["w_rope"].rearrange("(k p) c -> p k c", p=P)).then_inc(w_loaded[1], 16)
            for first_unit, end, first_column in ((U_GATE, U_C, COL_GATE), (U_C, U_B, COL_C), (U_B, U_X, COL_B),
                                                  (U_X, U_Z, COL_X), (U_Z, U_END, COL_Z)):
                with sp.Fori(first_unit // 2, end // 2) as i:
                    for u in range(2):
                        load(2 * i + u, u, column(2 * i + u, first_unit, first_column))

        @block.gpsimd
        def _(pool):
            for s in range(2):
                for side in (slice(0, 2), slice(SEQ + 2, SEQ + 4)):
                    nc.gpsimd.memset(pad[s][:, side], 0.0).then_inc(pad_zeroed, 1)

            def store_feat(n, s, dram, first_unit):
                pool.wait_ge(feat_done, n - U_GATE + 1)
                pool.dma_start(dram[bass.ds((n - first_unit) * P, P), :], feat[s][:]).then_inc(feat_stored[s], 16)

            def store_tok(n, s):
                pool.wait_ge(tok_done, n - U_B + 1)
                pool.dma_start(ap["tok"][:, bass.ds((n - U_B) * P, P)].rearrange("(t p) c -> p t c", p=P),
                               tok[s][:]).then_inc(tok_stored[s], 16)

            for first_unit, end, dram in ((U_GATE, U_C, ap["gates"]), (U_C, U_B, ap["CT"])):
                with pool.Fori(first_unit // 2, end // 2) as i:
                    for u in range(2):
                        store_feat(2 * i + u, u, dram, first_unit)
            with pool.Fori(U_B // 2, U_X // 2) as i:
                for u in range(2):
                    store_feat(2 * i + u, u, ap["BT"], U_B)
                    store_tok(2 * i + u, u)
            with pool.Fori(U_X // 2, U_END // 2) as i:
                for u in range(2):
                    store_tok(2 * i + u, u)
            pool.wait_ge(dt_step, dt_last)
            pool.dma_start(ap["la"], q[:]).then_inc(la_stored, 16)
            pool.dma_start(ap["ends"], ends[:]).then_inc(la_stored, 16)
            for s in range(2):
                pool.wait_ge(feat_stored[s], 16 * ((U_X - U_GATE) // 2))
                pool.wait_ge(tok_stored[s], 16 * ((U_END - U_B) // 2))
            pool.wait_ge(la_stored, 32)

        @block.scalar
        def _(act):
            def split_hi(n, s, i):
                act.wait_ge(w_loaded[s], 16 * i + 16)
                if not isinstance(n, int) or n >= 2:
                    act.wait_ge(mm_done, n - 1)
                nc.scalar.activation(w_hi[s][:], w_raw[s][:], ACT.Copy).then_inc(hi_done, 1)

            def split_next(i, u):
                split_hi(2 * i + u + 1, 1 - u, i + u)

            def product(i, u):
                act.wait_ge(mm_done, 2 * i + u + 1)

            def tok_copy(i, u):
                n = 2 * i + u
                act.wait_ge(turned_done, n - U_B + 1)
                if not isinstance(i, int) or i > U_B // 2:
                    act.wait_ge(tok_stored[u], 16 * (i - U_B // 2))
                nc.scalar.activation(tok[u][:], turned[u][:].rearrange("p (t c) -> p t c", t=TT), ACT.Copy).then_inc(tok_done, 1)

            def tok_copy_before(i, u):
                tok_copy(i - 1 + u, 1 - u)

            def feat_store_over(i, u):
                act.wait_ge(feat_stored[u], 16 * (i - U_GATE // 2))

            split_hi(0, 0, 0)
            for n in range(U_GATE):
                split_next(n // 2, n % 2)
                product(n // 2, n % 2)
                source = psum[n % 2]
                if n < U_DT:
                    nc.scalar.activation(lat[:, n, :], source[:], ACT.Copy).then_inc(psum_free, 1)
                elif n == U_DT:
                    nc.scalar.activation(v[:], source[0:2 * HEADS, :], ACT.Identity,
                                         bias=vec[0:2 * HEADS, V_DTB:V_DTB + 1]).then_inc(psum_free, 1)
                else:
                    nc.scalar.activation(kraw[:], source[0:2 * ROPE, :], ACT.Copy).then_inc(psum_free, 1)
            act.wait_ge(psum_free, U_DT + 1)
            nc.scalar.activation(e[:], v[:], ACT.Abs).then_inc(dt_in, 1)
            act.wait_ge(dt_in, 1)
            nc.scalar.activation(z[:], e[:], ACT.Exp, scale=-1.0).then_inc(dt_in, 1)
            nc.scalar.activation(a_exp[:], vec[0:2 * HEADS, V_ALOG:V_ALOG + 1], ACT.Exp).then_inc(dt_in, 1)

            def gates(i, first):
                for u in range(2):
                    split_next(i, u)
                    product(i, u)
                    if not first:
                        feat_store_over(i, u)
                    nc.scalar.activation(feat[u][:], psum[u][:], ACT.Sigmoid,
                                         bias=vec[:, bass.ds(2 * i + u - U_GATE + V_GATEB, 1)]).then_inc(feat_done, 1)
            pairs(act, U_GATE // 2, U_C // 2, gates)

            def conv_c(i, first):
                for u in range(2):
                    split_next(i, u)
                    product(i, u)
                    if not first:
                        act.wait_ge(conv_step, TAPS * (2 * i + u - U_C - 1))
                    nc.scalar.activation(pad[u][:, 2:2 + SEQ], psum[u][:], ACT.Copy).then_inc(psum_free, 1)
                    feat_store_over(i, u)
                    act.wait_ge(conv_step, TAPS * (2 * i + u - U_C + 1))
                    nc.scalar.activation(feat[u][:], acc[u][:], ACT.Silu).then_inc(feat_done, 1)
            act.wait_ge(pad_zeroed, 4)
            pairs(act, U_C // 2, U_B // 2, conv_c)

            def conv_b(i, first):
                for u in range(2):
                    split_next(i, u)
                    product(i, u)
                    act.wait_ge(conv_step, TAPS * (2 * i + u - U_C - 1))
                    nc.scalar.activation(pad[u][:, 2:2 + SEQ], psum[u][:], ACT.Copy).then_inc(psum_free, 1)
                    if not (first and u == 0):
                        tok_copy_before(i, u)
                    feat_store_over(i, u)
                    if not first:
                        act.wait_ge(turned_done, 2 * i + u - 1 - U_B)
                    act.wait_ge(conv_step, TAPS * (2 * i + u - U_C + 1))
                    nc.scalar.activation(feat[u][:], acc[u][:], ACT.Silu).then_inc(feat_done, 1)
            conv_b(U_B // 2, True)
            conv_b(U_B // 2 + 1, False)
            with act.Fori(U_B // 2 + 2, U_X // 2) as i:
                conv_b(i, False)

            def conv_x(i, first):
                for u in range(2):
                    split_next(i, u)
                    product(i, u)
                    act.wait_ge(conv_step, TAPS * (2 * i + u - U_C - 1))
                    nc.scalar.activation(pad[u][:, 2:2 + SEQ], psum[u][:], ACT.Copy).then_inc(psum_free, 1)
                    tok_copy_before(i, u)
                    if first:
                        act.wait_ge(feat_stored[u], 16 * ((U_X - U_GATE) // 2))
                    act.wait_ge(turned_done, 2 * i + u - 1 - U_B)
                    act.wait_ge(conv_step, TAPS * (2 * i + u - U_C + 1))
                    nc.scalar.activation(feat[u][:], acc[u][:], ACT.Silu).then_inc(feat_done, 1)
            pairs(act, U_X // 2, U_Z // 2, conv_x)

            def silu_z(i, first):
                for u in range(2):
                    if not (isinstance(i, int) and 2 * i + u == U_END - 1):
                        split_next(i, u)
                    product(i, u)
                    tok_copy_before(i, u)
                    act.wait_ge(turned_done, 2 * i + u - 1 - U_B)
                    nc.scalar.activation(feat[u][:], psum[u][:], ACT.Silu).then_inc(feat_done, 1)
            with act.Fori(U_Z // 2, U_END // 2 - 1) as i:
                silu_z(i, False)
            silu_z(U_END // 2 - 1, False)
            tok_copy(U_END // 2 - 1, 1)
            for n, dst in enumerate((dt_tok, la_tok)):
                act.wait_ge(small_turned, n + 1)
                nc.scalar.activation(dst[:], turned[n][:, 0:TT * 2 * HEADS], ACT.Copy).then_inc(tok_done, 1)

        @block.vector
        def _(dve):
            def split_lo(n, s):
                dve.wait_ge(hi_done, n + 1)
                nc.vector.tensor_tensor(w_lo[s][:], w_raw[s][:], w_hi[s][:].bitcast(F32), ALU.subtract).then_inc(lo_done, 1)

            def split_next(i, u):
                split_lo(2 * i + u + 1, 1 - u)

            split_lo(0, 0)
            for n in range(U_GATE):
                split_next(n // 2, n % 2)

            def softplus_1():
                dve.wait_ge(dt_in, 3)
                nc.vector.tensor_scalar(e[:], z[:], 2.0, None, ALU.add).then_inc(dt_step, 1)
                dve.wait_ge(dt_step, 1)
                nc.vector.reciprocal(q[:], e[:]).then_inc(dt_step, 1)

            def softplus_2():
                dve.wait_ge(dt_step, 2)
                nc.vector.tensor_tensor(z[:], z[:], q[:], ALU.mult).then_inc(dt_step, 1)
                dve.wait_ge(dt_step, 3)
                nc.vector.tensor_tensor(z2[:], z[:], z[:], ALU.mult).then_inc(dt_step, 1)
                dve.wait_ge(dt_step, 4)
                nc.vector.tensor_scalar(q[:], z2[:], 1.0 / (2 * LOG1P_TERMS + 1), None, ALU.mult).then_inc(dt_step, 1)
                for k in range(LOG1P_TERMS - 1):
                    dve.wait_ge(dt_step, 5 + k)
                    nc.vector.scalar_tensor_tensor(out=q[:], in0=q[:], scalar=1.0 / (2 * (LOG1P_TERMS - k) - 1), in1=z2[:],
                                                   op0=ALU.add, op1=ALU.mult).then_inc(dt_step, 1)

            def softplus_3():
                n = 4 + LOG1P_TERMS
                dve.wait_ge(dt_step, n)
                nc.vector.scalar_tensor_tensor(out=q[:], in0=q[:], scalar=1.0, in1=z[:], op0=ALU.add, op1=ALU.mult).then_inc(dt_step, 1)
                nc.vector.tensor_scalar(e[:], v[:], 0.0, None, ALU.max).then_inc(dt_step, 1)
                dve.wait_ge(dt_step, n + 2)
                nc.vector.scalar_tensor_tensor(out=v[:], in0=q[:], scalar=2.0, in1=e[:], op0=ALU.mult, op1=ALU.add).then_inc(dt_step, 1)
                dve.wait_ge(dt_step, n + 3)
                nc.vector.tensor_scalar(z[:], v[:], a_exp[:], -1.0, ALU.mult, ALU.mult).then_inc(dt_step, 1)
                nc.vector.memset(chain[0:2 * HEADS, :], 1.0).then_inc(dt_step, 1)
                dve.wait_ge(dt_step, n + 5)
                nc.vector.memset(chain[0:HEADS, :].rearrange("p (c t) -> p c t", t=P)[:, :, 0], 0.0).then_inc(dt_step, 1)
                nc.vector.memset(chain[HEADS:2 * HEADS, :].rearrange("p (c t) -> p c t", t=P)[:, :, P - 1], 0.0).then_inc(dt_step, 1)
                dve.wait_ge(dt_step, n + 7)
                nc.vector.tensor_tensor_scan(q[0:HEADS, :], chain[0:HEADS, :], z[0:HEADS, :], 0.0, ALU.mult, ALU.add).then_inc(dt_step, 1)
                nc.vector.tensor_tensor_scan(q[HEADS:, ::-1], chain[HEADS:2 * HEADS, ::-1], z[HEADS:, ::-1], 0.0,
                                             ALU.mult, ALU.add).then_inc(dt_step, 1)
                dve.wait_ge(dt_step, n + 9)
                for rows, at in ((slice(0, HEADS), P - 1), (slice(HEADS, 2 * HEADS), 0)):
                    nc.vector.tensor_copy(ends[rows, :], q[rows, :].rearrange("p (c t) -> p c t", t=P)[:, :, at]).then_inc(dt_step, 1)

            def rope_key():
                out = slice(2 * ROPE, 3 * ROPE)
                dve.wait_ge(psum_free, U_ROPE + 1)
                nc.vector.tensor_tensor(kpe[out, :], kraw[0:ROPE, :], trig[0:ROPE, :], ALU.mult).then_inc(rope_k, 1)
                nc.vector.tensor_tensor(krot[out, :], kraw[ROPE:2 * ROPE, :], trig[ROPE:2 * ROPE, :], ALU.mult).then_inc(rope_k, 1)
                dve.wait_ge(rope_k, 2)
                nc.vector.tensor_tensor(kpe[out, :], kpe[out, :], krot[out, :], ALU.add).then_inc(rope_k, 1)

            for n, part in enumerate((softplus_1, softplus_2, softplus_3, rope_key)):
                split_next((U_GATE + n) // 2, (U_GATE + n) % 2)
                part()
            with dve.Fori(U_GATE // 2 + 2, U_C // 2) as i:
                for u in range(2):
                    split_next(i, u)

            def conv(first_unit, first_tile):
                def body(i, first):
                    for u in range(2):
                        split_next(i, u)
                        n = 2 * i + u
                        tile = n - first_unit + first_tile
                        step = TAPS * (n - U_C)
                        dve.wait_ge(psum_free, n - U_C + U_GATE + 1)
                        if not first:
                            dve.wait_ge(feat_done, n - 1 - U_GATE)
                        nc.vector.tensor_scalar(acc[u][:], pad[u][:, 0:SEQ], vec[:, bass.ds(tile * TAPS + V_CONVW, 1)],
                                                vec[:, bass.ds(tile + V_CONVB, 1)], ALU.mult, ALU.add).then_inc(conv_step, 1)
                        for k in range(1, TAPS):
                            dve.wait_ge(conv_step, step + k)
                            nc.vector.scalar_tensor_tensor(out=acc[u][:], in0=pad[u][:, k:k + SEQ],
                                                           scalar=vec[:, bass.ds(tile * TAPS + V_CONVW + k, 1)], in1=acc[u][:],
                                                           op0=ALU.mult, op1=ALU.add).then_inc(conv_step, 1)
                return body
            dve.wait_ge(pad_zeroed, 4)
            pairs(dve, U_C // 2, U_B // 2, conv(U_C, 24))
            for first_unit, end, tile in ((U_B, U_X, 16), (U_X, U_Z, 0)):
                with dve.Fori(first_unit // 2, end // 2) as i:
                    conv(first_unit, tile)(i, False)
            with dve.Fori(U_Z // 2, U_END // 2 - 1) as i:
                for u in range(2):
                    split_next(i, u)
            split_next(U_END // 2 - 1, 0)

        @block.tensor
        def _(pe):
            def multiply(i, u):
                pe.wait_ge(lo_done, 2 * i + u + 1)
                unit_matmuls(pe, psum[u], w_hi[u], w_lo[u], hT_hi, hT_lo).then_inc(mm_done, 1)

            def turn(i, u):
                n = 2 * i + u
                pe.wait_ge(feat_done, n - U_GATE + 1)
                if not isinstance(i, int) or i > U_B // 2:
                    pe.wait_ge(tok_done, n - 1 - U_B)
                for t in range(TT):
                    last = pe.transpose(turned[u][:, t * P:(t + 1) * P], feat[u][:, t * P:(t + 1) * P], ident[:])
                last.then_inc(turned_done, 1)

            def turn_before(i, u):
                turn(i - 1 + u, 1 - u)

            for n in range(U_GATE):
                if n >= 2:
                    pe.wait_ge(psum_free, n - 1)
                multiply(n // 2, n % 2)

            def gates(i, first):
                for u in range(2):
                    n = 2 * i + u
                    if first:
                        pe.wait_ge(psum_free, n - 1)
                    else:
                        pe.wait_ge(feat_done, n - 1 - U_GATE)
                    multiply(i, u)
            pairs(pe, U_GATE // 2, U_C // 2, gates)

            def conv_c(i, first):
                for u in range(2):
                    n = 2 * i + u
                    if first:
                        pe.wait_ge(feat_done, n - 1 - U_GATE)
                    else:
                        pe.wait_ge(psum_free, n - 1 - U_C + U_GATE)
                    multiply(i, u)
            pairs(pe, U_C // 2, U_B // 2, conv_c)

            def conv_turned(i, first):
                for u in range(2):
                    pe.wait_ge(psum_free, 2 * i + u - 1 - U_C + U_GATE)
                    multiply(i, u)
                    if not (first and u == 0):
                        turn_before(i, u)
            conv_turned(U_B // 2, True)
            conv_turned(U_B // 2 + 1, False)
            with pe.Fori(U_B // 2 + 2, U_Z // 2) as i:
                conv_turned(i, False)

            def silu_z(i, first):
                for u in range(2):
                    n = 2 * i + u
                    if first:
                        pe.wait_ge(psum_free, n - 1 - U_C + U_GATE)
                    else:
                        pe.wait_ge(feat_done, n - 1 - U_GATE)
                    multiply(i, u)
                    turn_before(i, u)
            pairs(pe, U_Z // 2, U_END // 2, silu_z)
            turn(U_END // 2 - 1, 1)
            pe.wait_ge(dt_step, dt_last)
            pe.wait_ge(tok_done, U_END - U_B)
            for n, src in enumerate((v, q)):
                for t in range(TT):
                    last = pe.transpose(turned[n][:, t * 2 * HEADS:(t + 1) * 2 * HEADS], src[:, t * P:(t + 1) * P],
                                        ident[0:2 * HEADS, 0:2 * HEADS])
                last.then_inc(small_turned, 1)


STATES = 2 * (TT - 1)
SLOT = HPG * HD


def stage_ssd(nc, ap, keep, sem):
    with ExitStack() as ctx:
        def sb(name, shape, dt=F32):
            return ctx.enter_context(nc.sbuf_tensor(name, shape, dt))

        def two(name, shape, dt=F32):
            return [sb(f"{name}{s}", shape, dt) for s in range(2)]

        def ps(name, shape):
            return [ctx.enter_context(nc.psum_tensor(f"{name}{s}", shape, F32)) for s in range(2)]
        bc_raw = two("bc_raw", [P, 2, SEQ])
        b_raw = two("b_raw", [P, TT, N_STATE])
        x_raw = two("x_raw", [P, TT, SLOT])
        decay_in = two("decay_in", [P, 2, HPG, P])
        ends = sb("ends", [P, 2 * HEADS * TT])
        end_exp = sb("end_exp", [P, 2 * HEADS * TT])
        state_w = sb("state_w", [P, TT * 2 * HEADS])
        la_exp = sb("la_exp", [P, TT * 2 * HEADS])
        masks = sb("masks", [P, 2, P])
        d_all = sb("d_all", [P, HEADS])
        d_wide = [sb(f"d_wide{s}", [P, HPG, HD]) for s in range(2)]
        xs_raw = two("xs_raw", [P, SLOT])
        xs_hi, xs_lo = two("xs_hi", [P, SLOT], F32R), two("xs_lo", [P, SLOT], F32R)
        sb_hi, sb_lo = two("state_b_hi", [P, N_STATE], F32R), two("state_b_lo", [P, N_STATE], F32R)
        prev = sb("prev", [P, TT, 2, SLOT])
        decayed = two("decayed", [P, SLOT])
        bc_hi, bc_lo = two("bc_hi", [P, 2, P], F32R), two("bc_lo", [P, 2, P], F32R)
        x_hi, x_lo = two("x_hi", [P, SLOT], F32R), two("x_lo", [P, SLOT], F32R)
        prev_hi, prev_lo = two("prev_hi", [P, 2 * SLOT], F32R), two("prev_lo", [P, 2 * SLOT], F32R)
        cb_masked = two("cb_masked", [P, 2, P])
        decay = two("decay", [P, 2, HPG, P])
        m_raw = two("m_raw", [P, HPG, P])
        m_hi, m_lo = two("m_hi", [P, HPG, P], F32R), two("m_lo", [P, HPG, P], F32R)
        y_off = two("y_off", [P, 2, SLOT])
        y_sum = two("y_sum", [P, SLOT])
        y_skip = two("y_skip", [P, SLOT])
        y_out = two("y_out", [P, SLOT])
        ps_state, ps_cb, ps_off, ps_diag = ps("ps_state", [P, HALF]), ps("ps_cb", [P, HALF]), ps("ps_off", [P, HALF]), ps("ps_diag", [P, HALF])
        la_tok, dt_tok = keep["la_tok"], keep["dt_tok"]

        raw_loaded = [sem(f"ssd_raw_loaded{s}") for s in range(2)]
        decay_loaded = [sem(f"decay_loaded{s}") for s in range(2)]
        table_loaded, table_done, masks_made = sem("ssd_tables_loaded"), sem("ssd_tables"), sem("masks_made")
        xs_done, state_hi, state_lo, state_mm = sem("xs_done"), sem("state_hi"), sem("state_lo"), sem("state_mm")
        decayed_done, state_done = sem("state_decayed"), sem("state_done")
        in_hi, in_lo, seg_done, exp_done = sem("ssd_in_hi"), sem("ssd_in_lo"), sem("seg_done"), sem("decay_exp")
        cb_mm, cb_done, weighted, m_sum = sem("cb_mm"), sem("cb_masked"), sem("decay_weighted"), sem("m_sum")
        mhi_done, mlo_done, off_mm, diag_mm = sem("m_hi_done"), sem("m_lo_done"), sem("y_off_mm"), sem("y_diag_mm")
        off_done, sum_done, skip_done, y_step = sem("y_off_done"), sem("y_sum_done"), sem("y_skip_done"), sem("y_out_steps")
        y_stored = [sem(f"y_stored{s}") for s in range(2)]
        state_zero, d_spread = sem("states_zeroed"), sem("d_skip_spread")
        block = ctx.enter_context(nc.Block())

        def per_token(table, c, g, first, dirs=2):
            v = table[:].rearrange("p (c d h) -> p c d h", c=TT, d=2)[:, c, first:first + dirs, bass.ds(g * HPG, HPG)]
            return v.unsqueeze(3).to_broadcast([P, dirs, HPG, HD])

        def heads(t, dirs):
            return t.rearrange("p (d h e) -> p d h e", d=dirs, h=HPG)

        def chunk_of(k):
            return (TT - 1 - k, 1, TT - 2 - k) if k < TT - 1 else (k - (TT - 1), 0, k - (TT - 1) + 1)

        @block.sync
        def _(sp):
            sp.dma_start(ends[:], ap["ends"].rearrange("h c -> (h c)").partition_broadcast(P)).then_inc(table_loaded, 16)
            sp.dma_start(d_all[:], ap["d_skip"].partition_broadcast(P)).then_inc(table_loaded, 16)

            def load_raw(g, G):
                sp.dma_start(bc_raw[G][:, 0, :], ap["BT"][bass.ds(g * P, P), :]).then_inc(raw_loaded[G], 16)
                sp.dma_start(bc_raw[G][:, 1, :], ap["CT"][bass.ds(g * P, P), :]).then_inc(raw_loaded[G], 16)
                tok = ap["tok"].rearrange("(c p) f -> p c f", p=P)
                sp.dma_start(b_raw[G][:], tok[:, :, bass.ds(g * P + TOK_B, P)]).then_inc(raw_loaded[G], 16)
                sp.dma_start(x_raw[G][:], tok[:, :, bass.ds(g * SLOT + TOK_X, SLOT)]).then_inc(raw_loaded[G], 16)
            load_raw(0, 0)
            load_raw(1, 1)
            la = ap["la"].rearrange("(d h) t -> d h t", d=2)

            def body(i, first):
                for G in range(2):
                    g = 2 * i + G
                    for c in range(TT):
                        s = c % 2
                        if not (first and G == 0 and c < 2):
                            sp.wait_ge(seg_done, TT * g + c - 1)
                        for d in range(2):
                            sp.dma_start(decay_in[s][:, d], la[d, bass.ds(g * HPG, HPG), c * P:(c + 1) * P]
                                         .partition_broadcast(P)).then_inc(decay_loaded[s], 16)
                    if not isinstance(i, int) or i < GROUPS // 2 - 1:
                        sp.wait_ge(y_step, 2 * TT * (g + 1))
                        load_raw(g + 2, G)
            body(0, True)
            with sp.Fori(1, GROUPS // 2 - 1) as i:
                body(i, False)
            body(GROUPS // 2 - 1, False)

        @block.gpsimd
        def _(pool):
            nc.gpsimd.memset(masks[:], 1.0).then_inc(masks_made, 1)
            pool.wait_ge(masks_made, 1)
            for d, (a, b) in enumerate(((1, -1), (-1, 1))):
                nc.gpsimd.affine_select(out=masks[:, d, :], in_=masks[:, d, :], compare_op=ALU.is_ge, fill=0.0, base=0,
                                        pattern=[[a, P]], channel_multiplier=b).then_inc(masks_made, 1)
            pool.wait_ge(table_loaded, 32)

            def body(i, first):
                for G in range(2):
                    g = 2 * i + G
                    for c in range(TT):
                        s, m = c % 2, TT * g + c
                        fresh = first and G == 0 and c < 2
                        if c == 0:
                            pool.wait_ge(raw_loaded[G], 64 * i + 64)
                            d_here = d_all[:, bass.ds(g * HPG, HPG)].unsqueeze(2).to_broadcast([P, HPG, HD])
                            nc.gpsimd.tensor_copy(d_wide[G][:], d_here).then_inc(d_spread, 1)
                            pool.wait_ge(d_spread, g + 1)
                        if not fresh:
                            pool.wait_ge(y_step, 2 * m - 2)
                        nc.gpsimd.tensor_tensor(y_skip[s][:].rearrange("p (h e) -> p h e", h=HPG),
                                                x_raw[G][:, c, :].rearrange("p (h e) -> p h e", h=HPG), d_wide[G][:],
                                                ALU.mult).then_inc(skip_done, 1)
                        pool.wait_ge(weighted, m + 1)
                        if not fresh:
                            pool.wait_ge(mlo_done, m - 1)
                        nc.gpsimd.tensor_tensor(m_raw[s][:], decay[s][:, 0], decay[s][:, 1], ALU.add).then_inc(m_sum, 1)
                        pool.wait_ge(sum_done, m + 1)
                        pool.wait_ge(skip_done, m + 1)
                        if not fresh:
                            pool.wait_ge(y_stored[s], 16 * ((TT // 2) * g + c // 2))
                        nc.gpsimd.tensor_tensor(y_out[s][:], y_sum[s][:], y_off[s][:, 1], ALU.add).then_inc(y_step, 1)
                        pool.wait_ge(y_step, 2 * m + 1)
                        nc.gpsimd.tensor_tensor(y_out[s][:], y_out[s][:], y_skip[s][:], ALU.add).then_inc(y_step, 1)
                        pool.wait_ge(y_step, 2 * m + 2)
                        pool.dma_start(ap["y"][c * P:(c + 1) * P, bass.ds(g * SLOT, SLOT)], y_out[s][:]).then_inc(y_stored[s], 16)
            pairs(pool, 0, GROUPS // 2, body)
            for s in range(2):
                pool.wait_ge(y_stored[s], 16 * (TT // 2) * GROUPS)

        @block.scalar
        def _(act):
            act.wait_ge(table_loaded, 32)
            nc.scalar.activation(end_exp[:], ends[:], ACT.Exp).then_inc(table_done, 1)
            nc.scalar.activation(la_exp[:], la_tok[:], ACT.Exp).then_inc(table_done, 1)
            act.wait_ge(table_done, 3)
            nc.scalar.activation(state_w[:], state_w[:], ACT.Exp).then_inc(table_done, 1)

            def state_step(g, G, i, k, first):
                c, s = chunk_of(k)[0], k % 2
                act.wait_ge(xs_done, STATES * g + k + 1)
                if not (first and G == 0 and k < 2):
                    act.wait_ge(state_mm, STATES * g + k - 1)
                nc.scalar.activation(sb_hi[s][:], b_raw[G][:, c, :], ACT.Copy)
                nc.scalar.activation(xs_hi[s][:], xs_raw[s][:], ACT.Copy).then_inc(state_hi, 1)

            def m_split(g, G, c):
                s, m = c % 2, TT * g + c
                act.wait_ge(m_sum, m + 1)
                if not isinstance(g, int) or m >= 2:
                    act.wait_ge(diag_mm, m - 1)
                nc.scalar.activation(m_hi[s][:], m_raw[s][:], ACT.Copy).then_inc(mhi_done, 1)

            def body(i, first):
                for G in range(2):
                    g = 2 * i + G
                    act.wait_ge(raw_loaded[G], 64 * i + 64)
                    for k in range(TT - 1):
                        state_step(g, G, i, k, first)
                    for c in range(TT):
                        s, m = c % 2, TT * g + c
                        if not (first and G == 0 and c < 2):
                            act.wait_ge(diag_mm, m - 1)
                            act.wait_ge(off_mm, m - 1)
                        nc.scalar.activation(bc_hi[s][:], bc_raw[G][:, :, c * P:(c + 1) * P], ACT.Copy)
                        nc.scalar.activation(x_hi[s][:], x_raw[G][:, c, :], ACT.Copy)
                        act.wait_ge(state_done, STATES * g + TT - 1 + c)
                        nc.scalar.activation(prev_hi[s][:], prev[:, c].rearrange("p d f -> p (d f)"), ACT.Copy).then_inc(in_hi, 1)
                        if c < TT - 1:
                            state_step(g, G, i, TT - 1 + c, first)
                        if c:
                            m_split(g, G, c - 1)
                        act.wait_ge(seg_done, m + 1)
                        nc.scalar.activation(decay[s][:], decay[s][:], ACT.Exp).then_inc(exp_done, 1)
                    m_split(g, G, TT - 1)
            pairs(act, 0, GROUPS // 2, body)

        @block.vector
        def _(dve):
            dve.wait_ge(table_loaded, 32)
            nc.vector.tensor_tensor(state_w[:].rearrange("p (c h) -> p c h", c=TT), ends[:].rearrange("p (h c) -> p c h", c=TT),
                                    la_tok[:].rearrange("p (c h) -> p c h", c=TT), ALU.subtract).then_inc(table_done, 1)
            nc.vector.memset(prev[:, 0, 0], 0.0).then_inc(state_zero, 1)
            nc.vector.memset(prev[:, TT - 1, 1], 0.0).then_inc(state_zero, 1)
            dve.wait_ge(state_zero, 2)
            dve.wait_ge(table_done, 4)
            nc.vector.tensor_tensor(state_w[:], state_w[:], dt_tok[:], ALU.mult).then_inc(table_done, 1)
            dve.wait_ge(table_done, 5)
            dve.wait_ge(masks_made, 3)

            def weigh(g, G, k, first):
                c, d, _ = chunk_of(k)
                s, n = k % 2, STATES * g + k
                if not (first and G == 0 and k < 2):
                    dve.wait_ge(state_lo, n - 1)
                nc.vector.tensor_tensor(heads(xs_raw[s][:], 1), heads(x_raw[G][:, c, :], 1), per_token(state_w, c, g, d, 1),
                                        ALU.mult).then_inc(xs_done, 1)

            def state_split(g, G, k):
                c, s, n = chunk_of(k)[0], k % 2, STATES * g + k
                dve.wait_ge(state_hi, n + 1)
                nc.vector.tensor_tensor(sb_lo[s][:], b_raw[G][:, c, :], sb_hi[s][:].bitcast(F32), ALU.subtract)
                nc.vector.tensor_tensor(xs_lo[s][:], xs_raw[s][:], xs_hi[s][:].bitcast(F32), ALU.subtract).then_inc(state_lo, 1)

            def state_update(g, G, k, first):
                c, d, to = chunk_of(k)
                s, n = k % 2, STATES * g + k
                if not (first and G == 0 and k == 0):
                    dve.wait_ge(state_done, n)
                decay_c = end_exp[:].rearrange("p (h c) -> p h c", c=TT)[:, bass.ds(g * HPG + d * HEADS, HPG), c]
                nc.vector.tensor_tensor(decayed[s][:].rearrange("p (h e) -> p h e", h=HPG),
                                        prev[:, c, d].rearrange("p (h e) -> p h e", h=HPG),
                                        decay_c.unsqueeze(2).to_broadcast([P, HPG, HD]), ALU.mult).then_inc(decayed_done, 1)
                dve.wait_ge(decayed_done, n + 1)
                dve.wait_ge(state_mm, n + 1)
                nc.vector.tensor_tensor(prev[:, to, d], decayed[s][:], ps_state[s][:, 0:SLOT], ALU.add).then_inc(state_done, 1)

            def m_split(g, c):
                s, m = c % 2, TT * g + c
                dve.wait_ge(mhi_done, m + 1)
                nc.vector.tensor_tensor(m_lo[s][:], m_raw[s][:], m_hi[s][:].bitcast(F32), ALU.subtract).then_inc(mlo_done, 1)

            def y_add(g, G, c, first):
                s, m = c % 2, TT * g + c
                dve.wait_ge(off_mm, m + 1)
                if not (first and G == 0 and c < 2):
                    dve.wait_ge(y_step, 2 * m - 2)
                nc.vector.tensor_tensor(y_off[s][:].rearrange("p d (h e) -> p d h e", h=HPG), heads(ps_off[s][:], 2),
                                        per_token(la_exp, c, g, 0), ALU.mult).then_inc(off_done, 1)
                dve.wait_ge(off_done, m + 1)
                dve.wait_ge(diag_mm, m + 1)
                nc.vector.tensor_tensor(y_sum[s][:], y_off[s][:, 0], ps_diag[s][:, 0:SLOT], ALU.add).then_inc(sum_done, 1)

            def body(i, first):
                for G in range(2):
                    g = 2 * i + G
                    dve.wait_ge(raw_loaded[G], 64 * i + 64)
                    if not (first and G == 0):
                        dve.wait_ge(in_lo, TT * g)
                    weigh(g, G, 0, first)
                    for k in range(TT - 1):
                        if k < TT - 2:
                            weigh(g, G, k + 1, first)
                        state_split(g, G, k)
                        if k:
                            state_update(g, G, k - 1, first)
                    state_update(g, G, TT - 2, first)
                    for c in range(TT):
                        s, m = c % 2, TT * g + c
                        cs = slice(c * P, (c + 1) * P)
                        if c < TT - 1:
                            weigh(g, G, TT - 1 + c, first)
                        dve.wait_ge(in_hi, m + 1)
                        nc.vector.tensor_tensor(bc_lo[s][:], bc_raw[G][:, :, cs], bc_hi[s][:].bitcast(F32), ALU.subtract)
                        nc.vector.tensor_tensor(x_lo[s][:], x_raw[G][:, c, :], x_hi[s][:].bitcast(F32), ALU.subtract)
                        nc.vector.tensor_tensor(prev_lo[s][:], prev[:, c].rearrange("p d f -> p (d f)"),
                                                prev_hi[s][:].bitcast(F32), ALU.subtract).then_inc(in_lo, 1)
                        if c < TT - 1:
                            state_split(g, G, TT - 1 + c)
                        dve.wait_ge(decay_loaded[s], 32 * ((TT // 2) * g + c // 2 + 1))
                        if not (first and G == 0 and c < 2):
                            dve.wait_ge(m_sum, m - 1)
                        for d in range(2):
                            for h in range(HPG):
                                col = bass.ds(g * HPG + c * 2 * HEADS + d * HEADS + h, 1)
                                last = nc.vector.tensor_scalar(decay[s][:, d, h, :], decay_in[s][:, d, h, :], la_tok[:, col], 0.0,
                                                               ALU.subtract, ALU.min)
                        last.then_inc(seg_done, 1)
                        dve.wait_ge(cb_mm, m + 1)
                        if not (first and G == 0 and c < 2):
                            dve.wait_ge(weighted, m - 1)
                        nc.vector.tensor_tensor(cb_masked[s][:], ps_cb[s][:, 0:P].unsqueeze(1).to_broadcast([P, 2, P]), masks[:],
                                                ALU.mult).then_inc(cb_done, 1)
                        if c:
                            m_split(g, c - 1)
                        dve.wait_ge(cb_done, m + 1)
                        dve.wait_ge(exp_done, m + 1)
                        for d in range(2):
                            for h in range(HPG):
                                col = bass.ds(g * HPG + c * 2 * HEADS + d * HEADS + h, 1)
                                last = nc.vector.scalar_tensor_tensor(out=decay[s][:, d, h, :], in0=decay[s][:, d, h, :],
                                                                      scalar=dt_tok[:, col], in1=cb_masked[s][:, d, :],
                                                                      op0=ALU.mult, op1=ALU.mult)
                        last.then_inc(weighted, 1)
                        if c:
                            y_add(g, G, c - 1, first)
                        if c < TT - 1:
                            state_update(g, G, TT - 1 + c, first)
                    m_split(g, TT - 1)
                    y_add(g, G, TT - 1, first)
            pairs(dve, 0, GROUPS // 2, body)

        @block.tensor
        def _(pe):
            def three(out, pairs_of, **kw):
                for n, (a, b) in enumerate(pairs_of):
                    last = pe.matmul(out, a, b, start=n == 0, stop=n == 2, **kw)
                return last

            def state(g, G, k, first):
                s, n = k % 2, STATES * g + k
                pe.wait_ge(state_lo, n + 1)
                if not (first and G == 0 and k < 2):
                    pe.wait_ge(state_done, n - 1)
                three(ps_state[s][:, 0:SLOT], ((sb_hi[s][:], xs_hi[s][:]), (sb_hi[s][:], xs_lo[s][:]),
                                               (sb_lo[s][:], xs_hi[s][:]))).then_inc(state_mm, 1)

            def diagonal(g, G, c, first):
                s, m = c % 2, TT * g + c
                pe.wait_ge(mlo_done, m + 1)
                if not (first and G == 0 and c < 2):
                    pe.wait_ge(sum_done, m - 1)
                for h in range(HPG):
                    hs = slice(h * HD, (h + 1) * HD)
                    last = three(ps_diag[s][:, hs], ((m_hi[s][:, h, :], x_hi[s][:, hs]), (m_hi[s][:, h, :], x_lo[s][:, hs]),
                                                     (m_lo[s][:, h, :], x_hi[s][:, hs])))
                last.then_inc(diag_mm, 1)

            def body(i, first):
                for G in range(2):
                    g = 2 * i + G
                    for k in range(TT - 1):
                        state(g, G, k, first)
                    for c in range(TT):
                        s, m = c % 2, TT * g + c
                        fresh = first and G == 0 and c < 2
                        pe.wait_ge(in_lo, m + 1)
                        if not fresh:
                            pe.wait_ge(cb_done, m - 1)
                        three(ps_cb[s][:, 0:P], ((bc_hi[s][:, 0], bc_hi[s][:, 1]), (bc_hi[s][:, 0], bc_lo[s][:, 1]),
                                                 (bc_lo[s][:, 0], bc_hi[s][:, 1]))).then_inc(cb_mm, 1)
                        if not fresh:
                            pe.wait_ge(off_done, m - 1)
                        three(ps_off[s][:], ((bc_hi[s][:, 1], prev_hi[s][:]), (bc_hi[s][:, 1], prev_lo[s][:]),
                                             (bc_lo[s][:, 1], prev_hi[s][:]))).then_inc(off_mm, 1)
                        if c < TT - 1:
                            state(g, G, TT - 1 + c, first)
                        if c:
                            diagonal(g, G, c - 1, first)
                    diagonal(g, G, TT - 1, first)
            pairs(pe, 0, GROUPS // 2, body)


def stage_latents(nc, ap, keep, sem):
    with ExitStack() as ctx:
        def sb(name, shape, dt=F32):
            return ctx.enter_context(nc.sbuf_tensor(name, shape, dt))
        lat, vec, lat_hi, lat_lo = keep["lat"], keep["vec"], keep["lat_hi"], keep["lat_lo"]
        ones = sb("ones", [P, P], F32R)
        squares = sb("lat_squares", [P, 4, SEQ])
        roots = sb("lat_roots", [P, 2, SEQ])
        ps_q = ctx.enter_context(nc.psum_tensor("lat_ps_q", [P, SEQ], F32))
        ps_kv = ctx.enter_context(nc.psum_tensor("lat_ps_kv", [P, SEQ], F32))
        lat_step, lat_act, lat_mm, fill = sem("lat_steps"), sem("lat_act_steps"), sem("lat_mm"), sem("ones_set")
        block = ctx.enter_context(nc.Block())

        @block.gpsimd
        def _(pool):
            nc.gpsimd.memset(ones[:].bitcast(F32), 1.0).then_inc(fill, 1)

        @block.scalar
        def _(act):
            nc.scalar.activation(squares[:], lat[:], ACT.Square).then_inc(lat_act, 1)
            act.wait_ge(lat_act, 1)
            nc.scalar.activation(lat_hi[:], squares[:], ACT.Copy).then_inc(lat_act, 1)
            act.wait_ge(lat_step, 3)
            nc.scalar.activation(roots[:], roots[:], ACT.Sqrt).then_inc(lat_act, 1)
            act.wait_ge(lat_step, 8)
            nc.scalar.activation(lat_hi[:], lat[:], ACT.Copy).then_inc(lat_act, 1)

        @block.vector
        def _(dve):
            dve.wait_ge(lat_act, 2)
            nc.vector.tensor_tensor(lat_lo[:], squares[:], lat_hi[:].bitcast(F32), ALU.subtract).then_inc(lat_step, 1)
            dve.wait_ge(lat_mm, 2)
            for n, total in enumerate((ps_q, ps_kv)):
                nc.vector.tensor_scalar(roots[:, n, :], total[:], 1.0 / QR, EPS, ALU.mult, ALU.add).then_inc(lat_step, 1)
            dve.wait_ge(lat_act, 3)
            nc.vector.reciprocal(roots[:], roots[:]).then_inc(lat_step, 1)
            dve.wait_ge(lat_step, 4)
            for n in range(4):
                nc.vector.scalar_tensor_tensor(out=lat[:, n, :], in0=lat[:, n, :], scalar=vec[:, V_QN + n:V_QN + n + 1],
                                               in1=roots[:, n // 2, :], op0=ALU.mult, op1=ALU.mult).then_inc(lat_step, 1)
            dve.wait_ge(lat_step, 8)
            dve.wait_ge(lat_act, 4)
            nc.vector.tensor_tensor(lat_lo[:], lat[:], lat_hi[:].bitcast(F32), ALU.subtract).then_inc(lat_step, 1)

        @block.tensor
        def _(pe):
            pe.wait_ge(lat_step, 1)
            pe.wait_ge(fill, 1)
            for n, total in enumerate((ps_q, ps_kv)):
                for half in range(NHALF):
                    hs = slice(half * HALF, (half + 1) * HALF)
                    for m in range(4):
                        part = (lat_hi, lat_lo)[m % 2]
                        last = pe.matmul(total[:, hs], ones[:], part[:, 2 * n + m // 2, hs], start=m == 0, stop=m == 3)
                last.then_inc(lat_mm, 1)


STEPS = NHALF * TT
PBUF = 4
LAG = 2


def stage_attention(nc, ap, keep, sem):
    with ExitStack() as ctx:
        def sb(name, shape, dt=F32):
            return ctx.enter_context(nc.sbuf_tensor(name, shape, dt))

        def two(name, shape, dt=F32):
            return [sb(f"{name}{s}", shape, dt) for s in range(2)]
        trig, ident, kpe, lat_hi, lat_lo = keep["trig"], keep["ident"], keep["kpe"], keep["lat_hi"], keep["lat_lo"]
        attn = keep["attn"]
        w_raw = two("qkv_raw", [P, 2, 2, P])
        w_hi, w_lo = two("qkv_hi", [P, 2, 2, P], F32R), two("qkv_lo", [P, 2, 2, P], F32R)
        q_raw = sb("q_raw", [P, SEQ])
        rot = sb("q_turned", [P, SEQ])
        kv_raw = sb("kv_raw", [P, SEQ])
        q_hi, q_lo = two("q_hi", [P, SEQ], F32R), two("q_lo", [P, SEQ], F32R)
        k_hi, k_lo = two("k_hi", [P, SEQ], F32R), two("k_lo", [P, SEQ], F32R)
        v_hi, v_lo = two("v_hi", [P, TT, P], F32R), two("v_lo", [P, TT, P], F32R)
        maxima = two("maxima", [P, TT])
        neg_max = sb("neg_max", [TT, P], F32R)
        p_raw = [sb(f"p_raw{n}", [P, HALF]) for n in range(PBUF)]
        p_hi = [sb(f"p_hi{n}", [P, HALF], F32R) for n in range(PBUF)]
        p_lo = [sb(f"p_lo{n}", [P, HALF], F32R) for n in range(PBUF)]
        sums = sb("prob_sums", [P, NHALF, HALF])
        ps_q = ctx.enter_context(nc.psum_tensor("ps_q", [P, SEQ], F32))
        ps_kv = ctx.enter_context(nc.psum_tensor("ps_kv", [P, SEQ], F32))
        ps_s = [ctx.enter_context(nc.psum_tensor(f"ps_s{n}", [P, HALF], F32)) for n in range(2)]
        ps_o = [ctx.enter_context(nc.psum_tensor(f"ps_o{n}", [P, HALF], F32)) for n in range(2)]

        kpe_hi, kpe_lo, fill = sem("rope_key_hi"), sem("rope_key_lo"), sem("attention_fills")
        w_loaded = [sem(f"qkv_loaded{s}") for s in range(2)]
        whi_done, wlo_done, q_mm, kv_mm = sem("qkv_hi_done"), sem("qkv_lo_done"), sem("q_mm"), sem("kv_mm")
        q_copied, rope_parts, q_ready, kv_copied = sem("q_copied"), sem("q_rope_parts"), sem("q_ready"), sem("kv_copied")
        qk_hi, qk_lo, max_mm, max_done = sem("qk_hi_done"), sem("qk_lo_done"), sem("max_scores_mm"), sem("maxima_done")
        max_turned, neg_done, v_turned, vhi_done, vlo_done = sem("max_turned"), sem("neg_max_done"), sem("v_turned"), sem("v_hi_done"), sem("v_lo_done")
        row_loaded = [sem(f"max_row{s}") for s in range(2)]
        s_mm, phi_done, plo_done, pv_mm = sem("scores_mm"), sem("p_hi_done"), sem("p_lo_done"), sem("pv_mm")
        o_copied, sums_copied = sem("attn_copied"), sem("sums_copied")
        sums_stored = [sem(f"sums_stored{n}") for n in range(2)]
        block = ctx.enter_context(nc.Block())
        ROWS = slice(0, QK)

        def heads_loop(engine, body):
            for s in range(2):
                body(0, s, True, False)
            with engine.Fori(1, A_HEADS // 2 - 1) as i:
                for s in range(2):
                    body(i, s, False, False)
            for s in range(2):
                body(A_HEADS // 2 - 1, s, False, True)

        @block.sync
        def _(sp):
            def load(i, s):
                h = 2 * i + s
                for n, w in enumerate((ap["w_q"], ap["w_kv_b"])):
                    sp.dma_start(w_raw[s][:, n], w[:, bass.ds(h * P, P)].rearrange("(k p) c -> p k c", p=P)).then_inc(w_loaded[s], 16)

            def row(i, s):
                sp.wait_ge(neg_done, 2 * i + s + 1)
                sp.dma_start(q_hi[s][QK:QK + 1, :].bitcast(F32).rearrange("o (t q) -> o t q", t=TT), neg_max[:].bitcast(F32)).then_inc(row_loaded[s], 16)
            load(0, 0)
            load(0, 1)
            row(0, 0)

            def body(i, s, first, last):
                h = 2 * i + s
                if not last:
                    sp.wait_ge(wlo_done, h + 1)
                    load(i + 1, s)
                if not (last and s == 1):
                    row(i + s, 1 - s)
            heads_loop(sp, body)

        @block.gpsimd
        def _(pool):
            filled = 0
            for s in range(2):
                row = slice(QK, QK + 1)
                for tile, value in ((v_hi[s][:], 0.0), (v_lo[s][:], 0.0), (q_lo[s][row, :], 0.0), (k_lo[s][row, :], 0.0),
                                    (k_hi[s][row, :], 1.0), (v_hi[s][:, :, (1 - s) * VD], 1.0)):
                    if filled:
                        pool.wait_ge(fill, filled)
                    nc.gpsimd.memset(tile.bitcast(F32), value).then_inc(fill, 1)
                    filled += 1

            def body(i, s, first, last):
                for half in range(NHALF):
                    pool.wait_ge(sums_copied, 2 * (2 * i + s) + half + 1)
                    row = (1 - s) * VD
                    pool.dma_start(ap["sums"][bass.ds(2 * i + s, 1), half * HALF:(half + 1) * HALF],
                                   sums[row:row + 1, half, :]).then_inc(sums_stored[half], 16)
            heads_loop(pool, body)
            for half in range(NHALF):
                pool.wait_ge(sums_stored[half], 16 * A_HEADS)

        @block.scalar
        def _(act):
            act.wait_ge(fill, 1)
            for s in range(2):
                nc.scalar.activation(k_hi[s][NOPE:QK, :], kpe[NOPE:QK, :], ACT.Copy).then_inc(kpe_hi, 1)

            def split_w(i, s):
                act.wait_ge(w_loaded[s], 32 * i + 32)
                if not (isinstance(i, int) and i == 0):
                    act.wait_ge(kv_mm, 2 * i + s - 1)
                nc.scalar.activation(w_hi[s][:], w_raw[s][:], ACT.Copy).then_inc(whi_done, 1)

            def copy_q(i, s):
                h = 2 * i + s
                act.wait_ge(q_mm, h + 1)
                if not (isinstance(i, int) and h == 0):
                    act.wait_ge(qk_lo, h)
                nc.scalar.activation(q_raw[0:NOPE, :], ps_q[0:NOPE, :], ACT.Copy).then_inc(q_copied, 1)

            def copy_kv(i, s):
                h = 2 * i + s
                act.wait_ge(kv_mm, h + 1)
                if not (isinstance(i, int) and h == 0):
                    act.wait_ge(v_turned, h)
                nc.scalar.activation(kv_raw[:], ps_kv[:], ACT.Copy).then_inc(kv_copied, 1)

            def split_qk(i, s):
                h = 2 * i + s
                act.wait_ge(q_ready, h + 1)
                act.wait_ge(kv_copied, h + 1)
                if not (isinstance(i, int) and i == 0):
                    act.wait_ge(s_mm, STEPS * (h - 1))
                nc.scalar.activation(q_hi[s][ROWS, :], q_raw[ROWS, :], ACT.Copy)
                nc.scalar.activation(k_hi[s][0:NOPE, :], kv_raw[0:NOPE, :], ACT.Copy).then_inc(qk_hi, 1)

            def negate_max(i, s):
                h = 2 * i + s
                act.wait_ge(max_turned, h + 1)
                if not (isinstance(i, int) and h == 0):
                    act.wait_ge(row_loaded[1 - s], 16 * (i + s))
                nc.scalar.activation(neg_max[:], ps_q[0:TT, 0:P], ACT.Copy, scale=-1.0).then_inc(neg_done, 1)

            def split_v(i, s):
                h = 2 * i + s
                act.wait_ge(v_turned, h + 1)
                if not (isinstance(i, int) and i == 0):
                    act.wait_ge(pv_mm, STEPS * (h - 1))
                nc.scalar.activation(v_hi[s][:, :, s * VD:(s + 1) * VD],
                                     ps_q[:].rearrange("p (t c) -> p t c", t=TT)[:, :, NOPE:P], ACT.Copy).then_inc(vhi_done, 1)

            def copy_sums(i, s, half, first):
                h = 2 * i + s
                act.wait_ge(pv_mm, STEPS * h + (half + 1) * TT)
                if not first:
                    act.wait_ge(sums_stored[half], 16 * h)
                row = (1 - s) * VD
                nc.scalar.activation(sums[row:row + 1, half, :], ps_o[half][row:row + 1, :], ACT.Copy).then_inc(sums_copied, 1)

            for s in range(2):
                split_w(0, s)
            copy_q(0, 0)
            copy_kv(0, 0)
            act.wait_ge(fill, 12)
            split_qk(0, 0)
            negate_max(0, 0)
            split_v(0, 0)

            def body(i, s, first, last):
                h = 2 * i + s
                more = not (last and s == 1)
                for j in range(STEPS):
                    if j == 1 and more:
                        copy_q(i + s, 1 - s)
                    if j == 2 and more:
                        copy_kv(i + s, 1 - s)
                    if j == 2 and not (first and s == 0):
                        copy_sums(i - 1 + s, 1 - s, 1, first)
                    if j == 3 and more:
                        split_qk(i + s, 1 - s)
                    if j == 6 and not last:
                        split_w(i + 1, s)
                    if j == 10:
                        copy_sums(i, s, 0, first and s == 0)
                    if j == 13 and more:
                        negate_max(i + s, 1 - s)
                    if j == 14 and more:
                        split_v(i + s, 1 - s)
                    b = j % PBUF
                    act.wait_ge(s_mm, STEPS * h + j + 1)
                    if not (first and s == 0 and j < PBUF):
                        act.wait_ge(pv_mm, STEPS * h + j + 1 - PBUF)
                        act.wait_ge(plo_done, STEPS * h + j + 1 - PBUF)
                    nc.scalar.activation(p_raw[b][:], ps_s[j % 2][:], ACT.Exp, scale=SM_SCALE)
                    nc.scalar.activation(p_hi[b][:], ps_s[j % 2][:], ACT.Exp, scale=SM_SCALE).then_inc(phi_done, 1)
            heads_loop(act, body)
            copy_sums(A_HEADS // 2 - 1, 1, 1, False)

        @block.vector
        def _(dve):
            dve.wait_ge(kpe_hi, 2)
            for s in range(2):
                nc.vector.tensor_tensor(k_lo[s][NOPE:QK, :], kpe[NOPE:QK, :], k_hi[s][NOPE:QK, :].bitcast(F32),
                                        ALU.subtract).then_inc(kpe_lo, 1)

            def split_w(i, s):
                dve.wait_ge(whi_done, 2 * i + s + 1)
                nc.vector.tensor_tensor(w_lo[s][:], w_raw[s][:], w_hi[s][:].bitcast(F32), ALU.subtract).then_inc(wlo_done, 1)

            def rope_q(i, s, fresh):
                h = 2 * i + s
                pe_rows = slice(NOPE, QK)
                dve.wait_ge(q_mm, h + 1)
                if not fresh:
                    dve.wait_ge(qk_lo, h)
                nc.vector.tensor_tensor(q_raw[pe_rows, :], ps_q[pe_rows, :], trig[pe_rows, :], ALU.mult)
                nc.vector.tensor_tensor(rot[pe_rows, :], ps_q[QK:P, :], trig[QK:P, :], ALU.mult).then_inc(rope_parts, 1)
                dve.wait_ge(rope_parts, h + 1)
                nc.vector.tensor_tensor(q_raw[pe_rows, :], q_raw[pe_rows, :], rot[pe_rows, :], ALU.add).then_inc(q_ready, 1)

            def split_qk(i, s):
                h = 2 * i + s
                dve.wait_ge(qk_hi, h + 1)
                nc.vector.tensor_tensor(q_lo[s][ROWS, :], q_raw[ROWS, :], q_hi[s][ROWS, :].bitcast(F32), ALU.subtract)
                nc.vector.tensor_tensor(k_lo[s][0:NOPE, :], kv_raw[0:NOPE, :], k_hi[s][0:NOPE, :].bitcast(F32),
                                        ALU.subtract).then_inc(qk_lo, 1)

            def maximum(i, s, n):
                h = 2 * i + s
                dve.wait_ge(max_mm, TT * h + n + 1)
                nc.vector.reduce_max(maxima[s][:, n:n + 1], ps_kv[:], AX.X).then_inc(max_done, 1)

            def split_v(i, s):
                dve.wait_ge(vhi_done, 2 * i + s + 1)
                nc.vector.tensor_tensor(v_lo[s][:, :, s * VD:(s + 1) * VD],
                                        ps_q[:].rearrange("p (t c) -> p t c", t=TT)[:, :, NOPE:P],
                                        v_hi[s][:, :, s * VD:(s + 1) * VD].bitcast(F32), ALU.subtract).then_inc(vlo_done, 1)

            def copy_out(i, s, half):
                h = 2 * i + s
                rows = slice(s * VD, (s + 1) * VD)
                dve.wait_ge(pv_mm, STEPS * h + (half + 1) * TT)
                nc.vector.tensor_copy(attn[rows, bass.ds(i, 1), half * HALF:(half + 1) * HALF].rearrange("p o t -> p (o t)"),
                                      ps_o[half][rows, :]).then_inc(o_copied, 1)

            for s in range(2):
                split_w(0, s)
            rope_q(0, 0, True)
            dve.wait_ge(fill, 12)
            split_qk(0, 0)
            for n in range(TT):
                maximum(0, 0, n)
            split_v(0, 0)

            def body(i, s, first, last):
                h = 2 * i + s
                more = not (last and s == 1)
                for j in range(STEPS):
                    if j == 1 and more:
                        rope_q(i + s, 1 - s, False)
                    if j == 2 and not (first and s == 0):
                        copy_out(i - 1 + s, 1 - s, 1)
                    if j == 4 and more:
                        split_qk(i + s, 1 - s)
                    if 5 <= j < 5 + TT and more:
                        maximum(i + s, 1 - s, j - 5)
                    if j == 6 and not last:
                        split_w(i + 1, s)
                    if j == 10:
                        copy_out(i, s, 0)
                    if j == 14 and more:
                        split_v(i + s, 1 - s)
                    b = j % PBUF
                    dve.wait_ge(phi_done, STEPS * h + j + 1)
                    nc.vector.tensor_tensor(p_lo[b][:], p_raw[b][:], p_hi[b][:].bitcast(F32), ALU.subtract).then_inc(plo_done, 1)
            heads_loop(dve, body)
            copy_out(A_HEADS // 2 - 1, 1, 1)

        @block.tensor
        def _(pe):
            def project_q(i, s, fresh):
                h = 2 * i + s
                pe.wait_ge(wlo_done, h + 1)
                if not fresh:
                    pe.wait_ge(vlo_done, h)
                unit_matmuls(pe, ps_q, w_hi[s][:, 0], w_lo[s][:, 0], lat_hi[:, 0:2], lat_lo[:, 0:2], kt=2).then_inc(q_mm, 1)

            def project_kv(i, s, fresh):
                h = 2 * i + s
                if not fresh:
                    pe.wait_ge(max_done, TT * h)
                unit_matmuls(pe, ps_kv, w_hi[s][:, 1], w_lo[s][:, 1], lat_hi[:, 2:4], lat_lo[:, 2:4], kt=2).then_inc(kv_mm, 1)

            def max_scores(i, s, n):
                h = 2 * i + s
                pe.wait_ge(qk_hi, h + 1)
                if n:
                    pe.wait_ge(max_done, TT * h + n)
                for half in range(NHALF):
                    hs = slice(half * HALF, (half + 1) * HALF)
                    last = pe.matmul(ps_kv[:, hs], q_hi[s][ROWS, n * P:(n + 1) * P], k_hi[s][ROWS, hs], start=True, stop=True)
                last.then_inc(max_mm, 1)

            def turn_max(i, s):
                h = 2 * i + s
                pe.wait_ge(max_done, TT * (h + 1))
                pe.wait_ge(q_ready, h + 1)
                pe.wait_ge(q_copied, h + 1)
                pe.transpose(ps_q[0:TT, 0:P], maxima[s][:], ident[:]).then_inc(max_turned, 1)

            def turn_v(i, s):
                h = 2 * i + s
                pe.wait_ge(neg_done, h + 1)
                for t in range(TT):
                    last = pe.transpose(ps_q[:, t * P:(t + 1) * P], kv_raw[:, t * P:(t + 1) * P], ident[:])
                last.then_inc(v_turned, 1)

            def three(out, a, b, a_lo, b_lo, start=True, stop=True):
                pe.matmul(out, a, b, start=start, stop=False)
                pe.matmul(out, a, b_lo, start=False, stop=False)
                return pe.matmul(out, a_lo, b, start=False, stop=stop)

            def probs_v(i, s, j, fresh):
                h, b, half, t = 2 * i + s, j % PBUF, j // TT, j % TT
                pe.wait_ge(plo_done, STEPS * h + j + 1)
                if t == 0:
                    pe.wait_ge(vlo_done, h + 1)
                    if not fresh:
                        pe.wait_ge(o_copied, 2 * h + half - 1)
                        pe.wait_ge(sums_copied, 2 * h + half - 1)
                three(ps_o[half][:], v_hi[s][:, t], p_hi[b][:], v_lo[s][:, t], p_lo[b][:], t == 0, t == TT - 1).then_inc(pv_mm, 1)

            pe.wait_ge(kpe_lo, 2)
            project_q(0, 0, True)
            project_kv(0, 0, True)
            pe.wait_ge(kv_copied, 1)
            for n in range(TT):
                max_scores(0, 0, n)
            turn_max(0, 0)
            turn_v(0, 0)

            def body(i, s, first, last):
                h = 2 * i + s
                more = not (last and s == 1)
                for j in range(STEPS):
                    if j == 0 and more:
                        project_q(i + s, 1 - s, False)
                    if j == 1 and more:
                        project_kv(i + s, 1 - s, False)
                    if 4 <= j < 4 + TT and more:
                        max_scores(i + s, 1 - s, j - 4)
                    if j == 12 and more:
                        turn_max(i + s, 1 - s)
                    if j == 13 and more:
                        turn_v(i + s, 1 - s)
                    half, t = j // TT, j % TT
                    if j == 0:
                        pe.wait_ge(row_loaded[s], 16 * i + 16)
                        pe.wait_ge(qk_lo, h + 1)
                    if not (first and s == 0 and j < 2):
                        pe.wait_ge(phi_done, STEPS * h + j - 1)
                    ks, qs = slice(t * P, (t + 1) * P), slice(half * HALF, (half + 1) * HALF)
                    rows = slice(0, QK + 1)
                    three(ps_s[j % 2][:], k_hi[s][rows, ks], q_hi[s][rows, qs], k_lo[s][rows, ks], q_lo[s][rows, qs]).then_inc(s_mm, 1)
                    if j >= LAG:
                        probs_v(i, s, j - LAG, first and s == 0)
                    elif not (first and s == 0):
                        probs_v(i - 1 + s, 1 - s, j - LAG + STEPS, False)
            heads_loop(pe, body)
            for j in range(STEPS - LAG, STEPS):
                probs_v(A_HEADS // 2 - 1, 1, j, False)


YT = D_INNER // P


def stage_gate_y(nc, ap, keep, sem):
    with ExitStack() as ctx:
        def sb(name, shape, dt=F32):
            return ctx.enter_context(nc.sbuf_tensor(name, shape, dt))
        y_in = [sb(f"y_in{s}", [P, D_INNER]) for s in range(2)]
        z_in = sb("z_in", [P, D_INNER])
        wb = sb("ssm_norm_w", [P, D_INNER])
        squares = sb("y_squares", [P, SLOT])
        sums = [sb(f"y_sums{s}", [P, GROUPS]) for s in range(2)]
        turned = [ctx.enter_context(nc.psum_tensor(f"y_turned{s}", [P, YT, P], F32)) for s in range(2)]
        loaded, z_loaded = [sem(f"y_loaded{s}") for s in range(2)], sem("z_loaded")
        w_loaded, gated, sums_done, stat_step = sem("ssm_norm_w_loaded"), sem("y_gated"), sem("y_group_sums"), sem("y_stat_steps")
        rooted, normed, turned_done, hi_done, lo_done = sem("y_roots"), sem("y_normed"), sem("y_turned"), sem("yT_hi"), sem("yT_lo")
        yT_hi, yT_lo, ident = keep["yT_hi"], keep["yT_lo"], keep["ident"]
        block = ctx.enter_context(nc.Block())

        @block.sync
        def _(sp):
            def body(i, first):
                for s in range(2):
                    t = 2 * i + s
                    if not first:
                        sp.wait_ge(turned_done, t - 1)
                    sp.dma_start(y_in[s][:], ap["y"][bass.ds(t * P, P), :]).then_inc(loaded[s], 16)
                    if not (first and s == 0):
                        sp.wait_ge(gated, t)
                    sp.dma_start(z_in[:], ap["tok"][bass.ds(t * P, P), TOK_Z:TOK_W]).then_inc(z_loaded, 16)
                    if first and s == 0:
                        sp.dma_start(wb[:], ap["ssm_norm_w"].partition_broadcast(P)).then_inc(w_loaded, 16)
            pairs(sp, 0, TT // 2, body)

        @block.gpsimd
        def _(pool):
            def body(i, first):
                for s in range(2):
                    pool.wait_ge(loaded[s], 16 * i + 16)
                    pool.wait_ge(z_loaded, 32 * i + 16 * s + 16)
                    nc.gpsimd.tensor_tensor(y_in[s][:], y_in[s][:], z_in[:], ALU.mult).then_inc(gated, 1)
            pairs(pool, 0, TT // 2, body)

        @block.scalar
        def _(act):
            def copy_hi(i, s):
                act.wait_ge(turned_done, 2 * i + s + 1)
                nc.scalar.activation(yT_hi[:, :, bass.ds((2 * i + s) * P, P)], turned[s][:], ACT.Copy).then_inc(hi_done, 1)

            def body(i, first):
                for s in range(2):
                    t = 2 * i + s
                    act.wait_ge(gated, t + 1)
                    for g in range(GROUPS):
                        if not (first and s == 0 and g == 0):
                            act.wait_ge(sums_done, GROUPS * t + g)
                        nc.scalar.activation(squares[:], y_in[s][:, g * SLOT:(g + 1) * SLOT], ACT.Square,
                                             accum_out=sums[s][:, g:g + 1]).then_inc(sums_done, 1)
                    act.wait_ge(stat_step, 2 * t + 1)
                    nc.scalar.activation(sums[s][:], sums[s][:], ACT.Sqrt).then_inc(rooted, 1)
                    if not (first and s == 0):
                        copy_hi(i - 1 + s, 1 - s)
            pairs(act, 0, TT // 2, body)
            copy_hi(TT // 2 - 1, 1)

        @block.vector
        def _(dve):
            def split_lo(i, s):
                dve.wait_ge(hi_done, 2 * i + s + 1)
                ts = bass.ds((2 * i + s) * P, P)
                nc.vector.tensor_tensor(yT_lo[:, :, ts], turned[s][:], yT_hi[:, :, ts].bitcast(F32), ALU.subtract).then_inc(lo_done, 1)

            dve.wait_ge(w_loaded, 16)

            def body(i, first):
                for s in range(2):
                    t = 2 * i + s
                    dve.wait_ge(sums_done, GROUPS * (t + 1))
                    nc.vector.tensor_scalar(sums[s][:], sums[s][:], 1.0 / SLOT, EPS, ALU.mult, ALU.add).then_inc(stat_step, 1)
                    dve.wait_ge(rooted, t + 1)
                    nc.vector.reciprocal(sums[s][:], sums[s][:]).then_inc(stat_step, 1)
                    dve.wait_ge(stat_step, 2 * t + 2)
                    for g in range(GROUPS):
                        gs = slice(g * SLOT, (g + 1) * SLOT)
                        last = nc.vector.scalar_tensor_tensor(out=y_in[s][:, gs], in0=y_in[s][:, gs], scalar=sums[s][:, g:g + 1],
                                                              in1=wb[:, gs], op0=ALU.mult, op1=ALU.mult)
                    last.then_inc(normed, 1)
                    if not (first and s == 0):
                        split_lo(i - 1 + s, 1 - s)
            pairs(dve, 0, TT // 2, body)
            split_lo(TT // 2 - 1, 1)

        @block.tensor
        def _(pe):
            def body(i, first):
                for s in range(2):
                    t = 2 * i + s
                    pe.wait_ge(normed, t + 1)
                    if not first:
                        pe.wait_ge(lo_done, t - 1)
                    for k in range(YT):
                        last = pe.transpose(turned[s][:, k, :], y_in[s][:, k * P:(k + 1) * P], ident[:])
                    last.then_inc(turned_done, 1)
            pairs(pe, 0, TT // 2, body)


def stage_ssm_out(nc, ap, keep, sem):
    with ExitStack() as ctx:
        def two(name, shape, dt=F32):
            return [ctx.enter_context(nc.sbuf_tensor(f"{name}{s}", shape, dt)) for s in range(2)]
        w_raw, w_hi, w_lo = two("so_raw", [P, KT, P]), two("so_hi", [P, KT, P], F32R), two("so_lo", [P, KT, P], F32R)
        gate = two("so_gate", [P, SEQ])
        psum = [ctx.enter_context(nc.psum_tensor(f"so_ps{s}", [P, SEQ], F32)) for s in range(2)]
        w_loaded, gate_loaded = [sem(f"so_w_loaded{s}") for s in range(2)], [sem(f"so_gate_loaded{s}") for s in range(2)]
        stored = [sem(f"so_stored{s}") for s in range(2)]
        hi_done, lo_done, unit_mm, gated = sem("so_hi"), sem("so_lo"), sem("so_mm"), sem("so_gated")
        yT_hi, yT_lo = keep["yT_hi"], keep["yT_lo"]
        tiles = D_MODEL // P
        block = ctx.enter_context(nc.Block())

        @block.sync
        def _(sp):
            def body(i, first):
                for u in range(4):
                    s, j = u % 2, 2 * i + u // 2
                    if not (first and u < 2):
                        sp.wait_ge(lo_done, 4 * i + u - 1)
                    w = ap["w_ssm_out"][s * KT * P:(s + 1) * KT * P, bass.ds(j * P, P)]
                    sp.dma_start(w_raw[s][:], w.rearrange("(k p) c -> p k c", p=P)).then_inc(w_loaded[s], 16)
                    if s == 1:
                        if not first:
                            sp.wait_ge(stored[u // 2], 16 * i)
                        sp.dma_start(gate[u // 2][:], ap["gates"][bass.ds(j * P, P), :]).then_inc(gate_loaded[u // 2], 16)
            pairs(sp, 0, tiles // 2, body)

        @block.gpsimd
        def _(pool):
            def body(i, first):
                for s in range(2):
                    pool.wait_ge(gated, 2 * i + s + 1)
                    pool.dma_start(ap["mixed"][bass.ds((2 * i + s) * P, P), :], gate[s][:]).then_inc(stored[s], 16)
            pairs(pool, 0, tiles // 2, body)
            for s in range(2):
                pool.wait_ge(stored[s], 16 * (tiles // 2))

        @block.scalar
        def _(act):
            def body(i, first):
                for u in range(4):
                    act.wait_ge(w_loaded[u % 2], 32 * i + 16 * (u // 2) + 16)
                    if not (first and u < 2):
                        act.wait_ge(unit_mm, 4 * i + u - 1)
                    nc.scalar.activation(w_hi[u % 2][:], w_raw[u % 2][:], ACT.Copy).then_inc(hi_done, 1)
            pairs(act, 0, tiles // 2, body)

        @block.vector
        def _(dve):
            def gate_tile(i, s):
                j = 2 * i + s
                dve.wait_ge(unit_mm, 2 * j + 2)
                dve.wait_ge(gate_loaded[s], 16 * i + 16)
                nc.vector.tensor_tensor(gate[s][:], psum[s][:], gate[s][:], ALU.mult).then_inc(gated, 1)

            def body(i, first):
                for u in range(4):
                    dve.wait_ge(hi_done, 4 * i + u + 1)
                    nc.vector.tensor_tensor(w_lo[u % 2][:], w_raw[u % 2][:], w_hi[u % 2][:].bitcast(F32), ALU.subtract).then_inc(lo_done, 1)
                    if u == 2:
                        gate_tile(i, 0)
                    if u == 0 and not first:
                        gate_tile(i - 1, 1)
            pairs(dve, 0, tiles // 2, body)
            gate_tile(tiles // 2 - 1, 1)

        @block.tensor
        def _(pe):
            def body(i, first):
                for u in range(4):
                    pe.wait_ge(lo_done, 4 * i + u + 1)
                    s, half, j = u // 2, u % 2, 2 * i + u // 2
                    if half == 0 and not first:
                        pe.wait_ge(gated, j - 1)
                    ks = slice(half * KT, (half + 1) * KT)
                    unit_matmuls(pe, psum[s], w_hi[half], w_lo[half], yT_hi[:, ks], yT_lo[:, ks],
                                 start=half == 0, stop=half == 1).then_inc(unit_mm, 1)
            pairs(pe, 0, tiles // 2, body)


def stage_merge(nc, ap, keep, sem):
    with ExitStack() as ctx:
        def sb(name, shape, dt=F32):
            return ctx.enter_context(nc.sbuf_tensor(name, shape, dt))

        def two(name, shape, dt=F32):
            return [sb(f"{name}{s}", shape, dt) for s in range(2)]
        attn, mixed_hi, mixed_lo = keep["attn"], keep["mixed_hi"], keep["mixed_lo"]
        a_hi, a_lo = sb("attn_hi", [P, KT, SEQ], F32R), sb("attn_lo", [P, KT, SEQ], F32R)
        sums = sb("sums", [A_HEADS, SEQ])
        w_raw, w_hi, w_lo = two("mo_raw", [P, KT, P]), two("mo_hi", [P, KT, P], F32R), two("mo_lo", [P, KT, P], F32R)
        gate, mixed = two("mo_gate", [P, SEQ]), two("mo_mixed", [P, SEQ])
        recip = mixed
        psum = [ctx.enter_context(nc.psum_tensor(f"mo_ps{s}", [P, SEQ], F32)) for s in range(2)]
        sums_in, sums_inv, sums_out = sem("sums_in"), sem("sums_inverted"), sem("sums_out")
        recip_in, a_step, ahi, alo = [sem(f"recip_in{s}") for s in range(2)], sem("attn_normed"), sem("attn_hi_done"), sem("attn_lo_done")
        w_loaded, gate_loaded = [sem(f"mo_w_loaded{s}") for s in range(2)], [sem(f"mo_gate_loaded{s}") for s in range(2)]
        ssm_loaded = [sem(f"mo_ssm_loaded{s}") for s in range(2)]
        hi_done, lo_done, unit_mm, gated, mixed_sum = sem("mo_hi"), sem("mo_lo"), sem("mo_mm"), sem("mo_gated"), sem("mo_sum")
        mhi, mlo = sem("mixed_hi_done"), sem("mixed_lo_done")
        tiles = D_MODEL // P
        block = ctx.enter_context(nc.Block())

        @block.sync
        def _(sp):
            sp.dma_start(sums[:], ap["sums"]).then_inc(sums_in, 16)

            def load(i, s, fresh):
                j = 2 * i + s
                if not fresh:
                    sp.wait_ge(lo_done, j - 1)
                sp.dma_start(w_raw[s][:], ap["w_mla_out"][:, bass.ds(j * P, P)].rearrange("(k p) c -> p k c", p=P)).then_inc(w_loaded[s], 16)
                if not fresh:
                    sp.wait_ge(mlo, j - 1)
                sp.dma_start(gate[s][:], ap["gates"][bass.ds(j * P + D_MODEL, P), :]).then_inc(gate_loaded[s], 16)

            def load_ssm(i, s):
                sp.dma_start(mixed[s][:], ap["mixed"][bass.ds((2 * i + s) * P, P), :]).then_inc(ssm_loaded[s], 16)
            for s in range(2):
                load(0, s, True)
            sp.wait_ge(sums_inv, 1)
            sp.dma_start(ap["recip"], sums[:]).then_inc(sums_out, 16)
            sp.wait_ge(sums_out, 16)
            for k in range(KT):
                if k >= 2:
                    sp.wait_ge(a_step, k - 1)
                for half in range(2):
                    sp.dma_start(recip[k % 2][half * VD:(half + 1) * VD, :],
                                 ap["recip"][2 * k + half, :].partition_broadcast(VD)).then_inc(recip_in[k % 2], 16)
            for s in range(2):
                sp.wait_ge(a_step, KT - 1 + s)
                load_ssm(0, s)
            with sp.Fori(1, tiles // 2) as i:
                for s in range(2):
                    load(i, s, False)
                    load_ssm(i, s)

        @block.scalar
        def _(act):
            def split_w(i, s, fresh):
                act.wait_ge(w_loaded[s], 16 * i + 16)
                if not fresh:
                    act.wait_ge(unit_mm, 2 * i + s - 1)
                nc.scalar.activation(w_hi[s][:], w_raw[s][:], ACT.Copy).then_inc(hi_done, 1)
            for s in range(2):
                split_w(0, s, True)
            for k in range(KT):
                act.wait_ge(a_step, k + 1)
                nc.scalar.activation(a_hi[:, k, :], attn[:, k, :], ACT.Copy).then_inc(ahi, 1)

            def body(i, last):
                for s in range(2):
                    j = 2 * i + s
                    act.wait_ge(mixed_sum, j + 1)
                    nc.scalar.activation(mixed_hi[:, bass.ds(j, 1), :], mixed[s][:].unsqueeze(1), ACT.Copy).then_inc(mhi, 1)
                    if not last:
                        split_w(i + 1, s, False)
            with act.Fori(0, tiles // 2 - 1) as i:
                body(i, False)
            body(tiles // 2 - 1, True)

        @block.vector
        def _(dve):
            dve.wait_ge(sums_in, 16)
            nc.vector.reciprocal(sums[:], sums[:]).then_inc(sums_inv, 1)

            def split_w(i, s):
                dve.wait_ge(hi_done, 2 * i + s + 1)
                nc.vector.tensor_tensor(w_lo[s][:], w_raw[s][:], w_hi[s][:].bitcast(F32), ALU.subtract).then_inc(lo_done, 1)
            for s in range(2):
                split_w(0, s)
            for k in range(KT + 1):
                if k < KT:
                    dve.wait_ge(recip_in[k % 2], 32 * (k // 2 + 1))
                    nc.vector.tensor_tensor(attn[:, k, :], attn[:, k, :], recip[k % 2][:], ALU.mult).then_inc(a_step, 1)
                if k:
                    dve.wait_ge(ahi, k)
                    nc.vector.tensor_tensor(a_lo[:, k - 1, :], attn[:, k - 1, :], a_hi[:, k - 1, :].bitcast(F32), ALU.subtract).then_inc(alo, 1)

            def body(i, last):
                for s in range(2):
                    j = 2 * i + s
                    dve.wait_ge(unit_mm, j + 1)
                    dve.wait_ge(gate_loaded[s], 16 * i + 16)
                    nc.vector.tensor_tensor(gate[s][:], psum[s][:], gate[s][:], ALU.mult).then_inc(gated, 1)
                    dve.wait_ge(gated, j + 1)
                    dve.wait_ge(ssm_loaded[s], 16 * i + 16)
                    nc.vector.tensor_tensor(mixed[s][:], mixed[s][:], gate[s][:], ALU.add).then_inc(mixed_sum, 1)
                    if not last:
                        split_w(i + 1, s)
                    dve.wait_ge(mhi, j + 1)
                    nc.vector.tensor_tensor(mixed_lo[:, bass.ds(j, 1), :], mixed[s][:].unsqueeze(1),
                                            mixed_hi[:, bass.ds(j, 1), :].bitcast(F32), ALU.subtract).then_inc(mlo, 1)
            with dve.Fori(0, tiles // 2 - 1) as i:
                body(i, False)
            body(tiles // 2 - 1, True)

        @block.tensor
        def _(pe):
            pe.wait_ge(alo, KT)

            def body(i, first):
                for s in range(2):
                    j = 2 * i + s
                    pe.wait_ge(lo_done, j + 1)
                    if not first:
                        pe.wait_ge(gated, j - 1)
                    unit_matmuls(pe, psum[s], w_hi[s], w_lo[s], a_hi, a_lo).then_inc(unit_mm, 1)
            pairs(pe, 0, tiles // 2, body)


def stage_out_proj(nc, ap, keep, sem):
    with ExitStack() as ctx:
        def sb(name, shape, dt=F32):
            return ctx.enter_context(nc.sbuf_tensor(name, shape, dt))
        mixed_hi, mixed_lo, ident = keep["mixed_hi"], keep["mixed_lo"], keep["ident"]
        hT_hi, hT_lo = mixed_hi, mixed_lo
        w_raw = sb("wo_raw", [P, D_MODEL])
        w_hi, w_lo = sb("wo_hi", [P, KT, D_MODEL], F32R), sb("wo_lo", [P, KT, D_MODEL], F32R)
        x = [sb(f"res_x{s}", [P, D_MODEL]) for s in range(2)]
        h = sb("res_h", [P, D_MODEL])
        norm = sb("res_norm", [P, D_MODEL])
        w_post, w_pre = sb("w_post", [P, D_MODEL]), sb("w_pre", [P, D_MODEL])
        stat = sb("res_stats", [P, 2, 2])
        psum = [ctx.enter_context(nc.psum_tensor(f"wo_ps{s}", [P, D_MODEL], F32)) for s in range(2)]
        turned = [ctx.enter_context(nc.psum_tensor(f"wo_turned{s}", [P, D_MODEL], F32)) for s in range(2)]
        w_loaded, hi_done, lo_done, vec_loaded = sem("wo_loaded"), sem("wo_hi_done"), sem("wo_lo_done"), sem("res_weights_loaded")
        x_loaded, x_stored = [sem(f"res_x_loaded{s}") for s in range(2)], [sem(f"x1_stored{s}") for s in range(2)]
        tile_mm, sum_done, mean_done, root_done, rstd_done = sem("wo_mm"), sem("res_sums"), sem("res_means"), sem("res_roots"), sem("res_rstds")
        normed, x1_done, h_done, turned_done = sem("res_normed"), sem("x1_done"), sem("res_h_done"), sem("res_turned")
        thi, tlo = sem("h2T_hi_done"), sem("h2T_lo_done")
        block = ctx.enter_context(nc.Block())

        @block.sync
        def _(sp):
            for k in range(KT):
                if k:
                    sp.wait_ge(lo_done, k)
                sp.dma_start(w_raw[:], ap["w_out"][k * P:(k + 1) * P, :]).then_inc(w_loaded, 16)
                if k == 0:
                    sp.dma_start(w_post[:], ap["norm_mix_post"].partition_broadcast(P)).then_inc(vec_loaded, 16)
                    sp.dma_start(w_pre[:], ap["norm_mlp_pre"].partition_broadcast(P)).then_inc(vec_loaded, 16)
                    for s in range(2):
                        sp.dma_start(x[s][:], ap["x"][s * P:(s + 1) * P, :]).then_inc(x_loaded[s], 16)
            with sp.Fori(1, TT // 2) as i:
                for s in range(2):
                    sp.wait_ge(x_stored[s], 16 * i)
                    sp.dma_start(x[s][:], ap["x"][bass.ds((2 * i + s) * P, P), :]).then_inc(x_loaded[s], 16)

        @block.gpsimd
        def _(pool):
            def body(i, first):
                for s in range(2):
                    pool.wait_ge(h_done, 2 * i + s + 1)
                    pool.dma_start(ap["x1"][bass.ds((2 * i + s) * P, P), :], x[s][:]).then_inc(x_stored[s], 16)
            pairs(pool, 0, TT // 2, body)
            for s in range(2):
                pool.wait_ge(x_stored[s], 16 * (TT // 2))

        @block.scalar
        def _(act):
            for k in range(KT):
                act.wait_ge(w_loaded, 16 * (k + 1))
                nc.scalar.activation(w_hi[:, k, :], w_raw[:], ACT.Copy).then_inc(hi_done, 1)

            def body(i, first):
                for s in range(2):
                    t = 2 * i + s
                    for n in range(2):
                        if n == 0:
                            act.wait_ge(tile_mm, t + 1)
                            if not (first and s == 0):
                                act.wait_ge(turned_done, t)
                        else:
                            act.wait_ge(x1_done, t + 1)
                            act.wait_ge(sum_done, 2 * t + 1)
                        nc.scalar.activation(h[:], (psum[s] if n == 0 else x[s])[:], ACT.Square,
                                             accum_out=stat[:, s, n:n + 1]).then_inc(sum_done, 1)
                        act.wait_ge(mean_done, 2 * t + n + 1)
                        nc.scalar.activation(stat[:, s, n:n + 1], stat[:, s, n:n + 1], ACT.Sqrt).then_inc(root_done, 1)
                    act.wait_ge(turned_done, t + 1)
                    nc.scalar.activation(hT_hi[:, :, bass.ds(t * P, P)], turned[s][:].rearrange("p (k t) -> p k t", k=KT),
                                         ACT.Copy).then_inc(thi, 1)
            pairs(act, 0, TT // 2, body)

        @block.vector
        def _(dve):
            for k in range(KT):
                dve.wait_ge(hi_done, k + 1)
                nc.vector.tensor_tensor(w_lo[:, k, :], w_raw[:], w_hi[:, k, :].bitcast(F32), ALU.subtract).then_inc(lo_done, 1)
            dve.wait_ge(vec_loaded, 32)

            def rstd(t, s, n):
                dve.wait_ge(sum_done, 2 * t + n + 1)
                cell = stat[:, s, n:n + 1]
                nc.vector.tensor_scalar(cell, cell, 1.0 / D_MODEL, EPS, ALU.mult, ALU.add).then_inc(mean_done, 1)
                dve.wait_ge(root_done, 2 * t + n + 1)
                nc.vector.reciprocal(cell, cell).then_inc(rstd_done, 1)
                dve.wait_ge(rstd_done, 2 * t + n + 1)
                return cell

            def body(i, first):
                for s in range(2):
                    t = 2 * i + s
                    cell = rstd(t, s, 0)
                    nc.vector.scalar_tensor_tensor(out=norm[:], in0=psum[s][:], scalar=cell, in1=w_post[:],
                                                   op0=ALU.mult, op1=ALU.mult).then_inc(normed, 1)
                    dve.wait_ge(normed, t + 1)
                    dve.wait_ge(x_loaded[s], 16 * i + 16)
                    nc.vector.tensor_tensor(x[s][:], x[s][:], norm[:], ALU.add).then_inc(x1_done, 1)
                    cell = rstd(t, s, 1)
                    nc.vector.scalar_tensor_tensor(out=h[:], in0=x[s][:], scalar=cell, in1=w_pre[:],
                                                   op0=ALU.mult, op1=ALU.mult).then_inc(h_done, 1)
                    dve.wait_ge(thi, t + 1)
                    ts = bass.ds(t * P, P)
                    nc.vector.tensor_tensor(hT_lo[:, :, ts], turned[s][:].rearrange("p (k t) -> p k t", k=KT),
                                            hT_hi[:, :, ts].bitcast(F32), ALU.subtract).then_inc(tlo, 1)
            pairs(dve, 0, TT // 2, body)

        @block.tensor
        def _(pe):
            def turn(t):
                pe.wait_ge(h_done, t + 1)
                if t >= 2:
                    pe.wait_ge(tlo, t - 1)
                for k in range(KT):
                    last = pe.transpose(turned[t % 2][:, k * P:(k + 1) * P], h[:, k * P:(k + 1) * P], ident[:])
                last.then_inc(turned_done, 1)

            for t in range(TT):
                ts = slice(t * P, (t + 1) * P)
                if t >= 2:
                    pe.wait_ge(normed, t - 1)
                for k in range(KT):
                    if t == 0:
                        pe.wait_ge(lo_done, k + 1)
                    for n, (m, w) in enumerate(((mixed_hi, w_hi), (mixed_hi, w_lo), (mixed_lo, w_hi))):
                        for half in range(2):
                            hs = slice(half * HALF, (half + 1) * HALF)
                            last = pe.matmul(psum[t % 2][:, hs], m[:, k, ts], w[:, k, hs], start=k == 0 and n == 0,
                                             stop=k == KT - 1 and n == 2)
                last.then_inc(tile_mm, 1)
                if t:
                    turn(t - 1)
            turn(TT - 1)


FG = D_FF // HALF
UPG = HALF // P


def stage_mlp(nc, ap, keep, sem):
    with ExitStack() as ctx:
        def sb(name, shape, dt=F32):
            return ctx.enter_context(nc.sbuf_tensor(name, shape, dt))
        hT_hi, hT_lo, out_sum = keep["mixed_hi"], keep["mixed_lo"], keep["out_sum"]
        up_raw, up_hi, up_lo = sb("up_raw", [P, KT, P]), sb("up_hi", [P, KT, P], F32R), sb("up_lo", [P, KT, P], F32R)
        dn_raw, dn_hi, dn_lo = (sb(f"down_{n}", [P, UPG, 2 * P], d) for n, d in (("raw", F32), ("hi", F32R), ("lo", F32R)))
        relu, square = sb("relu", [P, SEQ]), sb("relu_squared", [P, SEQ])
        ff_hi = [sb(f"ff_hi{s}", [P, UPG, SEQ], F32R) for s in range(2)]
        ff_lo = [sb(f"ff_lo{s}", [P, UPG, SEQ], F32R) for s in range(2)]
        ps_up = ctx.enter_context(nc.psum_tensor("ps_up", [P, SEQ], F32))
        ps_dn = [ctx.enter_context(nc.psum_tensor(f"ps_down{s}", [P, SEQ], F32)) for s in range(2)]
        up_loaded, dn_loaded = sem("up_loaded"), sem("down_loaded")
        up_hi_done, up_lo_done, dn_hi_done, dn_lo_done = sem("up_hi_done"), sem("up_lo_done"), sem("down_hi_done"), sem("down_lo_done")
        up_mm, dn_mm, relu_done, square_done = sem("up_mm"), sem("down_mm"), sem("relu_done"), sem("square_done")
        ffhi_done, fflo_done, added = sem("ff_hi_done"), sem("ff_lo_done"), sem("down_added")
        block = ctx.enter_context(nc.Block())

        def groups(engine, up, down):
            up(0, 0, 0, True)
            with engine.Fori(1, UPG) as m:
                up(0, m, 0, False)
            up(1, 0, 1, False)
            down(0, 0, 0, True, False)
            with engine.Fori(1, UPG) as m:
                up(1, m, 1, False)
                down(0, m, 0, False, False)
            with engine.Fori(1, FG // 2) as i:
                for s in range(2):
                    with engine.Fori(0, UPG) as m:
                        up(2 * i + s, m, s, False)
                        down(2 * i + s - 1, m, 1 - s, False, True)
            with engine.Fori(0, UPG) as m:
                down(FG - 1, m, 1, False, True)

        @block.sync
        def _(sp):
            def up(g, m, slot, fresh):
                q = g * UPG + m
                if not fresh:
                    sp.wait_ge(up_lo_done, q)
                sp.dma_start(up_raw[:], ap["w_up"][:, bass.ds(q * P, P)].rearrange("(k p) c -> p k c", p=P)).then_inc(up_loaded, 16)

            def down(g, m, slot, fresh, add):
                q = g * UPG + m
                if not fresh:
                    sp.wait_ge(dn_lo_done, q)
                sp.dma_start(dn_raw[:], ap["w_down"][bass.ds(g * HALF, HALF), bass.ds(m * 2 * P, 2 * P)]
                             .rearrange("(k p) c -> p k c", p=P)).then_inc(dn_loaded, 16)
            groups(sp, up, down)

        @block.scalar
        def _(act):
            def up(g, m, slot, fresh):
                q = g * UPG + m
                act.wait_ge(up_loaded, 16 * q + 16)
                if not fresh:
                    act.wait_ge(up_mm, q)
                nc.scalar.activation(up_hi[:], up_raw[:], ACT.Copy).then_inc(up_hi_done, 1)
                act.wait_ge(up_mm, q + 1)
                if not fresh:
                    act.wait_ge(square_done, q)
                nc.scalar.activation(relu[:], ps_up[:], ACT.Relu).then_inc(relu_done, 1)
                act.wait_ge(square_done, q + 1)
                nc.scalar.activation(ff_hi[slot][:, bass.ds(m, 1), :], square[:].unsqueeze(1), ACT.Copy).then_inc(ffhi_done, 1)

            def down(g, m, slot, fresh, add):
                q = g * UPG + m
                act.wait_ge(dn_loaded, 16 * q + 16)
                if not fresh:
                    act.wait_ge(dn_mm, 2 * q)
                nc.scalar.activation(dn_hi[:], dn_raw[:], ACT.Copy).then_inc(dn_hi_done, 1)
            groups(act, up, down)

        @block.vector
        def _(dve):
            def up(g, m, slot, fresh):
                q = g * UPG + m
                dve.wait_ge(up_hi_done, q + 1)
                nc.vector.tensor_tensor(up_lo[:], up_raw[:], up_hi[:].bitcast(F32), ALU.subtract).then_inc(up_lo_done, 1)
                dve.wait_ge(relu_done, q + 1)
                if not fresh:
                    dve.wait_ge(fflo_done, q)
                nc.vector.tensor_tensor(square[:], relu[:], relu[:], ALU.mult).then_inc(square_done, 1)
                dve.wait_ge(ffhi_done, q + 1)
                nc.vector.tensor_tensor(ff_lo[slot][:, bass.ds(m, 1), :], square[:].unsqueeze(1),
                                        ff_hi[slot][:, bass.ds(m, 1), :].bitcast(F32), ALU.subtract).then_inc(fflo_done, 1)

            def down(g, m, slot, fresh, add):
                q = g * UPG + m
                dve.wait_ge(dn_hi_done, q + 1)
                nc.vector.tensor_tensor(dn_lo[:], dn_raw[:], dn_hi[:].bitcast(F32), ALU.subtract).then_inc(dn_lo_done, 1)
                for s in range(2):
                    dve.wait_ge(dn_mm, 2 * q + s + 1)
                    total = out_sum[:, bass.ds(m * 2 + s, 1), :]
                    if add:
                        dve.wait_ge(added, 2 * q + s - 2 * UPG + 1)
                        nc.vector.tensor_tensor(total, total, ps_dn[s][:].unsqueeze(1), ALU.add).then_inc(added, 1)
                    else:
                        nc.vector.tensor_copy(total, ps_dn[s][:].unsqueeze(1)).then_inc(added, 1)
            groups(dve, up, down)

        @block.tensor
        def _(pe):
            def up(g, m, slot, fresh):
                q = g * UPG + m
                pe.wait_ge(up_lo_done, q + 1)
                if not fresh:
                    pe.wait_ge(relu_done, q)
                unit_matmuls(pe, ps_up, up_hi, up_lo, hT_hi, hT_lo).then_inc(up_mm, 1)

            def down(g, m, slot, fresh, add):
                q = g * UPG + m
                pe.wait_ge(dn_lo_done, q + 1)
                pe.wait_ge(fflo_done, g * UPG + UPG)
                for s in range(2):
                    if not fresh:
                        pe.wait_ge(added, 2 * q + s - 1)
                    cs = slice(s * P, (s + 1) * P)
                    unit_matmuls(pe, ps_dn[s], dn_hi[:, :, cs], dn_lo[:, :, cs], ff_hi[slot], ff_lo[slot], kt=UPG).then_inc(dn_mm, 1)
            groups(pe, up, down)


def stage_last(nc, ap, keep, sem):
    with ExitStack() as ctx:
        def sb(name, shape, dt=F32):
            return ctx.enter_context(nc.sbuf_tensor(name, shape, dt))
        out_sum, ident = keep["out_sum"], keep["ident"]
        x = [sb(f"last_x{s}", [P, D_MODEL]) for s in range(TT)]
        junk = sb("last_squares", [P, D_MODEL])
        w_post = sb("last_w", [P, D_MODEL])
        norm = [sb(f"last_norm{s}", [P, D_MODEL]) for s in range(2)]
        stat = sb("last_stats", [P, TT])
        root = sb("last_roots", [P, TT])
        turned = [ctx.enter_context(nc.psum_tensor(f"last_turned{s}", [P, D_MODEL], F32)) for s in range(4)]
        loaded, w_loaded, stored = sem("last_x_loaded"), sem("last_w_loaded"), sem("out_stored")
        turned_done, sum_done, mean_done, root_done, rstd_done = sem("last_turned"), sem("last_sums"), sem("last_means"), sem("last_roots"), sem("last_rstds")
        normed, added = sem("last_normed"), sem("last_added")
        block = ctx.enter_context(nc.Block())

        @block.sync
        def _(sp):
            sp.dma_start(w_post[:], ap["norm_mlp_post"].partition_broadcast(P)).then_inc(w_loaded, 16)
            for t in range(TT):
                sp.dma_start(x[t][:], ap["x1"][t * P:(t + 1) * P, :]).then_inc(loaded, 16)
            for t in range(TT):
                sp.wait_ge(added, t + 1)
                sp.dma_start(ap["out"][t * P:(t + 1) * P, :], x[t][:]).then_inc(stored, 16)
            sp.wait_ge(stored, 16 * TT)

        @block.scalar
        def _(act):
            for t in range(TT):
                act.wait_ge(turned_done, t + 1)
                if t:
                    act.wait_ge(sum_done, t)
                nc.scalar.activation(junk[:], turned[t % 4][:], ACT.Square, accum_out=stat[:, t:t + 1]).then_inc(sum_done, 1)
                act.wait_ge(mean_done, t + 1)
                nc.scalar.activation(root[:, t:t + 1], stat[:, t:t + 1], ACT.Sqrt).then_inc(root_done, 1)

        @block.vector
        def _(dve):
            dve.wait_ge(w_loaded, 16)
            dve.wait_ge(loaded, 16 * TT)
            for t in range(TT):
                cell = stat[:, t:t + 1]
                dve.wait_ge(sum_done, t + 1)
                nc.vector.tensor_scalar(cell, cell, 1.0 / D_MODEL, EPS, ALU.mult, ALU.add).then_inc(mean_done, 1)
                dve.wait_ge(root_done, t + 1)
                nc.vector.reciprocal(root[:, t:t + 1], root[:, t:t + 1]).then_inc(rstd_done, 1)
                dve.wait_ge(rstd_done, t + 1)
                if t >= 2:
                    dve.wait_ge(added, t - 1)
                nc.vector.scalar_tensor_tensor(out=norm[t % 2][:], in0=turned[t % 4][:], scalar=root[:, t:t + 1], in1=w_post[:],
                                               op0=ALU.mult, op1=ALU.mult).then_inc(normed, 1)
                dve.wait_ge(normed, t + 1)
                nc.vector.tensor_tensor(x[t][:], x[t][:], norm[t % 2][:], ALU.add).then_inc(added, 1)

        @block.tensor
        def _(pe):
            for t in range(TT):
                if t >= 4:
                    pe.wait_ge(normed, t - 3)
                for k in range(KT):
                    last = pe.transpose(turned[t % 4][:, k * P:(k + 1) * P], out_sum[:, k, t * P:(t + 1) * P], ident[:])
                last.then_inc(turned_done, 1)


def build(nc, ap):
    with ExitStack() as ctx:
        attended = ctx.enter_context(ExitStack())

        def sb(name, shape, dt=F32, scope=ctx, side=None):
            return scope.enter_context(nc.sbuf_tensor(name, shape, dt, side=side))

        used = []

        def sem(name):
            used.append(nc.alloc_semaphore(name=name))
            return used[-1]

        def clear_semaphores():
            nc.clear_and_free_semaphores(used)
            used.clear()
            nc.all_engine_barrier()

        keep = {"ident": sb("ident", [P, P]), "vec": sb("vec", [P, V_N])}
        with ExitStack() as mid:
            keep |= {
                "trig": sb("trig", [P, SEQ], scope=mid),
                "lat_hi": sb("lat_hi", [P, 4, SEQ], F32R, scope=mid),
                "lat_lo": sb("lat_lo", [P, 4, SEQ], F32R, scope=mid),
                "kpe": sb("rope_key", [P, SEQ], scope=mid),
                "dt_tok": sb("dt_tok", [P, TT * 2 * HEADS], scope=mid),
                "la_tok": sb("la_tok", [P, TT * 2 * HEADS], scope=mid),
            }
            with ExitStack() as raw:
                keep["lat"] = sb("latents", [P, 4, SEQ], scope=raw)
                with ExitStack() as inner:
                    keep["kraw"] = sb("rope_key_raw", [2 * ROPE, SEQ], scope=inner)
                    keep["hT_hi"] = sb("hT_hi", [P, KT, SEQ], F32R, scope=inner)
                    keep["hT_lo"] = sb("hT_lo", [P, KT, SEQ], F32R, scope=inner)
                    stage_norm_in(nc, ap, keep, sem)
                    stage_in_proj(nc, ap, keep, sem)
                stage_latents(nc, ap, keep, sem)
            stage_ssd(nc, ap, keep, sem)
            with ExitStack() as yt:
                keep["yT_hi"] = sb("yT_hi", [P, YT, SEQ], F32R, scope=yt)
                keep["yT_lo"] = sb("yT_lo", [P, YT, SEQ], F32R, scope=yt)
                stage_gate_y(nc, ap, keep, sem)
                stage_ssm_out(nc, ap, keep, sem)
            clear_semaphores()
            keep["attn"] = sb("attn", [P, KT, SEQ], scope=attended, side="right")
            stage_attention(nc, ap, keep, sem)
        with ExitStack() as merged:
            keep["mixed_hi"] = sb("mixed_hi", [P, KT, SEQ], F32R, scope=merged)
            keep["mixed_lo"] = sb("mixed_lo", [P, KT, SEQ], F32R, scope=merged)
            stage_merge(nc, ap, keep, sem)
            attended.close()
            stage_out_proj(nc, ap, keep, sem)
            keep["out_sum"] = sb("out_sum", [P, KT, SEQ], scope=ctx, side="right")
            stage_mlp(nc, ap, keep, sem)
        stage_last(nc, ap, keep, sem)


SCRATCH = {"gates": (2 * D_MODEL, SEQ), "CT": (GROUPS * N_STATE, SEQ), "BT": (GROUPS * N_STATE, SEQ),
           "tok": (SEQ, TOK_W), "la": (2 * HEADS, SEQ), "ends": (2 * HEADS, TT), "y": (SEQ, D_INNER),
           "sums": (A_HEADS, SEQ), "recip": (A_HEADS, SEQ), "mixed": (D_MODEL, SEQ), "x1": (SEQ, D_MODEL)}


def host_layout(inputs):
    a = {k: np.ascontiguousarray(np.asarray(v)[0]) for k, v in inputs.items()}
    w_in = a["w_in"]
    vec = np.zeros((P, V_N), np.float32)
    def cols(at, x):
        x = x.reshape(-1, P).T
        vec[:, at:at + x.shape[1]] = x
    vec[:, V_CONVW:V_CONVB] = a["conv_w"].reshape(TAPS, 32, P).transpose(2, 1, 0).reshape(P, -1)
    cols(V_CONVB, a["conv_b"])
    cols(V_GATEB, a["gate_b"])
    cols(V_QN, a["q_a_norm"])
    cols(V_KVN, a["kv_a_norm"])
    vec[:2 * HEADS, V_DTB] = np.concatenate([a["dt_bias_fwd"], a["dt_bias_bwd"]])
    vec[:2 * HEADS, V_ALOG] = np.concatenate([a["a_log_fwd"], a["a_log_bwd"]])
    freq = (np.float32(10000.0) ** (-np.arange(0, ROPE, 2, dtype=np.float32) / np.float32(ROPE))).astype(np.float32)
    vec[:, V_FREQ] = np.tile(freq, P // len(freq))
    vec[:, V_SIGN] = np.tile(np.repeat(np.float32([-1, 1]), ROPE // 2), P // ROPE)
    rope = w_in[:, COL_ROPE:COL_ROPE + ROPE]
    wq = a["w_q_b"].reshape(QR, A_HEADS, QK)
    out = {
        "x": a["x"], "positions": a["positions"], "norm_mix_pre": a["norm_mix_pre"], "w_in": w_in, "vec": vec,
        "w_rope": np.concatenate([rope, rope[:, ROPE // 2:], rope[:, :ROPE // 2], np.zeros((D_MODEL, 64), np.float32)], 1),
        "w_q": np.concatenate([wq, wq[:, :, QK - ROPE // 2:], wq[:, :, NOPE:NOPE + ROPE // 2]], 2).reshape(QR, A_HEADS * P),
    }
    for n in ("d_skip", "ssm_norm_w", "w_ssm_out", "w_kv_b", "w_mla_out", "w_out", "norm_mix_post", "norm_mlp_pre",
              "w_up", "w_down", "norm_mlp_post"):
        out[n] = a[n]
    return {k: np.ascontiguousarray(v) for k, v in out.items()}


def kernel(**inputs):
    import concourse.bacc as bacc
    from concourse.bass_utils import run_bass_kernel_spmd

    arrays = host_layout(inputs)
    nc = bacc.Bacc("TRN2", target_bir_lowering=False, num_devices=1)
    ap = {k: nc.dram_tensor(f"in_{k}", a.shape, mybir.dt.from_np(a.dtype), kind="ExternalInput").ap() for k, a in arrays.items()}
    ap |= {k: nc.dram_tensor(f"scratch_{k}", s, F32, kind="Internal").ap() for k, s in SCRATCH.items()}
    ap["out"] = nc.dram_tensor("out", (SEQ, D_MODEL), F32, kind="ExternalOutput").ap()
    build(nc, ap)
    got = run_bass_kernel_spmd(nc, [{f"in_{k}": a for k, a in arrays.items()}], core_ids=[0])
    return got.results[0]["out"].reshape(1, SEQ, D_MODEL)
```

```python
import math
from contextlib import ExitStack

import numpy as np

import concourse.bass as bass
from concourse import mybir

F32 = mybir.dt.float32
F32R = mybir.dt.float32r
I32 = mybir.dt.int32
ACT = mybir.ActivationFunctionType
ALU = mybir.AluOpType
AX = mybir.AxisListType

P = 128
SEQ = 1024
D_MODEL = 1024
HALF = 512
NHALF = SEQ // HALF
TT = SEQ // P
KT = D_MODEL // P
EPS = 1e-6

D_INNER = 2048
HEADS = 32
HD = 64
GROUPS = 8
HPG = HEADS // GROUPS
GW = HPG * HD
N_STATE = 128
TAPS = 5
QR = 256
KVR = 256
ROPE = 32
NOPE = 64
VD = 64
A_HEADS = 16
QK = NOPE + ROPE
D_FF = 4096
SM_SCALE = float(QK) ** -0.5

ROUND = 1.5 * 2.0 ** 23
TWO_PI_1 = 6.28125
TWO_PI_2 = math.floor((2 * math.pi - TWO_PI_1) * 2 ** 20) / 2 ** 20
TWO_PI_3 = 2 * math.pi - TWO_PI_1 - TWO_PI_2
PI_F32 = 3.1415925

COL_Z = 0
COL_X = D_INNER
COL_B = COL_X + D_INNER
COL_C = COL_B + GROUPS * N_STATE
COL_DT = COL_C + GROUPS * N_STATE
COL_Q = COL_DT + 2 * HEADS
COL_KV = COL_Q + QR
COL_ROPE = COL_KV + KVR
COL_GATE = COL_ROPE + ROPE
D_IN = COL_GATE + 2 * D_MODEL

V_CONVW = 0
V_CONVB = V_CONVW + 32 * TAPS
V_GATEB = V_CONVB + 32
V_QN = V_GATEB + 16
V_KVN = V_QN + 2
V_DTB = V_KVN + 2
V_ALOG = V_DTB + 1
V_FREQ = V_ALOG + 1
V_SIGN = V_FREQ + 1
V_N = V_SIGN + 1

TOK_B = 0
TOK_X = GROUPS * N_STATE
TOK_Z = TOK_X + D_INNER
TOK_W = TOK_Z + D_INNER

U_LAT = 0
U_DT = 4
U_ROPE = 5
U_GATE = 6
U_C = U_GATE + 16
U_B = U_C + 8
U_X = U_B + 8
U_Z = U_X + 16
U_END = U_Z + 16
LAT_UNIT = U_GATE + 4


def unit_matmuls(pe, psum, w_hi, w_lo, act_hi, act_lo, kt=KT, start=True, stop=True, split=None):
    for k in range(kt):
        if split is not None:
            pe.wait_ge(split, k + 1)
        for n, (w, a) in enumerate(((w_hi, act_hi), (w_hi, act_lo), (w_lo, act_hi))):
            for h in range(NHALF):
                last = pe.matmul(psum[:, h * HALF:(h + 1) * HALF], w[:, k, :], a[:, k, h * HALF:(h + 1) * HALF],
                                 start=start and k == 0 and n == 0, stop=stop and k == kt - 1 and n == 2)
    return last


def pairs(engine, lo, hi, body):
    body(lo, True)
    if hi - lo > 1:
        with engine.Fori(lo + 1, hi) as i:
            body(i, False)


def stage_norm_in(nc, ap, keep, sem):
    with ExitStack() as ctx:
        def sb(name, shape, dt=F32):
            return ctx.enter_context(nc.sbuf_tensor(name, shape, dt))
        x_in = [sb(f"n1_x{s}", [P, D_MODEL]) for s in range(4)]
        squares = sb("n1_sq", [P, D_MODEL])
        wb = sb("n1_w", [P, D_MODEL])
        h = [sb(f"n1_h{s}", [P, D_MODEL]) for s in range(2)]
        sums, means, roots, rstd = (sb(f"n1_{n}", [P, TT]) for n in ("sums", "means", "roots", "rstd"))
        turned = [ctx.enter_context(nc.psum_tensor(f"n1_turned{i}", [P, D_MODEL], F32)) for i in range(2)]
        x_loaded = [sem(f"n1_x_loaded{i}") for i in range(4)]
        vec_loaded, ident_steps = sem("vectors_loaded"), sem("ident_steps")
        sums_done, means_done, roots_done, rstd_done = sem("n1_sums"), sem("n1_means"), sem("n1_roots"), sem("n1_rstd")
        h_done, turned_done, hi_done, lo_done = sem("n1_h"), sem("n1_turned"), sem("n1_hi"), sem("n1_lo")
        hT_hi, hT_lo, ident, vec = keep["hT_hi"], keep["hT_lo"], keep["ident"], keep["vec"]
        block = ctx.enter_context(nc.Block())

        def turned_tile(t):
            return turned[t % 2][:].rearrange("p (k t) -> p k t", k=KT)

        def columns(t):
            return slice(t * P, (t + 1) * P)

        @block.sync
        def _(sp):
            for t in range(TT):
                if t >= 4:
                    sp.wait_ge(h_done, t - 3)
                sp.dma_start(x_in[t % 4][:], ap["x"][columns(t), :]).then_inc(x_loaded[t % 4], 16)
                if t == 0:
                    sp.dma_start(wb[:], ap["norm_mix_pre"].partition_broadcast(P)).then_inc(vec_loaded, 16)
                if t == 3:
                    sp.dma_start(vec[:], ap["vec"]).then_inc(vec_loaded, 16)

        @block.gpsimd
        def _(pool):
            nc.gpsimd.memset(ident[:], 0.0).then_inc(ident_steps, 1)
            pool.wait_ge(ident_steps, 1)
            nc.gpsimd.affine_select(out=ident[:], in_=ident[:], compare_op=ALU.not_equal, fill=1.0, base=0,
                                    pattern=[[-1, P]], channel_multiplier=1).then_inc(ident_steps, 1)

        @block.scalar
        def _(act):
            def copy_hi(t):
                act.wait_ge(turned_done, t + 1)
                nc.scalar.activation(hT_hi[:, :, columns(t)], turned_tile(t), ACT.Copy).then_inc(hi_done, 1)

            for t in range(TT):
                act.wait_ge(x_loaded[t % 4], 16 * (t // 4 + 1))
                if t:
                    act.wait_ge(sums_done, t)
                nc.scalar.activation(squares[:], x_in[t % 4][:], ACT.Square, accum_out=sums[:, t:t + 1]).then_inc(sums_done, 1)
                act.wait_ge(means_done, t + 1)
                nc.scalar.activation(roots[:, t:t + 1], means[:, t:t + 1], ACT.Sqrt).then_inc(roots_done, 1)
                if t:
                    copy_hi(t - 1)
            copy_hi(TT - 1)

        @block.vector
        def _(dve):
            def split_lo(t):
                dve.wait_ge(hi_done, t + 1)
                nc.vector.tensor_tensor(hT_lo[:, :, columns(t)], turned_tile(t), hT_hi[:, :, columns(t)].bitcast(F32),
                                        ALU.subtract).then_inc(lo_done, 1)

            dve.wait_ge(vec_loaded, 32)
            for t in range(TT):
                dve.wait_ge(sums_done, t + 1)
                nc.vector.tensor_scalar(means[:, t:t + 1], sums[:, t:t + 1], 1.0 / D_MODEL, EPS, ALU.mult, ALU.add).then_inc(means_done, 1)
                dve.wait_ge(roots_done, t + 1)
                nc.vector.reciprocal(rstd[:, t:t + 1], roots[:, t:t + 1]).then_inc(rstd_done, 1)
                dve.wait_ge(rstd_done, t + 1)
                if t >= 2:
                    dve.wait_ge(turned_done, t - 1)
                nc.vector.scalar_tensor_tensor(out=h[t % 2][:], in0=x_in[t % 4][:], scalar=rstd[:, t:t + 1],
                                               in1=wb[:], op0=ALU.mult, op1=ALU.mult).then_inc(h_done, 1)
                if t:
                    split_lo(t - 1)
            split_lo(TT - 1)

        @block.tensor
        def _(pe):
            pe.wait_ge(ident_steps, 2)
            for t in range(TT):
                pe.wait_ge(h_done, t + 1)
                if t >= 2:
                    pe.wait_ge(lo_done, t - 1)
                for k in range(KT):
                    last = pe.transpose(turned[t % 2][:, k * P:(k + 1) * P], h[t % 2][:, k * P:(k + 1) * P], ident[:])
                last.then_inc(turned_done, 1)


LOG1P_TERMS = 8


def stage_in_proj(nc, ap, keep, sem):
    with ExitStack() as ctx:
        def sb(name, shape, dt=F32):
            return ctx.enter_context(nc.sbuf_tensor(name, shape, dt))
        w_raw = [sb(f"w_raw{s}", [P, KT, P]) for s in range(2)]
        w_hi = [sb(f"w_hi{s}", [P, KT, P], F32R) for s in range(2)]
        w_lo = [sb(f"w_lo{s}", [P, KT, P], F32R) for s in range(2)]
        pad = [sb(f"conv_in{s}", [P, SEQ + TAPS - 1]) for s in range(2)]
        acc = [sb(f"conv_sum{s}", [P, SEQ]) for s in range(2)]
        feat = [sb(f"feature_major{s}", [P, SEQ]) for s in range(2)]
        tok = [sb(f"token_major{s}", [P, TT, P]) for s in range(2)]
        v, e, z, z2, q = (sb(f"dt_{n}", [2 * HEADS, SEQ]) for n in "vezsq")
        ends = sb("chunk_ends", [2 * HEADS, TT])
        a_exp = sb("a_exp", [2 * HEADS, 1])
        psum = [ctx.enter_context(nc.psum_tensor(f"proj{s}", [P, SEQ], F32)) for s in range(2)]
        turned = [ctx.enter_context(nc.psum_tensor(f"turned{s}", [P, SEQ], F32)) for s in range(2)]
        w_loaded = [sem(f"w_loaded{s}") for s in range(2)]
        hi_done, lo_done, mm_done, psum_free = sem("w_hi_done"), sem("w_lo_done"), sem("proj_done"), sem("proj_read")
        pad_zeroed, conv_step, feat_done = sem("conv_pads_zeroed"), sem("conv_steps"), sem("feature_major_done")
        turned_done, tok_done = sem("turned"), sem("token_major_done")
        feat_stored = [sem(f"feature_major_stored{s}") for s in range(2)]
        tok_stored = [sem(f"token_major_stored{s}") for s in range(2)]
        dt_in, dt_step, la_stored = sem("dt_inputs"), sem("dt_steps"), sem("decays_stored")
        small_turned, rope_k = sem("dt_turned"), sem("rope_key_steps")
        hT_hi, hT_lo, ident, vec, trig = keep["hT_hi"], keep["hT_lo"], keep["ident"], keep["vec"], keep["trig"]
        lat, kpe, kraw = keep["lat"], keep["kpe"], keep["kraw"]
        krot, chain = acc[0], acc[1]
        sin_half, pos = pad[0][:, 2:2 + SEQ], pad[1][:, 2:2 + SEQ].bitcast(I32)
        angle, turns = tok[1][:].rearrange("p t c -> p (t c)"), feat[0][:]
        sin_full = tok[0][:].rearrange("p t c -> p (t c)")
        lat_squares, lat_roots = sb("lat_squares", [P, 4, SEQ]), sb("lat_roots", [P, 2, SEQ])
        ones = sb("ones", [P, P])
        ones_set, lat_squared, lat_sums, lat_means = sem("ones_set"), sem("latents_squared"), sem("latent_sums_mm"), sem("latent_means")
        lat_rooted, lat_rstd, lat_normed = sem("latent_roots"), sem("latent_rstd"), sem("latents_normed")
        pos_loaded, rope_step, sines_done = sem("positions_loaded"), sem("rope_steps"), sem("rope_sines")
        dt_tok, la_tok = keep["dt_tok"], keep["la_tok"]
        dt_last = 4 + LOG1P_TERMS + 11
        block = ctx.enter_context(nc.Block())

        def column(n, first_unit, first_column):
            return bass.ds((n - first_unit) * P + first_column, P)

        @block.sync
        def _(sp):
            def load(n, s, cols, wait=True):
                if wait:
                    sp.wait_ge(lo_done, n - 1)
                sp.dma_start(w_raw[s][:], ap["w_in"][:, cols].rearrange("(k p) c -> p k c", p=P)).then_inc(w_loaded[s], 16)

            sp.dma_start(pos, ap["positions"].partition_broadcast(P)).then_inc(pos_loaded, 16)
            for n in range(U_ROPE):
                load(n, n % 2, bass.ds(COL_Q + n * P if n < U_DT else COL_DT, P), wait=n >= 2)
            sp.wait_ge(lo_done, U_ROPE - 1)
            sp.dma_start(w_raw[1][:], ap["w_rope"].rearrange("(k p) c -> p k c", p=P)).then_inc(w_loaded[1], 16)
            for first_unit, end, first_column in ((U_GATE, U_C, COL_GATE), (U_C, U_B, COL_C), (U_B, U_X, COL_B),
                                                  (U_X, U_Z, COL_X), (U_Z, U_END, COL_Z)):
                with sp.Fori(first_unit // 2, end // 2) as i:
                    for u in range(2):
                        load(2 * i + u, u, column(2 * i + u, first_unit, first_column))

        @block.gpsimd
        def _(pool):
            nc.gpsimd.memset(ones[:], 1.0).then_inc(ones_set, 1)
            for s in range(2):
                for side in (slice(0, 2), slice(SEQ + 2, SEQ + 4)):
                    nc.gpsimd.memset(pad[s][:, side], 0.0).then_inc(pad_zeroed, 1)

            def store_feat(n, s, dram, first_unit):
                pool.wait_ge(feat_done, n - U_GATE + 1)
                pool.dma_start(dram[bass.ds((n - first_unit) * P, P), :], feat[s][:]).then_inc(feat_stored[s], 16)

            def store_tok(n, s):
                pool.wait_ge(tok_done, n - U_B + 1)
                pool.dma_start(ap["tok"][:, bass.ds((n - U_B) * P, P)].rearrange("(t p) c -> p t c", p=P),
                               tok[s][:]).then_inc(tok_stored[s], 16)

            for first_unit, end, dram in ((U_GATE, U_C, ap["gates"]), (U_C, U_B, ap["CT"])):
                with pool.Fori(first_unit // 2, end // 2) as i:
                    for u in range(2):
                        store_feat(2 * i + u, u, dram, first_unit)
            with pool.Fori(U_B // 2, U_X // 2) as i:
                for u in range(2):
                    store_feat(2 * i + u, u, ap["BT"], U_B)
                    store_tok(2 * i + u, u)
            with pool.Fori(U_X // 2, U_END // 2) as i:
                for u in range(2):
                    store_tok(2 * i + u, u)
            pool.wait_ge(dt_step, dt_last)
            pool.dma_start(ap["la"], q[:]).then_inc(la_stored, 16)
            pool.dma_start(ap["ends"], ends[:]).then_inc(la_stored, 16)
            for s in range(2):
                pool.wait_ge(feat_stored[s], 16 * ((U_X - U_GATE) // 2))
                pool.wait_ge(tok_stored[s], 16 * ((U_END - U_B) // 2))
            pool.wait_ge(la_stored, 32)

        @block.scalar
        def _(act):
            def split_hi(n, s, i):
                act.wait_ge(w_loaded[s], 16 * i + 16)
                if not isinstance(n, int) or n >= 2:
                    act.wait_ge(mm_done, n - 1)
                nc.scalar.activation(w_hi[s][:], w_raw[s][:], ACT.Copy).then_inc(hi_done, 1)

            def split_next(i, u):
                split_hi(2 * i + u + 1, 1 - u, i + u)

            def product(i, u):
                act.wait_ge(mm_done, 2 * i + u + 1)

            def tok_copy(i, u):
                n = 2 * i + u
                act.wait_ge(turned_done, n - U_B + 1)
                if not isinstance(i, int) or i > U_B // 2:
                    act.wait_ge(tok_stored[u], 16 * (i - U_B // 2))
                nc.scalar.activation(tok[u][:], turned[u][:].rearrange("p (t c) -> p t c", t=TT), ACT.Copy).then_inc(tok_done, 1)

            def tok_copy_before(i, u):
                tok_copy(i - 1 + u, 1 - u)

            def feat_store_over(i, u):
                act.wait_ge(feat_stored[u], 16 * (i - U_GATE // 2))

            split_hi(0, 0, 0)
            for n in range(U_GATE):
                split_next(n // 2, n % 2)
                product(n // 2, n % 2)
                source = psum[n % 2]
                if n < U_DT:
                    nc.scalar.activation(lat[:, n, :], source[:], ACT.Copy).then_inc(psum_free, 1)
                elif n == U_DT:
                    nc.scalar.activation(v[:], source[0:2 * HEADS, :], ACT.Identity,
                                         bias=vec[0:2 * HEADS, V_DTB:V_DTB + 1]).then_inc(psum_free, 1)
                else:
                    nc.scalar.activation(kraw[:], source[0:2 * ROPE, :], ACT.Copy).then_inc(psum_free, 1)
                if n == U_DT - 1:
                    act.wait_ge(rope_step, 8)
                    nc.scalar.activation(sin_full, angle, ACT.Sin).then_inc(sines_done, 1)
                    act.wait_ge(rope_step, 9)
                    nc.scalar.activation(sin_half, turns, ACT.Sin).then_inc(sines_done, 1)
            act.wait_ge(psum_free, U_DT + 1)
            nc.scalar.activation(e[:], v[:], ACT.Abs).then_inc(dt_in, 1)
            act.wait_ge(dt_in, 1)
            nc.scalar.activation(z[:], e[:], ACT.Exp, scale=-1.0).then_inc(dt_in, 1)
            nc.scalar.activation(a_exp[:], vec[0:2 * HEADS, V_ALOG:V_ALOG + 1], ACT.Exp).then_inc(dt_in, 1)

            def gates(i, first):
                for u in range(2):
                    split_next(i, u)
                    product(i, u)
                    if not first:
                        feat_store_over(i, u)
                    nc.scalar.activation(feat[u][:], psum[u][:], ACT.Sigmoid,
                                         bias=vec[:, bass.ds(2 * i + u - U_GATE + V_GATEB, 1)]).then_inc(feat_done, 1)
            act.wait_ge(rope_step, 14)
            gates(U_GATE // 2, True)
            for n in range(4):
                nc.scalar.activation(lat_squares[:, n, :], lat[:, n, :], ACT.Square).then_inc(lat_squared, 1)
            for i in range(U_GATE // 2 + 1, LAT_UNIT // 2 + 1):
                gates(i, False)
            for n in range(2):
                act.wait_ge(lat_means, n + 1)
                nc.scalar.activation(lat_roots[:, n, :], lat_roots[:, n, :], ACT.Sqrt).then_inc(lat_rooted, 1)
            with act.Fori(LAT_UNIT // 2 + 1, U_C // 2) as i:
                gates(i, False)

            def conv_c(i, first):
                for u in range(2):
                    split_next(i, u)
                    product(i, u)
                    if not first:
                        act.wait_ge(conv_step, TAPS * (2 * i + u - U_C - 1))
                    nc.scalar.activation(pad[u][:, 2:2 + SEQ], psum[u][:], ACT.Copy).then_inc(psum_free, 1)
                    feat_store_over(i, u)
                    act.wait_ge(conv_step, TAPS * (2 * i + u - U_C + 1))
                    nc.scalar.activation(feat[u][:], acc[u][:], ACT.Silu).then_inc(feat_done, 1)
            act.wait_ge(pad_zeroed, 4)
            pairs(act, U_C // 2, U_B // 2, conv_c)

            def conv_b(i, first):
                for u in range(2):
                    split_next(i, u)
                    product(i, u)
                    act.wait_ge(conv_step, TAPS * (2 * i + u - U_C - 1))
                    nc.scalar.activation(pad[u][:, 2:2 + SEQ], psum[u][:], ACT.Copy).then_inc(psum_free, 1)
                    if not (first and u == 0):
                        tok_copy_before(i, u)
                    feat_store_over(i, u)
                    if not first:
                        act.wait_ge(turned_done, 2 * i + u - 1 - U_B)
                    act.wait_ge(conv_step, TAPS * (2 * i + u - U_C + 1))
                    nc.scalar.activation(feat[u][:], acc[u][:], ACT.Silu).then_inc(feat_done, 1)
            conv_b(U_B // 2, True)
            conv_b(U_B // 2 + 1, False)
            with act.Fori(U_B // 2 + 2, U_X // 2) as i:
                conv_b(i, False)

            def conv_x(i, first):
                for u in range(2):
                    split_next(i, u)
                    product(i, u)
                    act.wait_ge(conv_step, TAPS * (2 * i + u - U_C - 1))
                    nc.scalar.activation(pad[u][:, 2:2 + SEQ], psum[u][:], ACT.Copy).then_inc(psum_free, 1)
                    tok_copy_before(i, u)
                    if first:
                        act.wait_ge(feat_stored[u], 16 * ((U_X - U_GATE) // 2))
                    act.wait_ge(turned_done, 2 * i + u - 1 - U_B)
                    act.wait_ge(conv_step, TAPS * (2 * i + u - U_C + 1))
                    nc.scalar.activation(feat[u][:], acc[u][:], ACT.Silu).then_inc(feat_done, 1)
            pairs(act, U_X // 2, U_Z // 2, conv_x)

            def silu_z(i, first):
                for u in range(2):
                    if not (isinstance(i, int) and 2 * i + u == U_END - 1):
                        split_next(i, u)
                    product(i, u)
                    tok_copy_before(i, u)
                    act.wait_ge(turned_done, 2 * i + u - 1 - U_B)
                    nc.scalar.activation(feat[u][:], psum[u][:], ACT.Silu).then_inc(feat_done, 1)
            with act.Fori(U_Z // 2, U_END // 2 - 1) as i:
                silu_z(i, False)
            silu_z(U_END // 2 - 1, False)
            tok_copy(U_END // 2 - 1, 1)
            for n, dst in enumerate((dt_tok, la_tok)):
                act.wait_ge(small_turned, n + 1)
                nc.scalar.activation(dst[:], turned[n][:, 0:TT * 2 * HEADS], ACT.Copy).then_inc(tok_done, 1)

        @block.vector
        def _(dve):
            def split_lo(n, s):
                dve.wait_ge(hi_done, n + 1)
                nc.vector.tensor_tensor(w_lo[s][:], w_raw[s][:], w_hi[s][:].bitcast(F32), ALU.subtract).then_inc(lo_done, 1)

            def split_next(i, u):
                split_lo(2 * i + u + 1, 1 - u)

            def angle_1():
                dve.wait_ge(pos_loaded, 16)
                nc.vector.tensor_copy(sin_half, pos).then_inc(rope_step, 1)
                dve.wait_ge(rope_step, 1)
                nc.vector.tensor_scalar(angle, sin_half, vec[:, V_FREQ:V_FREQ + 1], None, ALU.mult).then_inc(rope_step, 1)
                dve.wait_ge(rope_step, 2)
                nc.vector.tensor_scalar(turns, angle, 1.0 / (2 * math.pi), ROUND, ALU.mult, ALU.add).then_inc(rope_step, 1)
                dve.wait_ge(rope_step, 3)
                nc.vector.tensor_scalar(turns, turns, ROUND, None, ALU.subtract).then_inc(rope_step, 1)

            def angle_2():
                for n, part in enumerate((TWO_PI_1, TWO_PI_2, TWO_PI_3)):
                    dve.wait_ge(rope_step, 4 + n)
                    nc.vector.scalar_tensor_tensor(out=angle, in0=turns, scalar=-part, in1=angle,
                                                   op0=ALU.mult, op1=ALU.add).then_inc(rope_step, 1)

            def angle_3():
                dve.wait_ge(rope_step, 7)
                nc.vector.tensor_scalar(angle, angle, PI_F32, -PI_F32, ALU.min, ALU.max).then_inc(rope_step, 1)
                dve.wait_ge(rope_step, 8)
                nc.vector.tensor_scalar(turns, angle, 0.5, None, ALU.mult).then_inc(rope_step, 1)

            def trig_table():
                dve.wait_ge(sines_done, 2)
                nc.vector.tensor_tensor(sin_half, sin_half, sin_half, ALU.mult).then_inc(rope_step, 1)
                dve.wait_ge(rope_step, 10)
                for q in (1, 3):
                    s = slice(32 * q, 32 * q + 32)
                    nc.vector.tensor_scalar(trig[s, :], sin_full[s, :], vec[s, V_SIGN:V_SIGN + 1], None, ALU.mult).then_inc(rope_step, 1)
                for q in (0, 2):
                    s = slice(32 * q, 32 * q + 32)
                    nc.vector.tensor_scalar(trig[s, :], sin_half[s, :], -2.0, 1.0, ALU.mult, ALU.add).then_inc(rope_step, 1)

            split_lo(0, 0)
            for n, part in enumerate((angle_1, angle_2, angle_3, None, trig_table, None)):
                split_next(n // 2, n % 2)
                if part:
                    part()

            def softplus_1():
                dve.wait_ge(dt_in, 3)
                nc.vector.tensor_scalar(e[:], z[:], 2.0, None, ALU.add).then_inc(dt_step, 1)
                dve.wait_ge(dt_step, 1)
                nc.vector.reciprocal(q[:], e[:]).then_inc(dt_step, 1)

            def softplus_2():
                dve.wait_ge(dt_step, 2)
                nc.vector.tensor_tensor(z[:], z[:], q[:], ALU.mult).then_inc(dt_step, 1)
                dve.wait_ge(dt_step, 3)
                nc.vector.tensor_tensor(z2[:], z[:], z[:], ALU.mult).then_inc(dt_step, 1)
                dve.wait_ge(dt_step, 4)
                nc.vector.tensor_scalar(q[:], z2[:], 1.0 / (2 * LOG1P_TERMS + 1), None, ALU.mult).then_inc(dt_step, 1)
                for k in range(LOG1P_TERMS - 1):
                    dve.wait_ge(dt_step, 5 + k)
                    nc.vector.scalar_tensor_tensor(out=q[:], in0=q[:], scalar=1.0 / (2 * (LOG1P_TERMS - k) - 1), in1=z2[:],
                                                   op0=ALU.add, op1=ALU.mult).then_inc(dt_step, 1)

            def softplus_3():
                n = 4 + LOG1P_TERMS
                dve.wait_ge(dt_step, n)
                nc.vector.scalar_tensor_tensor(out=q[:], in0=q[:], scalar=1.0, in1=z[:], op0=ALU.add, op1=ALU.mult).then_inc(dt_step, 1)
                nc.vector.tensor_scalar(e[:], v[:], 0.0, None, ALU.max).then_inc(dt_step, 1)
                dve.wait_ge(dt_step, n + 2)
                nc.vector.scalar_tensor_tensor(out=v[:], in0=q[:], scalar=2.0, in1=e[:], op0=ALU.mult, op1=ALU.add).then_inc(dt_step, 1)
                dve.wait_ge(dt_step, n + 3)
                nc.vector.tensor_scalar(z[:], v[:], a_exp[:], -1.0, ALU.mult, ALU.mult).then_inc(dt_step, 1)
                nc.vector.memset(chain[0:2 * HEADS, :], 1.0).then_inc(dt_step, 1)
                dve.wait_ge(dt_step, n + 5)
                nc.vector.memset(chain[0:HEADS, :].rearrange("p (c t) -> p c t", t=P)[:, :, 0], 0.0).then_inc(dt_step, 1)
                nc.vector.memset(chain[HEADS:2 * HEADS, :].rearrange("p (c t) -> p c t", t=P)[:, :, P - 1], 0.0).then_inc(dt_step, 1)
                dve.wait_ge(dt_step, n + 7)
                nc.vector.tensor_tensor_scan(q[0:HEADS, :], chain[0:HEADS, :], z[0:HEADS, :], 0.0, ALU.mult, ALU.add).then_inc(dt_step, 1)
                nc.vector.tensor_tensor_scan(q[HEADS:, ::-1], chain[HEADS:2 * HEADS, ::-1], z[HEADS:, ::-1], 0.0,
                                             ALU.mult, ALU.add).then_inc(dt_step, 1)
                dve.wait_ge(dt_step, n + 9)
                for rows, at in ((slice(0, HEADS), P - 1), (slice(HEADS, 2 * HEADS), 0)):
                    nc.vector.tensor_copy(ends[rows, :], q[rows, :].rearrange("p (c t) -> p c t", t=P)[:, :, at]).then_inc(dt_step, 1)

            def rope_key():
                out = slice(2 * ROPE, 3 * ROPE)
                dve.wait_ge(psum_free, U_ROPE + 1)
                dve.wait_ge(rope_step, 14)
                nc.vector.tensor_tensor(kpe[out, :], kraw[0:ROPE, :], trig[0:ROPE, :], ALU.mult).then_inc(rope_k, 1)
                nc.vector.tensor_tensor(krot[out, :], kraw[ROPE:2 * ROPE, :], trig[ROPE:2 * ROPE, :], ALU.mult).then_inc(rope_k, 1)
                dve.wait_ge(rope_k, 2)
                nc.vector.tensor_tensor(kpe[out, :], kpe[out, :], krot[out, :], ALU.add).then_inc(rope_k, 1)

            def latent_means():
                for n in range(2):
                    dve.wait_ge(lat_sums, n + 1)
                    nc.vector.tensor_scalar(lat_roots[:, n, :], turned[n][:], 1.0 / QR, EPS, ALU.mult, ALU.add).then_inc(lat_means, 1)

            def latent_rstd(n):
                dve.wait_ge(lat_rooted, n + 1)
                nc.vector.reciprocal(lat_roots[:, n, :], lat_roots[:, n, :]).then_inc(lat_rstd, 1)

            def norm_latents():
                dve.wait_ge(lat_rstd, 2)
                for n in range(4):
                    nc.vector.scalar_tensor_tensor(out=lat[:, n, :], in0=lat[:, n, :], scalar=vec[:, V_QN + n:V_QN + n + 1],
                                                   in1=lat_roots[:, n // 2, :], op0=ALU.mult, op1=ALU.mult).then_inc(lat_normed, 1)

            parts = (softplus_1, softplus_2, softplus_3, rope_key, latent_means, None, lambda: latent_rstd(0),
                     lambda: latent_rstd(1), norm_latents, None)
            for n, part in enumerate(parts):
                split_next((U_GATE + n) // 2, (U_GATE + n) % 2)
                if part:
                    part()
            with dve.Fori((U_GATE + len(parts)) // 2, U_C // 2) as i:
                for u in range(2):
                    split_next(i, u)

            def conv(first_unit, first_tile):
                def body(i, first):
                    for u in range(2):
                        split_next(i, u)
                        n = 2 * i + u
                        tile = n - first_unit + first_tile
                        step = TAPS * (n - U_C)
                        dve.wait_ge(psum_free, n - U_C + U_GATE + 1)
                        if not first:
                            dve.wait_ge(feat_done, n - 1 - U_GATE)
                        nc.vector.tensor_scalar(acc[u][:], pad[u][:, 0:SEQ], vec[:, bass.ds(tile * TAPS + V_CONVW, 1)],
                                                vec[:, bass.ds(tile + V_CONVB, 1)], ALU.mult, ALU.add).then_inc(conv_step, 1)
                        for k in range(1, TAPS):
                            dve.wait_ge(conv_step, step + k)
                            nc.vector.scalar_tensor_tensor(out=acc[u][:], in0=pad[u][:, k:k + SEQ],
                                                           scalar=vec[:, bass.ds(tile * TAPS + V_CONVW + k, 1)], in1=acc[u][:],
                                                           op0=ALU.mult, op1=ALU.add).then_inc(conv_step, 1)
                return body
            dve.wait_ge(pad_zeroed, 4)
            pairs(dve, U_C // 2, U_B // 2, conv(U_C, 24))
            for first_unit, end, tile in ((U_B, U_X, 16), (U_X, U_Z, 0)):
                with dve.Fori(first_unit // 2, end // 2) as i:
                    conv(first_unit, tile)(i, False)
            with dve.Fori(U_Z // 2, U_END // 2 - 1) as i:
                for u in range(2):
                    split_next(i, u)
            split_next(U_END // 2 - 1, 0)

        @block.tensor
        def _(pe):
            def multiply(i, u):
                pe.wait_ge(lo_done, 2 * i + u + 1)
                unit_matmuls(pe, psum[u], w_hi[u], w_lo[u], hT_hi, hT_lo).then_inc(mm_done, 1)

            def turn(i, u):
                n = 2 * i + u
                pe.wait_ge(feat_done, n - U_GATE + 1)
                if not isinstance(i, int) or i > U_B // 2:
                    pe.wait_ge(tok_done, n - 1 - U_B)
                for t in range(TT):
                    last = pe.transpose(turned[u][:, t * P:(t + 1) * P], feat[u][:, t * P:(t + 1) * P], ident[:])
                last.then_inc(turned_done, 1)

            def turn_before(i, u):
                turn(i - 1 + u, 1 - u)

            for n in range(U_GATE):
                if n >= 2:
                    pe.wait_ge(psum_free, n - 1)
                multiply(n // 2, n % 2)

            def gates(i, first):
                for u in range(2):
                    n = 2 * i + u
                    if first:
                        pe.wait_ge(psum_free, n - 1)
                    else:
                        pe.wait_ge(feat_done, n - 1 - U_GATE)
                    multiply(i, u)
            gates(U_GATE // 2, True)
            pe.wait_ge(ones_set, 1)
            pe.wait_ge(lat_squared, 4)
            for n in range(2):
                for half in range(NHALF):
                    hs = slice(half * HALF, (half + 1) * HALF)
                    for m in range(2):
                        last = pe.matmul(turned[n][:, hs], ones[:], lat_squares[:, 2 * n + m, hs], start=m == 0, stop=m == 1)
                last.then_inc(lat_sums, 1)
            with pe.Fori(U_GATE // 2 + 1, U_C // 2) as i:
                gates(i, False)

            def conv_c(i, first):
                for u in range(2):
                    n = 2 * i + u
                    if first:
                        pe.wait_ge(feat_done, n - 1 - U_GATE)
                    else:
                        pe.wait_ge(psum_free, n - 1 - U_C + U_GATE)
                    multiply(i, u)
            pairs(pe, U_C // 2, U_B // 2, conv_c)

            def conv_turned(i, first):
                for u in range(2):
                    pe.wait_ge(psum_free, 2 * i + u - 1 - U_C + U_GATE)
                    multiply(i, u)
                    if not (first and u == 0):
                        turn_before(i, u)
            conv_turned(U_B // 2, True)
            conv_turned(U_B // 2 + 1, False)
            with pe.Fori(U_B // 2 + 2, U_Z // 2) as i:
                conv_turned(i, False)

            def silu_z(i, first):
                for u in range(2):
                    n = 2 * i + u
                    if first:
                        pe.wait_ge(psum_free, n - 1 - U_C + U_GATE)
                    else:
                        pe.wait_ge(feat_done, n - 1 - U_GATE)
                    multiply(i, u)
                    turn_before(i, u)
            pairs(pe, U_Z // 2, U_END // 2, silu_z)
            turn(U_END // 2 - 1, 1)
            pe.wait_ge(dt_step, dt_last)
            pe.wait_ge(tok_done, U_END - U_B)
            for n, src in enumerate((v, q)):
                for t in range(TT):
                    last = pe.transpose(turned[n][:, t * 2 * HEADS:(t + 1) * 2 * HEADS], src[:, t * P:(t + 1) * P],
                                        ident[0:2 * HEADS, 0:2 * HEADS])
                last.then_inc(small_turned, 1)


STEPS_D = TT - 1
BEHIND = 4
SLOT = HPG * HD


def stage_ssd(nc, ap, keep, sem):
    with ExitStack() as ctx:
        def sb(name, shape, dt=F32):
            return ctx.enter_context(nc.sbuf_tensor(name, shape, dt))

        def two(name, shape, dt=F32):
            return [sb(f"{name}{s}", shape, dt) for s in range(2)]

        def ps(name, shape):
            return [ctx.enter_context(nc.psum_tensor(f"{name}{s}", shape, F32)) for s in range(2)]
        bc_raw = two("bc_raw", [P, 2, SEQ])
        b_raw = two("b_raw", [P, TT, N_STATE])
        x_raw = two("x_raw", [P, TT, SLOT])
        decay_in = two("decay_in", [P, 2, HPG, P])
        ends = sb("ends", [P, 2 * HEADS * TT])
        end_exp = sb("end_exp", [P, 2 * HEADS * TT])
        state_w = sb("state_w", [P, TT * 2 * HEADS])
        la_exp = sb("la_exp", [P, TT * 2 * HEADS])
        masks = sb("masks", [P, 2, P])
        d_all = sb("d_all", [P, HEADS])
        d_wide = [sb(f"d_wide{s}", [P, HPG, HD]) for s in range(2)]
        w_group = two("w_group", [P, TT, 2, HPG])
        xs = [two(f"xs{d}_", [P, SLOT]) for d in range(2)]
        decayed = [two(f"decayed{d}_", [P, SLOT]) for d in range(2)]
        prev = two("prev", [P, TT, 2, SLOT])
        m = two("m", [P, HPG, P])
        cb_masked = two("cb_masked", [P, 2, P])
        decay = two("decay", [P, 2, HPG, P])
        y_off = two("y_off", [P, 2, SLOT])
        y_sum = two("y_sum", [P, SLOT])
        y_skip = two("y_skip", [P, SLOT])
        y_out = two("y_out", [P, SLOT])
        ps_state_f, ps_off, ps_diag = ps("ps_state_f", [P, HALF]), ps("ps_off", [P, HALF]), ps("ps_diag", [P, HALF])
        ps_state_b = ctx.enter_context(nc.psum_tensor("ps_state_b", [P, HALF], F32))
        ps_cb = ctx.enter_context(nc.psum_tensor("ps_cb", [P, HALF], F32))
        la_tok, dt_tok = keep["la_tok"], keep["dt_tok"]

        raw_loaded = [sem(f"ssd_tokens_loaded{s}") for s in range(2)]
        bc_loaded = [sem(f"ssd_bc_loaded{s}") for s in range(2)]
        decay_loaded = [sem(f"decay_loaded{s}") for s in range(2)]
        table_loaded, table_done, masks_made = sem("ssd_tables_loaded"), sem("ssd_tables"), sem("masks_made")
        xs_done, state_mm = [sem(f"xs_done{d}") for d in range(2)], [sem(f"state_mm{d}") for d in range(2)]
        decayed_done, state_done = [sem(f"state_decayed{d}") for d in range(2)], [sem(f"state_done{d}") for d in range(2)]
        m_done = sem("m_done")
        seg_done, exp_done, cb_mm, cb_done, weighted = sem("seg_done"), sem("decay_exp"), sem("cb_mm"), sem("cb_masked"), sem("decay_weighted")
        off_mm, diag_mm, off_done, sum_done = sem("y_off_mm"), sem("y_diag_mm"), sem("y_off_done"), sem("y_sum_done")
        skip_done, y_step = sem("y_skip_done"), sem("y_out_steps")
        y_stored = [sem(f"y_stored{s}") for s in range(2)]
        state_zero, d_spread = sem("states_zeroed"), sem("d_skip_spread")
        block = ctx.enter_context(nc.Block())

        def per_token(table, c, g, first, dirs=2):
            v = table[:].rearrange("p (c d h) -> p c d h", c=TT, d=2)[:, c, first:first + dirs, bass.ds(g * HPG, HPG)]
            return v.unsqueeze(3).to_broadcast([P, dirs, HPG, HD])

        def heads(t, dirs):
            return t.rearrange("p (d h e) -> p d h e", d=dirs, h=HPG)

        def chunk_of(d, k):
            return (k, k + 1) if d == 0 else (TT - 1 - k, TT - 2 - k)

        def ps_state(d, k):
            return (ps_state_b if d else ps_state_f[k % 2])[:, 0:SLOT]

        def back_steps(c):
            return () if c < 2 else (c - 2,) if c < TT - 1 else (TT - 3, TT - 2)

        def slot_free(d, g, k):
            return STEPS_D * g + k - (1 if k else 0)

        def chunk_before(i, G, c, back=1):
            return (i, G, c - back) if c >= back else (i - 1 + G, 1 - G, TT + c - back)

        def group_loop(engine, body):
            for G in range(2):
                body(0, G, True, False)
            with engine.Fori(1, GROUPS // 2 - 1) as i:
                for G in range(2):
                    body(i, G, False, False)
            for G in range(2):
                body(GROUPS // 2 - 1, G, False, True)

        @block.sync
        def _(sp):
            sp.dma_start(ends[:], ap["ends"].rearrange("h c -> (h c)").partition_broadcast(P)).then_inc(table_loaded, 16)
            sp.dma_start(d_all[:], ap["d_skip"].partition_broadcast(P)).then_inc(table_loaded, 16)

            def load_raw(g, G):
                tok = ap["tok"].rearrange("(c p) f -> p c f", p=P)
                sp.dma_start(b_raw[G][:], tok[:, :, bass.ds(g * P + TOK_B, P)]).then_inc(raw_loaded[G], 16)
                sp.dma_start(x_raw[G][:], tok[:, :, bass.ds(g * SLOT + TOK_X, SLOT)]).then_inc(raw_loaded[G], 16)
                sp.dma_start(bc_raw[G][:, 0, :], ap["BT"][bass.ds(g * P, P), :]).then_inc(bc_loaded[G], 16)
                sp.dma_start(bc_raw[G][:, 1, :], ap["CT"][bass.ds(g * P, P), :]).then_inc(bc_loaded[G], 16)
            load_raw(0, 0)
            load_raw(1, 1)
            la = ap["la"].rearrange("(d h) t -> d h t", d=2)

            def store(i, G, c):
                g = 2 * i + G
                sp.wait_ge(y_step, 2 * (TT * g + c) + 2)
                if c == 0:
                    sp.nop(nofuse=True)
                sp.dma_start(ap["y"][c * P:(c + 1) * P, bass.ds(g * SLOT, SLOT)], y_out[c % 2][:]).then_inc(y_stored[c % 2], 16)

            def body(i, G, first, last):
                g = 2 * i + G
                opening = first and G == 0
                for c in range(TT):
                    s = c % 2
                    if not (opening and c < 2):
                        sp.wait_ge(seg_done, TT * g + c - 1)
                        if c == 0:
                            sp.nop(nofuse=True)
                    for d in range(2):
                        sp.dma_start(decay_in[s][:, d], la[d, bass.ds(g * HPG, HPG), c * P:(c + 1) * P]
                                     .partition_broadcast(P)).then_inc(decay_loaded[s], 16)
                    if c == 2 and not opening and not (last and G == 1):
                        sp.wait_ge(skip_done, TT * g)
                        sp.wait_ge(diag_mm, TT * g)
                        sp.nop(nofuse=True)
                        load_raw(g + 1, 1 - G)
                    if not (opening and c < BEHIND):
                        store(*chunk_before(i, G, c, BEHIND))
            group_loop(sp, body)
            for c in range(TT - BEHIND, TT):
                store(GROUPS // 2 - 1, 1, c)
            for s in range(2):
                sp.wait_ge(y_stored[s], 16 * (TT // 2) * GROUPS)

        @block.gpsimd
        def _(pool):
            nc.gpsimd.memset(masks[:], 1.0).then_inc(masks_made, 1)
            pool.wait_ge(masks_made, 1)
            for d, (a, b) in enumerate(((1, -1), (-1, 1))):
                nc.gpsimd.affine_select(out=masks[:, d, :], in_=masks[:, d, :], compare_op=ALU.is_ge, fill=0.0, base=0,
                                        pattern=[[a, P]], channel_multiplier=b).then_inc(masks_made, 1)
            pool.wait_ge(table_loaded, 32)
            pool.wait_ge(table_done, 5)

            def spread(g, G):
                d_here = d_all[:, bass.ds(g * HPG, HPG)].unsqueeze(2).to_broadcast([P, HPG, HD])
                nc.gpsimd.tensor_copy(d_wide[G][:], d_here).then_inc(d_spread, 1)
                w_here = state_w[:].rearrange("p (c d h) -> p c d h", c=TT, d=2)[:, :, :, bass.ds(g * HPG, HPG)]
                for d in range(2):
                    nc.gpsimd.tensor_copy(w_group[G][:, :, d], w_here[:, :, d]).then_inc(d_spread, 1)
                pool.wait_ge(d_spread, 3 * g + 3)

            def weigh(g, G, d, k):
                c = chunk_of(d, k)[0]
                if not (isinstance(g, int) and g == 0 and k < 2):
                    pool.wait_ge(state_mm[d], slot_free(d, g, k))
                nc.gpsimd.tensor_tensor(xs[d][k % 2][:].rearrange("p (h e) -> p h e", h=HPG),
                                        x_raw[G][:, c, :].rearrange("p (h e) -> p h e", h=HPG),
                                        w_group[G][:, c, d].unsqueeze(2).to_broadcast([P, HPG, HD]),
                                        ALU.mult).then_inc(xs_done[d], 1)

            def finish(i, G, c, fresh):
                s, m = c % 2, TT * (2 * i + G) + c
                pool.wait_ge(sum_done, m + 1)
                pool.wait_ge(skip_done, m + 1)
                if not fresh:
                    pool.wait_ge(y_stored[s], 16 * ((TT // 2) * (2 * i + G) + c // 2))
                nc.gpsimd.tensor_tensor(y_out[s][:], y_sum[s][:], y_off[s][:, 1], ALU.add).then_inc(y_step, 1)
                pool.wait_ge(y_step, 2 * m + 1)
                nc.gpsimd.tensor_tensor(y_out[s][:], y_out[s][:], y_skip[s][:], ALU.add).then_inc(y_step, 1)

            spread(0, 0)
            pool.wait_ge(raw_loaded[0], 32)
            for k in range(STEPS_D):
                weigh(0, 0, 1, k)

            def body(i, G, first, last):
                g = 2 * i + G
                more = not (last and G == 1)
                if more:
                    if not (first and G == 0):
                        pool.wait_ge(skip_done, TT * g)
                        pool.wait_ge(xs_done[0], STEPS_D * g)
                    spread(g + 1, 1 - G)
                for c in range(TT):
                    s, n = c % 2, TT * g + c
                    if c < STEPS_D:
                        weigh(g, G, 0, c)
                    if c == 2 and more:
                        pool.wait_ge(raw_loaded[1 - G], 32 * (i + G) + 32)
                    for k in back_steps(c) if more else ():
                        weigh(g + 1, 1 - G, 1, k)
                    if not (first and G == 0 and c < 2):
                        finish(*chunk_before(i, G, c, 2), first and G == 0 and c < 4)
                        pool.wait_ge(y_step, 2 * n - 2)
                    nc.gpsimd.tensor_tensor(y_skip[s][:].rearrange("p (h e) -> p h e", h=HPG),
                                            x_raw[G][:, c, :].rearrange("p (h e) -> p h e", h=HPG), d_wide[G][:],
                                            ALU.mult).then_inc(skip_done, 1)
                    pool.wait_ge(weighted, n + 1)
                    if not (first and G == 0 and c < 2):
                        pool.wait_ge(diag_mm, n - 1)
                    nc.gpsimd.tensor_tensor(m[s][:], decay[s][:, 0], decay[s][:, 1], ALU.add).then_inc(m_done, 1)
            group_loop(pool, body)
            for c in range(TT - 2, TT):
                finish(GROUPS // 2 - 1, 1, c, False)

        @block.scalar
        def _(act):
            act.wait_ge(table_loaded, 32)
            nc.scalar.activation(end_exp[:], ends[:], ACT.Exp).then_inc(table_done, 1)
            nc.scalar.activation(la_exp[:], la_tok[:], ACT.Exp).then_inc(table_done, 1)
            act.wait_ge(table_done, 3)
            nc.scalar.activation(state_w[:], state_w[:], ACT.Exp).then_inc(table_done, 1)

            def body(i, G, first, last):
                g = 2 * i + G
                for c in range(TT):
                    s, m = c % 2, TT * g + c
                    if not (first and G == 0 and c < 2):
                        act.wait_ge(m_done, m - 1)
                    act.wait_ge(decay_loaded[s], 32 * ((TT // 2) * g + c // 2 + 1))
                    for d in range(2):
                        for h in range(HPG):
                            col = bass.ds(g * HPG + c * 2 * HEADS + d * HEADS + h, 1)
                            last_relu = nc.scalar.activation(decay[s][:, d, h, :], decay_in[s][:, d, h, :], ACT.Relu, scale=-1.0,
                                                             bias=la_tok[:, col])
                    last_relu.then_inc(seg_done, 1)
                    act.wait_ge(seg_done, m + 1)
                    nc.scalar.activation(decay[s][:], decay[s][:], ACT.Exp, scale=-1.0).then_inc(exp_done, 1)
            group_loop(act, body)

        @block.vector
        def _(dve):
            dve.wait_ge(table_loaded, 32)
            nc.vector.tensor_tensor(state_w[:].rearrange("p (c h) -> p c h", c=TT), ends[:].rearrange("p (h c) -> p c h", c=TT),
                                    la_tok[:].rearrange("p (c h) -> p c h", c=TT), ALU.subtract).then_inc(table_done, 1)
            for G in range(2):
                nc.vector.memset(prev[G][:, 0, 0], 0.0).then_inc(state_zero, 1)
                nc.vector.memset(prev[G][:, TT - 1, 1], 0.0).then_inc(state_zero, 1)
            dve.wait_ge(state_zero, 4)
            dve.wait_ge(table_done, 4)
            nc.vector.tensor_tensor(state_w[:], state_w[:], dt_tok[:], ALU.mult).then_inc(table_done, 1)
            dve.wait_ge(table_done, 5)
            dve.wait_ge(masks_made, 3)

            def state_update(g, G, d, k):
                c, to = chunk_of(d, k)
                s, n = k % 2, STEPS_D * g + k
                if not (isinstance(g, int) and n == 0):
                    dve.wait_ge(state_done[d], n)
                decay_c = end_exp[:].rearrange("p (h c) -> p h c", c=TT)[:, bass.ds(g * HPG + d * HEADS, HPG), c]
                nc.vector.tensor_tensor(decayed[d][s][:].rearrange("p (h e) -> p h e", h=HPG),
                                        prev[G][:, c, d].rearrange("p (h e) -> p h e", h=HPG),
                                        decay_c.unsqueeze(2).to_broadcast([P, HPG, HD]), ALU.mult).then_inc(decayed_done[d], 1)
                dve.wait_ge(decayed_done[d], n + 1)
                dve.wait_ge(state_mm[d], n + 1)
                nc.vector.tensor_tensor(prev[G][:, to, d], decayed[d][s][:], ps_state(d, k),
                                        ALU.add).then_inc(state_done[d], 1)

            def y_add(i, G, c, fresh):
                g = 2 * i + G
                s, m = c % 2, TT * g + c
                dve.wait_ge(off_mm, m + 1)
                if not fresh:
                    dve.wait_ge(y_step, 2 * m - 2)
                nc.vector.tensor_tensor(y_off[s][:].rearrange("p d (h e) -> p d h e", h=HPG), heads(ps_off[s][:], 2),
                                        per_token(la_exp, c, g, 0), ALU.mult).then_inc(off_done, 1)
                dve.wait_ge(off_done, m + 1)
                dve.wait_ge(diag_mm, m + 1)
                nc.vector.tensor_tensor(y_sum[s][:], y_off[s][:, 0], ps_diag[s][:, 0:SLOT], ALU.add).then_inc(sum_done, 1)

            for k in range(STEPS_D):
                state_update(0, 0, 1, k)

            def body(i, G, first, last):
                g = 2 * i + G
                more = not (last and G == 1)
                for c in range(TT):
                    if c == 0 and not (first and G == 0):
                        dve.wait_ge(off_mm, TT * g)
                    s, n = c % 2, TT * g + c
                    fresh = first and G == 0 and c < 2
                    dve.wait_ge(cb_mm, n + 1)
                    if not fresh:
                        dve.wait_ge(weighted, n - 1)
                    nc.vector.tensor_tensor(cb_masked[s][:], ps_cb[:, 0:P].unsqueeze(1).to_broadcast([P, 2, P]), masks[:],
                                            ALU.mult).then_inc(cb_done, 1)
                    dve.wait_ge(cb_done, n + 1)
                    dve.wait_ge(exp_done, n + 1)
                    for d in range(2):
                        for h in range(HPG):
                            col = bass.ds(g * HPG + c * 2 * HEADS + d * HEADS + h, 1)
                            weigh = nc.vector.scalar_tensor_tensor(out=decay[s][:, d, h, :], in0=decay[s][:, d, h, :],
                                                                   scalar=dt_tok[:, col], in1=cb_masked[s][:, d, :],
                                                                   op0=ALU.mult, op1=ALU.mult)
                    weigh.then_inc(weighted, 1)
                    if c < STEPS_D:
                        state_update(g, G, 0, c)
                    for k in back_steps(c) if more else ():
                        state_update(g + 1, 1 - G, 1, k)
                    if not (first and G == 0 and c == 0):
                        y_add(*chunk_before(i, G, c), first and G == 0 and c <= 2)
            group_loop(dve, body)
            y_add(GROUPS // 2 - 1, 1, TT - 1, False)

        @block.tensor
        def _(pe):
            def state(g, G, d, k):
                n = STEPS_D * g + k
                pe.wait_ge(xs_done[d], n + 1)
                if not (isinstance(g, int) and g == 0 and k < 2 - d):
                    pe.wait_ge(state_done[d], n if d else slot_free(d, g, k))
                pe.matmul(ps_state(d, k), b_raw[G][:, chunk_of(d, k)[0], :], xs[d][k % 2][:], start=True, stop=True).then_inc(state_mm[d], 1)

            def cb(i, G, c):
                if c == 0:
                    pe.wait_ge(bc_loaded[G], 32 * i + 32)
                cs = slice(c * P, (c + 1) * P)
                if not (isinstance(i, int) and i == G == c == 0):
                    pe.wait_ge(cb_done, TT * (2 * i + G) + c)
                pe.matmul(ps_cb[:, 0:P], bc_raw[G][:, 0, cs], bc_raw[G][:, 1, cs], start=True, stop=True).then_inc(cb_mm, 1)

            def diagonal(i, G, c, fresh):
                s, n = c % 2, TT * (2 * i + G) + c
                pe.wait_ge(m_done, n + 1)
                if not fresh:
                    pe.wait_ge(sum_done, n - 1)
                for h in range(HPG):
                    hs = slice(h * HD, (h + 1) * HD)
                    last = pe.matmul(ps_diag[s][:, hs], m[s][:, h, :], x_raw[G][:, c, hs], start=True, stop=True)
                last.then_inc(diag_mm, 1)

            pe.wait_ge(raw_loaded[0], 32)
            for k in range(STEPS_D):
                state(0, 0, 1, k)

            cb(0, 0, 0)

            def body(i, G, first, last):
                g = 2 * i + G
                more = not (last and G == 1)
                for c in range(TT):
                    s, n = c % 2, TT * g + c
                    cs = slice(c * P, (c + 1) * P)
                    if c < STEPS_D:
                        state(g, G, 0, c)
                    if c == 2 and more:
                        pe.wait_ge(raw_loaded[1 - G], 32 * (i + G) + 32)
                    if c >= 2 and more:
                        state(g + 1, 1 - G, 1, c - 2)
                    if c == 0:
                        pe.wait_ge(state_done[1], STEPS_D * g + STEPS_D)
                    else:
                        pe.wait_ge(state_done[0], STEPS_D * g + c)
                    if not (first and G == 0 and c < 2):
                        pe.wait_ge(off_done, n - 1)
                    pe.matmul(ps_off[s][:], bc_raw[G][:, 1, cs], prev[G][:, c].rearrange("p d f -> p (d f)"),
                              start=True, stop=True).then_inc(off_mm, 1)
                    if c < TT - 1:
                        cb(i, G, c + 1)
                    elif more:
                        cb(i + G, 1 - G, 0)
                        state(g + 1, 1 - G, 1, TT - 2)
                    if not (first and G == 0 and c == 0):
                        diagonal(*chunk_before(i, G, c), first and G == 0 and c <= 2)
            group_loop(pe, body)
            diagonal(GROUPS // 2 - 1, 1, TT - 1, False)


STEPS = NHALF * TT
PBUF = 4
MAX_STEPS = (4, 6, 7, 8, 9, 10, 11, 12)
LAG = 2


def stage_attention(nc, ap, keep, sem):
    with ExitStack() as ctx:
        def sb(name, shape, dt=F32):
            return ctx.enter_context(nc.sbuf_tensor(name, shape, dt))

        def two(name, shape, dt=F32):
            return [sb(f"{name}{s}", shape, dt) for s in range(2)]
        trig, ident, kpe, lat = keep["trig"], keep["ident"], keep["kpe"], keep["lat"]
        lat_hi, lat_lo = sb("lat_hi", [P, 4, SEQ], F32R), sb("lat_lo", [P, 4, SEQ], F32R)
        lat_hi_done, lat_lo_done = sem("lat_hi_done"), sem("lat_lo_done")
        attn = keep["attn"]
        w_raw = two("qkv_raw", [P, 2, 2, P])
        w_hi, w_lo = two("qkv_hi", [P, 2, 2, P], F32R), two("qkv_lo", [P, 2, 2, P], F32R)
        q_raw = sb("q_raw", [P, SEQ])
        rot = sb("q_turned", [P, SEQ])
        kv_raw = sb("kv_raw", [P, SEQ])
        q_hi, q_lo = two("q_hi", [P, SEQ], F32R), two("q_lo", [P, SEQ], F32R)
        k_hi, k_lo = two("k_hi", [P, SEQ], F32R), two("k_lo", [P, SEQ], F32R)
        v_hi, v_lo = two("v_hi", [P, TT, P], F32R), two("v_lo", [P, TT, P], F32R)
        half_max = two("half_maxima", [P, NHALF, TT])
        maxima = two("maxima", [P, TT])
        neg_max = sb("neg_max", [TT, P], F32R)
        p_raw = [sb(f"p_raw{n}", [P, HALF]) for n in range(PBUF)]
        p_hi = [sb(f"p_hi{n}", [P, HALF], F32R) for n in range(PBUF)]
        p_lo = [sb(f"p_lo{n}", [P, HALF], F32R) for n in range(PBUF)]
        sums = sb("prob_sums", [P, NHALF, HALF])
        ps_q = ctx.enter_context(nc.psum_tensor("ps_q", [P, SEQ], F32))
        ps_kv = ctx.enter_context(nc.psum_tensor("ps_kv", [P, SEQ], F32))
        ps_s = [ctx.enter_context(nc.psum_tensor(f"ps_s{n}", [P, HALF], F32)) for n in range(2)]
        ps_o = [ctx.enter_context(nc.psum_tensor(f"ps_o{n}", [P, HALF], F32)) for n in range(2)]

        kpe_hi, kpe_lo, fill = sem("rope_key_hi"), sem("rope_key_lo"), sem("attention_fills")
        w_loaded = [sem(f"qkv_loaded{s}") for s in range(2)]
        whi_done, wlo_done, q_mm, kv_mm = sem("qkv_hi_done"), sem("qkv_lo_done"), sem("q_mm"), sem("kv_mm")
        q_copied, rope_parts, q_ready, kv_copied = sem("q_copied"), sem("q_rope_parts"), sem("q_ready"), sem("kv_copied")
        qk_hi, qk_lo, max_mm, max_done = sem("qk_hi_done"), sem("qk_lo_done"), sem("max_scores_mm"), sem("half_maxima_done")
        max_joined = sem("maxima_joined")
        max_turned, neg_done, v_turned, vhi_done, vlo_done = sem("max_turned"), sem("neg_max_done"), sem("v_turned"), sem("v_hi_done"), sem("v_lo_done")
        row_loaded = [sem(f"max_row{s}") for s in range(2)]
        s_mm, phi_done, plo_done, pv_mm = sem("scores_mm"), sem("p_hi_done"), sem("p_lo_done"), sem("pv_mm")
        o_copied, sums_copied = sem("attn_copied"), sem("sums_copied")
        sums_stored = [sem(f"sums_stored{n}") for n in range(2)]
        block = ctx.enter_context(nc.Block())
        ROWS = slice(0, QK)

        def heads_loop(engine, body):
            for s in range(2):
                body(0, s, True, False)
            with engine.Fori(1, A_HEADS // 2 - 1) as i:
                for s in range(2):
                    body(i, s, False, False)
            for s in range(2):
                body(A_HEADS // 2 - 1, s, False, True)

        @block.sync
        def _(sp):
            def load(i, s):
                h = 2 * i + s
                for n, w in enumerate((ap["w_q"], ap["w_kv_b"])):
                    sp.dma_start(w_raw[s][:, n], w[:, bass.ds(h * P, P)].rearrange("(k p) c -> p k c", p=P)).then_inc(w_loaded[s], 16)

            def row(i, s):
                sp.wait_ge(neg_done, 2 * i + s + 1)
                sp.dma_start(q_hi[s][QK:QK + 1, :].bitcast(F32).rearrange("o (t q) -> o t q", t=TT), neg_max[:].bitcast(F32)).then_inc(row_loaded[s], 16)
            load(0, 0)
            load(0, 1)
            row(0, 0)

            def body(i, s, first, last):
                h = 2 * i + s
                if not last:
                    sp.wait_ge(wlo_done, h + 1)
                    load(i + 1, s)
                if not (last and s == 1):
                    row(i + s, 1 - s)
            heads_loop(sp, body)

        @block.gpsimd
        def _(pool):
            filled = 0
            for s in range(2):
                row = slice(QK, QK + 1)
                for tile, value in ((v_hi[s][:], 0.0), (v_lo[s][:], 0.0), (q_lo[s][row, :], 0.0), (k_lo[s][row, :], 0.0),
                                    (k_hi[s][row, :], 1.0), (v_hi[s][:, :, (1 - s) * VD], 1.0)):
                    if filled:
                        pool.wait_ge(fill, filled)
                    nc.gpsimd.memset(tile.bitcast(F32), value).then_inc(fill, 1)
                    filled += 1

            def body(i, s, first, last):
                for half in range(NHALF):
                    pool.wait_ge(sums_copied, 2 * (2 * i + s) + half + 1)
                    row = (1 - s) * VD
                    pool.dma_start(ap["sums"][bass.ds(2 * i + s, 1), half * HALF:(half + 1) * HALF],
                                   sums[row:row + 1, half, :]).then_inc(sums_stored[half], 16)
            heads_loop(pool, body)
            for half in range(NHALF):
                pool.wait_ge(sums_stored[half], 16 * A_HEADS)

        @block.scalar
        def _(act):
            act.wait_ge(fill, 1)
            for s in range(2):
                nc.scalar.activation(k_hi[s][NOPE:QK, :], kpe[NOPE:QK, :], ACT.Copy).then_inc(kpe_hi, 1)

            def split_w(i, s):
                act.wait_ge(w_loaded[s], 32 * i + 32)
                if not (isinstance(i, int) and i == 0):
                    act.wait_ge(kv_mm, 2 * i + s - 1)
                nc.scalar.activation(w_hi[s][:], w_raw[s][:], ACT.Copy).then_inc(whi_done, 1)

            def copy_q(i, s):
                h = 2 * i + s
                act.wait_ge(q_mm, h + 1)
                if not (isinstance(i, int) and h == 0):
                    act.wait_ge(qk_lo, h)
                nc.scalar.activation(q_raw[0:NOPE, :], ps_q[0:NOPE, :], ACT.Copy).then_inc(q_copied, 1)

            def copy_kv(i, s):
                h = 2 * i + s
                act.wait_ge(kv_mm, h + 1)
                if not (isinstance(i, int) and h == 0):
                    act.wait_ge(v_turned, h)
                nc.scalar.activation(kv_raw[:], ps_kv[:], ACT.Copy).then_inc(kv_copied, 1)

            def split_qk(i, s):
                h = 2 * i + s
                act.wait_ge(q_ready, h + 1)
                act.wait_ge(kv_copied, h + 1)
                if not (isinstance(i, int) and i == 0):
                    act.wait_ge(s_mm, STEPS * (h - 1))
                nc.scalar.activation(q_hi[s][ROWS, :], q_raw[ROWS, :], ACT.Copy)
                nc.scalar.activation(k_hi[s][0:NOPE, :], kv_raw[0:NOPE, :], ACT.Copy).then_inc(qk_hi, 1)

            def negate_max(i, s):
                h = 2 * i + s
                act.wait_ge(max_turned, h + 1)
                if not (isinstance(i, int) and h == 0):
                    act.wait_ge(row_loaded[1 - s], 16 * (i + s))
                nc.scalar.activation(neg_max[:], ps_q[0:TT, 0:P], ACT.Copy, scale=-1.0).then_inc(neg_done, 1)

            def split_v(i, s):
                h = 2 * i + s
                act.wait_ge(v_turned, h + 1)
                if not (isinstance(i, int) and i == 0):
                    act.wait_ge(pv_mm, STEPS * (h - 1))
                nc.scalar.activation(v_hi[s][:, :, s * VD:(s + 1) * VD],
                                     ps_q[:].rearrange("p (t c) -> p t c", t=TT)[:, :, NOPE:P], ACT.Copy).then_inc(vhi_done, 1)

            def copy_sums(i, s, half, first):
                h = 2 * i + s
                act.wait_ge(pv_mm, STEPS * h + (half + 1) * TT)
                if not first:
                    act.wait_ge(sums_stored[half], 16 * h)
                row = (1 - s) * VD
                nc.scalar.activation(sums[row:row + 1, half, :], ps_o[half][row:row + 1, :], ACT.Copy).then_inc(sums_copied, 1)

            for n in range(4):
                nc.scalar.activation(lat_hi[:, n, :], lat[:, n, :], ACT.Copy).then_inc(lat_hi_done, 1)
                if n == 1:
                    split_w(0, 0)
            split_w(0, 1)
            copy_q(0, 0)
            copy_kv(0, 0)
            act.wait_ge(fill, 12)
            split_qk(0, 0)
            negate_max(0, 0)
            split_v(0, 0)

            def body(i, s, first, last):
                h = 2 * i + s
                more = not (last and s == 1)
                for j in range(STEPS):
                    if j == 1 and more:
                        copy_q(i + s, 1 - s)
                    if j == 2 and more:
                        copy_kv(i + s, 1 - s)
                    if j == 2 and not (first and s == 0):
                        copy_sums(i - 1 + s, 1 - s, 1, first)
                    if j == 3 and more:
                        split_qk(i + s, 1 - s)
                    if j == 6 and not last:
                        split_w(i + 1, s)
                    if j == 10:
                        copy_sums(i, s, 0, first and s == 0)
                    if j == 14 and more:
                        negate_max(i + s, 1 - s)
                    if j == 15 and more:
                        split_v(i + s, 1 - s)
                    b = j % PBUF
                    act.wait_ge(s_mm, STEPS * h + j + 1)
                    if not (first and s == 0 and j < PBUF):
                        act.wait_ge(pv_mm, STEPS * h + j + 1 - PBUF)
                        act.wait_ge(plo_done, STEPS * h + j + 1 - PBUF)
                    nc.scalar.activation(p_raw[b][:], ps_s[j % 2][:], ACT.Exp, scale=SM_SCALE)
                    nc.scalar.activation(p_hi[b][:], ps_s[j % 2][:], ACT.Exp, scale=SM_SCALE).then_inc(phi_done, 1)
            heads_loop(act, body)
            copy_sums(A_HEADS // 2 - 1, 1, 1, False)

        @block.vector
        def _(dve):
            dve.wait_ge(kpe_hi, 2)
            for s in range(2):
                nc.vector.tensor_tensor(k_lo[s][NOPE:QK, :], kpe[NOPE:QK, :], k_hi[s][NOPE:QK, :].bitcast(F32),
                                        ALU.subtract).then_inc(kpe_lo, 1)

            def split_w(i, s):
                dve.wait_ge(whi_done, 2 * i + s + 1)
                nc.vector.tensor_tensor(w_lo[s][:], w_raw[s][:], w_hi[s][:].bitcast(F32), ALU.subtract).then_inc(wlo_done, 1)

            def rope_q(i, s, fresh):
                h = 2 * i + s
                pe_rows = slice(NOPE, QK)
                dve.wait_ge(q_mm, h + 1)
                if not fresh:
                    dve.wait_ge(qk_lo, h)
                nc.vector.tensor_tensor(q_raw[pe_rows, :], ps_q[pe_rows, :], trig[pe_rows, :], ALU.mult)
                nc.vector.tensor_tensor(rot[pe_rows, :], ps_q[QK:P, :], trig[QK:P, :], ALU.mult).then_inc(rope_parts, 1)
                dve.wait_ge(rope_parts, h + 1)
                nc.vector.tensor_tensor(q_raw[pe_rows, :], q_raw[pe_rows, :], rot[pe_rows, :], ALU.add).then_inc(q_ready, 1)

            def split_qk(i, s):
                h = 2 * i + s
                dve.wait_ge(qk_hi, h + 1)
                nc.vector.tensor_tensor(q_lo[s][ROWS, :], q_raw[ROWS, :], q_hi[s][ROWS, :].bitcast(F32), ALU.subtract)
                nc.vector.tensor_tensor(k_lo[s][0:NOPE, :], kv_raw[0:NOPE, :], k_hi[s][0:NOPE, :].bitcast(F32),
                                        ALU.subtract).then_inc(qk_lo, 1)

            def maximum(i, s, n):
                h = 2 * i + s
                for half in range(NHALF):
                    dve.wait_ge(max_mm, STEPS * h + NHALF * n + half + 1)
                    nc.vector.reduce_max(half_max[s][:, half, n:n + 1], ps_kv[:, half * HALF:(half + 1) * HALF],
                                         AX.X).then_inc(max_done, 1)
                if n == TT - 1:
                    dve.wait_ge(max_done, STEPS * h + STEPS)
                    nc.vector.tensor_tensor(maxima[s][:], half_max[s][:, 0], half_max[s][:, 1], ALU.max).then_inc(max_joined, 1)

            def split_v(i, s):
                dve.wait_ge(vhi_done, 2 * i + s + 1)
                nc.vector.tensor_tensor(v_lo[s][:, :, s * VD:(s + 1) * VD],
                                        ps_q[:].rearrange("p (t c) -> p t c", t=TT)[:, :, NOPE:P],
                                        v_hi[s][:, :, s * VD:(s + 1) * VD].bitcast(F32), ALU.subtract).then_inc(vlo_done, 1)

            def copy_out(i, s, half):
                h = 2 * i + s
                rows = slice(s * VD, (s + 1) * VD)
                dve.wait_ge(pv_mm, STEPS * h + (half + 1) * TT)
                nc.vector.tensor_copy(attn[rows, bass.ds(i, 1), half * HALF:(half + 1) * HALF].rearrange("p o t -> p (o t)"),
                                      ps_o[half][rows, :]).then_inc(o_copied, 1)

            for n in range(4):
                dve.wait_ge(lat_hi_done, n + 1)
                nc.vector.tensor_tensor(lat_lo[:, n, :], lat[:, n, :], lat_hi[:, n, :].bitcast(F32), ALU.subtract).then_inc(lat_lo_done, 1)
                if n == 1:
                    split_w(0, 0)
            split_w(0, 1)
            rope_q(0, 0, True)
            dve.wait_ge(fill, 12)
            split_qk(0, 0)
            for n in range(TT):
                maximum(0, 0, n)
            split_v(0, 0)

            def body(i, s, first, last):
                h = 2 * i + s
                more = not (last and s == 1)
                for j in range(STEPS):
                    if j == 1 and more:
                        rope_q(i + s, 1 - s, False)
                    if j == 2 and not (first and s == 0):
                        copy_out(i - 1 + s, 1 - s, 1)
                    if j == 4 and more:
                        split_qk(i + s, 1 - s)
                    if j - 1 in MAX_STEPS and more:
                        maximum(i + s, 1 - s, MAX_STEPS.index(j - 1))
                    if j == 6 and not last:
                        split_w(i + 1, s)
                    if j == 10:
                        copy_out(i, s, 0)
                    if j == 15 and more:
                        split_v(i + s, 1 - s)
                    b = j % PBUF
                    dve.wait_ge(phi_done, STEPS * h + j + 1)
                    nc.vector.tensor_tensor(p_lo[b][:], p_raw[b][:], p_hi[b][:].bitcast(F32), ALU.subtract).then_inc(plo_done, 1)
            heads_loop(dve, body)
            copy_out(A_HEADS // 2 - 1, 1, 1)

        @block.tensor
        def _(pe):
            def project_q(i, s, fresh):
                h = 2 * i + s
                pe.wait_ge(wlo_done, h + 1)
                if not fresh:
                    pe.wait_ge(vlo_done, h)
                unit_matmuls(pe, ps_q, w_hi[s][:, 0], w_lo[s][:, 0], lat_hi[:, 0:2], lat_lo[:, 0:2], kt=2).then_inc(q_mm, 1)

            def project_kv(i, s, fresh):
                h = 2 * i + s
                if not fresh:
                    pe.wait_ge(max_done, STEPS * h)
                unit_matmuls(pe, ps_kv, w_hi[s][:, 1], w_lo[s][:, 1], lat_hi[:, 2:4], lat_lo[:, 2:4], kt=2).then_inc(kv_mm, 1)

            def max_scores(i, s, n):
                h = 2 * i + s
                pe.wait_ge(qk_hi, h + 1)
                for half in range(NHALF):
                    if n:
                        pe.wait_ge(max_done, STEPS * h + NHALF * (n - 1) + half + 1)
                    hs = slice(half * HALF, (half + 1) * HALF)
                    pe.matmul(ps_kv[:, hs], q_hi[s][ROWS, n * P:(n + 1) * P], k_hi[s][ROWS, hs],
                              start=True, stop=True).then_inc(max_mm, 1)

            def turn_max(i, s):
                h = 2 * i + s
                pe.wait_ge(max_joined, h + 1)
                pe.wait_ge(q_ready, h + 1)
                pe.wait_ge(q_copied, h + 1)
                pe.transpose(ps_q[0:TT, 0:P], maxima[s][:], ident[:]).then_inc(max_turned, 1)

            def turn_v(i, s):
                h = 2 * i + s
                pe.wait_ge(neg_done, h + 1)
                for t in range(TT):
                    last = pe.transpose(ps_q[:, t * P:(t + 1) * P], kv_raw[:, t * P:(t + 1) * P], ident[:])
                last.then_inc(v_turned, 1)

            def three(out, a, b, a_lo, b_lo, start=True, stop=True):
                pe.matmul(out, a, b, start=start, stop=False)
                pe.matmul(out, a, b_lo, start=False, stop=False)
                return pe.matmul(out, a_lo, b, start=False, stop=stop)

            def probs_v(i, s, j, fresh):
                h, b, half, t = 2 * i + s, j % PBUF, j // TT, j % TT
                pe.wait_ge(plo_done, STEPS * h + j + 1)
                if t == 0:
                    pe.wait_ge(vlo_done, h + 1)
                    if not fresh:
                        pe.wait_ge(o_copied, 2 * h + half - 1)
                        pe.wait_ge(sums_copied, 2 * h + half - 1)
                three(ps_o[half][:], v_hi[s][:, t], p_hi[b][:], v_lo[s][:, t], p_lo[b][:], t == 0, t == TT - 1).then_inc(pv_mm, 1)

            pe.wait_ge(lat_lo_done, 2)
            project_q(0, 0, True)
            pe.wait_ge(lat_lo_done, 4)
            project_kv(0, 0, True)
            pe.wait_ge(kv_copied, 1)
            pe.wait_ge(kpe_lo, 2)
            for n in range(TT):
                max_scores(0, 0, n)
            turn_max(0, 0)
            turn_v(0, 0)

            def body(i, s, first, last):
                h = 2 * i + s
                more = not (last and s == 1)
                for j in range(STEPS):
                    if j == 0 and more:
                        project_q(i + s, 1 - s, False)
                    if j == 1 and more:
                        project_kv(i + s, 1 - s, False)
                    if j == 14 and more:
                        turn_max(i + s, 1 - s)
                    if j == 15 and more:
                        turn_v(i + s, 1 - s)
                    half, t = j // TT, j % TT
                    if j == 0:
                        pe.wait_ge(row_loaded[s], 16 * i + 16)
                        pe.wait_ge(qk_lo, h + 1)
                    if not (first and s == 0 and j < 2):
                        pe.wait_ge(phi_done, STEPS * h + j - 1)
                    ks, qs = slice(t * P, (t + 1) * P), slice(half * HALF, (half + 1) * HALF)
                    rows = slice(0, QK + 1)
                    three(ps_s[j % 2][:], k_hi[s][rows, ks], q_hi[s][rows, qs], k_lo[s][rows, ks], q_lo[s][rows, qs]).then_inc(s_mm, 1)
                    if j >= LAG:
                        probs_v(i, s, j - LAG, first and s == 0)
                    elif not (first and s == 0):
                        probs_v(i - 1 + s, 1 - s, j - LAG + STEPS, False)
                    if j in MAX_STEPS and more:
                        max_scores(i + s, 1 - s, MAX_STEPS.index(j))
            heads_loop(pe, body)
            for j in range(STEPS - LAG, STEPS):
                probs_v(A_HEADS // 2 - 1, 1, j, False)


YT = D_INNER // P
YBUF = 4


def stage_gate_y(nc, ap, keep, sem):
    with ExitStack() as ctx:
        def sb(name, shape, dt=F32):
            return ctx.enter_context(nc.sbuf_tensor(name, shape, dt))
        y_in = [sb(f"y_in{s}", [P, D_INNER]) for s in range(YBUF)]
        z_in = [sb(f"z_in{h}", [P, D_INNER // 2]) for h in range(2)]
        wb = sb("ssm_norm_w", [P, D_INNER])
        squares = sb("y_squares", [P, SLOT])
        sums = [sb(f"y_sums{s}", [P, GROUPS]) for s in range(2)]
        turned = [ctx.enter_context(nc.psum_tensor(f"y_turned{s}", [P, YT, P], F32)) for s in range(2)]
        loaded, z_loaded = [sem(f"y_loaded{s}") for s in range(YBUF)], [sem(f"z_loaded{h}") for h in range(2)]
        w_loaded, gated, sums_done, stat_step = sem("ssm_norm_w_loaded"), sem("y_gated"), sem("y_group_sums"), sem("y_stat_steps")
        rooted, normed, turned_done, hi_done, lo_done = sem("y_roots"), sem("y_normed"), sem("y_turned"), sem("yT_hi"), sem("yT_lo")
        yT_hi, yT_lo, ident = keep["yT_hi"], keep["yT_lo"], keep["ident"]
        half = D_INNER // 2
        block = ctx.enter_context(nc.Block())

        @block.sync
        def _(sp):
            for t in range(TT):
                if t >= YBUF:
                    sp.wait_ge(turned_done, t - YBUF + 1)
                rows = slice(t * P, (t + 1) * P)
                sp.dma_start(y_in[t % YBUF][:], ap["y"][rows, :]).then_inc(loaded[t % YBUF], 16)
                for h in range(2):
                    if t:
                        sp.wait_ge(gated, 2 * t + h - 1)
                    sp.dma_start(z_in[h][:], ap["tok"][rows, TOK_Z + h * half:TOK_Z + (h + 1) * half]).then_inc(z_loaded[h], 16)
                if t == 0:
                    sp.dma_start(wb[:], ap["ssm_norm_w"].partition_broadcast(P)).then_inc(w_loaded, 16)

        @block.gpsimd
        def _(pool):
            for t in range(TT):
                y = y_in[t % YBUF]
                pool.wait_ge(loaded[t % YBUF], 16 * (t // YBUF + 1))
                for h in range(2):
                    hs = slice(h * half, (h + 1) * half)
                    pool.wait_ge(z_loaded[h], 16 * (t + 1))
                    nc.gpsimd.tensor_tensor(y[:, hs], y[:, hs], z_in[h][:], ALU.mult).then_inc(gated, 1)

        @block.scalar
        def _(act):
            def copy_hi(t):
                act.wait_ge(turned_done, t + 1)
                nc.scalar.activation(yT_hi[:, :, t * P:(t + 1) * P], turned[t % 2][:], ACT.Copy).then_inc(hi_done, 1)

            for t in range(TT):
                for g in range(GROUPS):
                    if g % (GROUPS // 2) == 0:
                        act.wait_ge(gated, 2 * t + 1 + g // (GROUPS // 2))
                    if t or g:
                        act.wait_ge(sums_done, GROUPS * t + g)
                    nc.scalar.activation(squares[:], y_in[t % YBUF][:, g * SLOT:(g + 1) * SLOT], ACT.Square,
                                         accum_out=sums[t % 2][:, g:g + 1]).then_inc(sums_done, 1)
                act.wait_ge(stat_step, 2 * t + 1)
                nc.scalar.activation(sums[t % 2][:], sums[t % 2][:], ACT.Sqrt).then_inc(rooted, 1)
                if t:
                    copy_hi(t - 1)
            copy_hi(TT - 1)

        @block.vector
        def _(dve):
            def split_lo(t):
                dve.wait_ge(hi_done, t + 1)
                ts = slice(t * P, (t + 1) * P)
                nc.vector.tensor_tensor(yT_lo[:, :, ts], turned[t % 2][:], yT_hi[:, :, ts].bitcast(F32), ALU.subtract).then_inc(lo_done, 1)

            dve.wait_ge(w_loaded, 16)
            for t in range(TT):
                y, stat = y_in[t % YBUF], sums[t % 2]
                dve.wait_ge(sums_done, GROUPS * (t + 1))
                nc.vector.tensor_scalar(stat[:], stat[:], 1.0 / SLOT, EPS, ALU.mult, ALU.add).then_inc(stat_step, 1)
                dve.wait_ge(rooted, t + 1)
                nc.vector.reciprocal(stat[:], stat[:]).then_inc(stat_step, 1)
                dve.wait_ge(stat_step, 2 * t + 2)
                for g in range(GROUPS):
                    gs = slice(g * SLOT, (g + 1) * SLOT)
                    last = nc.vector.scalar_tensor_tensor(out=y[:, gs], in0=y[:, gs], scalar=stat[:, g:g + 1],
                                                          in1=wb[:, gs], op0=ALU.mult, op1=ALU.mult)
                last.then_inc(normed, 1)
                if t:
                    split_lo(t - 1)
            split_lo(TT - 1)

        @block.tensor
        def _(pe):
            for t in range(TT):
                pe.wait_ge(normed, t + 1)
                if t >= 2:
                    pe.wait_ge(lo_done, t - 1)
                for k in range(YT):
                    last = pe.transpose(turned[t % 2][:, k, :], y_in[t % YBUF][:, k * P:(k + 1) * P], ident[:])
                last.then_inc(turned_done, 1)


def stage_ssm_out(nc, ap, keep, sem):
    with ExitStack() as ctx:
        def two(name, shape, dt=F32):
            return [ctx.enter_context(nc.sbuf_tensor(f"{name}{s}", shape, dt)) for s in range(2)]
        w_raw, w_hi, w_lo = two("so_raw", [P, KT, P]), two("so_hi", [P, KT, P], F32R), two("so_lo", [P, KT, P], F32R)
        gate = two("so_gate", [P, SEQ])
        psum = [ctx.enter_context(nc.psum_tensor(f"so_ps{s}", [P, SEQ], F32)) for s in range(2)]
        w_loaded, gate_loaded = [sem(f"so_w_loaded{s}") for s in range(2)], [sem(f"so_gate_loaded{s}") for s in range(2)]
        stored = [sem(f"so_stored{s}") for s in range(2)]
        hi_done, lo_done, unit_mm, gated = sem("so_hi"), sem("so_lo"), sem("so_mm"), sem("so_gated")
        yT_hi, yT_lo = keep["yT_hi"], keep["yT_lo"]
        tiles = D_MODEL // P
        block = ctx.enter_context(nc.Block())

        @block.sync
        def _(sp):
            def body(i, first):
                for u in range(4):
                    s, j = u % 2, 2 * i + u // 2
                    if not (first and u < 2):
                        sp.wait_ge(lo_done, 4 * i + u - 1)
                    w = ap["w_ssm_out"][s * KT * P:(s + 1) * KT * P, bass.ds(j * P, P)]
                    sp.dma_start(w_raw[s][:], w.rearrange("(k p) c -> p k c", p=P)).then_inc(w_loaded[s], 16)
                    if s == 1:
                        if not first:
                            sp.wait_ge(stored[u // 2], 16 * i)
                        sp.dma_start(gate[u // 2][:], ap["gates"][bass.ds(j * P, P), :]).then_inc(gate_loaded[u // 2], 16)
            pairs(sp, 0, tiles // 2, body)

        @block.gpsimd
        def _(pool):
            def body(i, first):
                for s in range(2):
                    pool.wait_ge(gated, 2 * i + s + 1)
                    pool.dma_start(ap["mixed"][bass.ds((2 * i + s) * P, P), :], gate[s][:]).then_inc(stored[s], 16)
            pairs(pool, 0, tiles // 2, body)
            for s in range(2):
                pool.wait_ge(stored[s], 16 * (tiles // 2))

        @block.scalar
        def _(act):
            def body(i, first):
                for u in range(4):
                    act.wait_ge(w_loaded[u % 2], 32 * i + 16 * (u // 2) + 16)
                    if not (first and u < 2):
                        act.wait_ge(unit_mm, 4 * i + u - 1)
                    nc.scalar.activation(w_hi[u % 2][:], w_raw[u % 2][:], ACT.Copy).then_inc(hi_done, 1)
            pairs(act, 0, tiles // 2, body)

        @block.vector
        def _(dve):
            def gate_tile(i, s):
                j = 2 * i + s
                dve.wait_ge(unit_mm, 2 * j + 2)
                dve.wait_ge(gate_loaded[s], 16 * i + 16)
                nc.vector.tensor_tensor(gate[s][:], psum[s][:], gate[s][:], ALU.mult).then_inc(gated, 1)

            def body(i, first):
                for u in range(4):
                    dve.wait_ge(hi_done, 4 * i + u + 1)
                    nc.vector.tensor_tensor(w_lo[u % 2][:], w_raw[u % 2][:], w_hi[u % 2][:].bitcast(F32), ALU.subtract).then_inc(lo_done, 1)
                    if u == 2:
                        gate_tile(i, 0)
                    if u == 0 and not first:
                        gate_tile(i - 1, 1)
            pairs(dve, 0, tiles // 2, body)
            gate_tile(tiles // 2 - 1, 1)

        @block.tensor
        def _(pe):
            def body(i, first):
                for u in range(4):
                    pe.wait_ge(lo_done, 4 * i + u + 1)
                    s, half, j = u // 2, u % 2, 2 * i + u // 2
                    if half == 0 and not first:
                        pe.wait_ge(gated, j - 1)
                    ks = slice(half * KT, (half + 1) * KT)
                    unit_matmuls(pe, psum[s], w_hi[half], w_lo[half], yT_hi[:, ks], yT_lo[:, ks],
                                 start=half == 0, stop=half == 1).then_inc(unit_mm, 1)
            pairs(pe, 0, tiles // 2, body)


def stage_merge(nc, ap, keep, sem):
    with ExitStack() as ctx:
        def sb(name, shape, dt=F32):
            return ctx.enter_context(nc.sbuf_tensor(name, shape, dt))

        def two(name, shape, dt=F32):
            return [sb(f"{name}{s}", shape, dt) for s in range(2)]
        attn, mixed_hi, mixed_lo = keep["attn"], keep["mixed_hi"], keep["mixed_lo"]
        a_hi, a_lo = sb("attn_hi", [P, KT, SEQ], F32R), sb("attn_lo", [P, KT, SEQ], F32R)
        sums = sb("sums", [A_HEADS, SEQ])
        w_raw, w_hi, w_lo = two("mo_raw", [P, KT, P]), two("mo_hi", [P, KT, P], F32R), two("mo_lo", [P, KT, P], F32R)
        gate, mixed = two("mo_gate", [P, SEQ]), two("mo_mixed", [P, SEQ])
        recip = mixed
        psum = [ctx.enter_context(nc.psum_tensor(f"mo_ps{s}", [P, SEQ], F32)) for s in range(2)]
        sums_in, sums_inv, sums_out = sem("sums_in"), sem("sums_inverted"), sem("sums_out")
        recip_in, a_step, ahi, alo = [sem(f"recip_in{s}") for s in range(2)], sem("attn_normed"), sem("attn_hi_done"), sem("attn_lo_done")
        w_loaded, gate_loaded = [sem(f"mo_w_loaded{s}") for s in range(2)], [sem(f"mo_gate_loaded{s}") for s in range(2)]
        ssm_loaded = [sem(f"mo_ssm_loaded{s}") for s in range(2)]
        hi_done, lo_done, unit_mm, gated, mixed_sum = sem("mo_hi"), sem("mo_lo"), sem("mo_mm"), sem("mo_gated"), sem("mo_sum")
        mhi, mlo = sem("mixed_hi_done"), sem("mixed_lo_done")
        tiles = D_MODEL // P
        block = ctx.enter_context(nc.Block())

        @block.sync
        def _(sp):
            sp.dma_start(sums[:], ap["sums"]).then_inc(sums_in, 16)

            def load(i, s, fresh):
                j = 2 * i + s
                if not fresh:
                    sp.wait_ge(lo_done, j - 1)
                sp.dma_start(w_raw[s][:], ap["w_mla_out"][:, bass.ds(j * P, P)].rearrange("(k p) c -> p k c", p=P)).then_inc(w_loaded[s], 16)
                if not fresh:
                    sp.wait_ge(mlo, j - 1)
                sp.dma_start(gate[s][:], ap["gates"][bass.ds(j * P + D_MODEL, P), :]).then_inc(gate_loaded[s], 16)

            def load_ssm(i, s):
                sp.dma_start(mixed[s][:], ap["mixed"][bass.ds((2 * i + s) * P, P), :]).then_inc(ssm_loaded[s], 16)
            for s in range(2):
                load(0, s, True)
            sp.wait_ge(sums_inv, 1)
            sp.dma_start(ap["recip"], sums[:]).then_inc(sums_out, 16)
            sp.wait_ge(sums_out, 16)
            for k in range(KT):
                if k >= 2:
                    sp.wait_ge(a_step, k - 1)
                for half in range(2):
                    sp.dma_start(recip[k % 2][half * VD:(half + 1) * VD, :],
                                 ap["recip"][2 * k + half, :].partition_broadcast(VD)).then_inc(recip_in[k % 2], 16)
            for s in range(2):
                sp.wait_ge(a_step, KT - 1 + s)
                load_ssm(0, s)
            with sp.Fori(1, tiles // 2) as i:
                for s in range(2):
                    load(i, s, False)
                    load_ssm(i, s)

        @block.scalar
        def _(act):
            def split_w(i, s, fresh):
                act.wait_ge(w_loaded[s], 16 * i + 16)
                if not fresh:
                    act.wait_ge(unit_mm, 2 * i + s - 1)
                nc.scalar.activation(w_hi[s][:], w_raw[s][:], ACT.Copy).then_inc(hi_done, 1)
            for s in range(2):
                split_w(0, s, True)
            for k in range(KT):
                act.wait_ge(a_step, k + 1)
                nc.scalar.activation(a_hi[:, k, :], attn[:, k, :], ACT.Copy).then_inc(ahi, 1)

            def body(i, last):
                for s in range(2):
                    j = 2 * i + s
                    act.wait_ge(mixed_sum, j + 1)
                    nc.scalar.activation(mixed_hi[:, bass.ds(j, 1), :], mixed[s][:].unsqueeze(1), ACT.Copy).then_inc(mhi, 1)
                    if not last:
                        split_w(i + 1, s, False)
            with act.Fori(0, tiles // 2 - 1) as i:
                body(i, False)
            body(tiles // 2 - 1, True)

        @block.vector
        def _(dve):
            dve.wait_ge(sums_in, 16)
            nc.vector.reciprocal(sums[:], sums[:]).then_inc(sums_inv, 1)

            def split_w(i, s):
                dve.wait_ge(hi_done, 2 * i + s + 1)
                nc.vector.tensor_tensor(w_lo[s][:], w_raw[s][:], w_hi[s][:].bitcast(F32), ALU.subtract).then_inc(lo_done, 1)
            for s in range(2):
                split_w(0, s)
            for k in range(KT + 1):
                if k < KT:
                    dve.wait_ge(recip_in[k % 2], 32 * (k // 2 + 1))
                    nc.vector.tensor_tensor(attn[:, k, :], attn[:, k, :], recip[k % 2][:], ALU.mult).then_inc(a_step, 1)
                if k:
                    dve.wait_ge(ahi, k)
                    nc.vector.tensor_tensor(a_lo[:, k - 1, :], attn[:, k - 1, :], a_hi[:, k - 1, :].bitcast(F32), ALU.subtract).then_inc(alo, 1)

            def body(i, last):
                for s in range(2):
                    j = 2 * i + s
                    dve.wait_ge(unit_mm, j + 1)
                    dve.wait_ge(gate_loaded[s], 16 * i + 16)
                    nc.vector.tensor_tensor(gate[s][:], psum[s][:], gate[s][:], ALU.mult).then_inc(gated, 1)
                    dve.wait_ge(gated, j + 1)
                    dve.wait_ge(ssm_loaded[s], 16 * i + 16)
                    nc.vector.tensor_tensor(mixed[s][:], mixed[s][:], gate[s][:], ALU.add).then_inc(mixed_sum, 1)
                    if not last:
                        split_w(i + 1, s)
                    dve.wait_ge(mhi, j + 1)
                    nc.vector.tensor_tensor(mixed_lo[:, bass.ds(j, 1), :], mixed[s][:].unsqueeze(1),
                                            mixed_hi[:, bass.ds(j, 1), :].bitcast(F32), ALU.subtract).then_inc(mlo, 1)
            with dve.Fori(0, tiles // 2 - 1) as i:
                body(i, False)
            body(tiles // 2 - 1, True)

        @block.tensor
        def _(pe):
            def body(i, first):
                for s in range(2):
                    j = 2 * i + s
                    pe.wait_ge(lo_done, j + 1)
                    if not first:
                        pe.wait_ge(gated, j - 1)
                    unit_matmuls(pe, psum[s], w_hi[s], w_lo[s], a_hi, a_lo,
                                 split=alo if first and s == 0 else None).then_inc(unit_mm, 1)
            pairs(pe, 0, tiles // 2, body)


def stage_out_proj(nc, ap, keep, sem):
    with ExitStack() as ctx:
        def sb(name, shape, dt=F32):
            return ctx.enter_context(nc.sbuf_tensor(name, shape, dt))
        mixed_hi, mixed_lo, ident = keep["mixed_hi"], keep["mixed_lo"], keep["ident"]
        hT_hi, hT_lo = mixed_hi, mixed_lo
        w_raw = [sb(f"wo_raw{k}", [P, D_MODEL]) for k in range(4)]
        w_hi, w_lo = sb("wo_hi", [P, KT, D_MODEL], F32R), sb("wo_lo", [P, KT, D_MODEL], F32R)
        x = [sb(f"res_x{s}", [P, D_MODEL]) for s in range(2)]
        h = sb("res_h", [P, D_MODEL])
        norm = sb("res_norm", [P, D_MODEL])
        w_post, w_pre = sb("w_post", [P, D_MODEL]), sb("w_pre", [P, D_MODEL])
        stat = sb("res_stats", [P, 2, 2])
        psum = [ctx.enter_context(nc.psum_tensor(f"wo_ps{s}", [P, D_MODEL], F32)) for s in range(2)]
        turned = [ctx.enter_context(nc.psum_tensor(f"wo_turned{s}", [P, D_MODEL], F32)) for s in range(2)]
        w_loaded = [sem(f"wo_loaded{k}") for k in range(4)]
        hi_done, lo_done, vec_loaded = sem("wo_hi_done"), sem("wo_lo_done"), sem("res_weights_loaded")
        x_loaded, x_stored = [sem(f"res_x_loaded{s}") for s in range(2)], [sem(f"x1_stored{s}") for s in range(2)]
        tile_mm, sum_done, mean_done, root_done, rstd_done = sem("wo_mm"), sem("res_sums"), sem("res_means"), sem("res_roots"), sem("res_rstds")
        normed, x1_done, h_done, turned_done = sem("res_normed"), sem("x1_done"), sem("res_h_done"), sem("res_turned")
        thi, tlo = sem("h2T_hi_done"), sem("h2T_lo_done")
        block = ctx.enter_context(nc.Block())

        @block.sync
        def _(sp):
            for k in range(KT):
                if k >= 4:
                    sp.wait_ge(lo_done, k - 3)
                sp.dma_start(w_raw[k % 4][:], ap["w_out"][k * P:(k + 1) * P, :]).then_inc(w_loaded[k % 4], 16)
                if k == 3:
                    sp.dma_start(w_post[:], ap["norm_mix_post"].partition_broadcast(P)).then_inc(vec_loaded, 16)
                    sp.dma_start(w_pre[:], ap["norm_mlp_pre"].partition_broadcast(P)).then_inc(vec_loaded, 16)
                    for s in range(2):
                        sp.dma_start(x[s][:], ap["x"][s * P:(s + 1) * P, :]).then_inc(x_loaded[s], 16)
            with sp.Fori(1, TT // 2) as i:
                for s in range(2):
                    sp.wait_ge(x_stored[s], 16 * i)
                    sp.dma_start(x[s][:], ap["x"][bass.ds((2 * i + s) * P, P), :]).then_inc(x_loaded[s], 16)

        @block.gpsimd
        def _(pool):
            def body(i, first):
                for s in range(2):
                    pool.wait_ge(h_done, 2 * i + s + 1)
                    pool.dma_start(ap["x1"][bass.ds((2 * i + s) * P, P), :], x[s][:]).then_inc(x_stored[s], 16)
            pairs(pool, 0, TT // 2, body)
            for s in range(2):
                pool.wait_ge(x_stored[s], 16 * (TT // 2))

        @block.scalar
        def _(act):
            for k in range(KT):
                act.wait_ge(w_loaded[k % 4], 16 * (k // 4 + 1))
                nc.scalar.activation(w_hi[:, k, :], w_raw[k % 4][:], ACT.Copy).then_inc(hi_done, 1)

            def body(i, first):
                for s in range(2):
                    t = 2 * i + s
                    for n in range(2):
                        if n == 0:
                            act.wait_ge(tile_mm, t + 1)
                            if not (first and s == 0):
                                act.wait_ge(turned_done, t)
                        else:
                            act.wait_ge(x1_done, t + 1)
                            act.wait_ge(sum_done, 2 * t + 1)
                        nc.scalar.activation(h[:], (psum[s] if n == 0 else x[s])[:], ACT.Square,
                                             accum_out=stat[:, s, n:n + 1]).then_inc(sum_done, 1)
                        act.wait_ge(mean_done, 2 * t + n + 1)
                        nc.scalar.activation(stat[:, s, n:n + 1], stat[:, s, n:n + 1], ACT.Sqrt).then_inc(root_done, 1)
                    act.wait_ge(turned_done, t + 1)
                    nc.scalar.activation(hT_hi[:, :, bass.ds(t * P, P)], turned[s][:].rearrange("p (k t) -> p k t", k=KT),
                                         ACT.Copy).then_inc(thi, 1)
            pairs(act, 0, TT // 2, body)

        @block.vector
        def _(dve):
            for k in range(KT):
                dve.wait_ge(hi_done, k + 1)
                nc.vector.tensor_tensor(w_lo[:, k, :], w_raw[k % 4][:], w_hi[:, k, :].bitcast(F32), ALU.subtract).then_inc(lo_done, 1)
            dve.wait_ge(vec_loaded, 32)

            def rstd(t, s, n):
                dve.wait_ge(sum_done, 2 * t + n + 1)
                cell = stat[:, s, n:n + 1]
                nc.vector.tensor_scalar(cell, cell, 1.0 / D_MODEL, EPS, ALU.mult, ALU.add).then_inc(mean_done, 1)
                dve.wait_ge(root_done, 2 * t + n + 1)
                nc.vector.reciprocal(cell, cell).then_inc(rstd_done, 1)
                dve.wait_ge(rstd_done, 2 * t + n + 1)
                return cell

            def body(i, first):
                for s in range(2):
                    t = 2 * i + s
                    cell = rstd(t, s, 0)
                    nc.vector.scalar_tensor_tensor(out=norm[:], in0=psum[s][:], scalar=cell, in1=w_post[:],
                                                   op0=ALU.mult, op1=ALU.mult).then_inc(normed, 1)
                    dve.wait_ge(normed, t + 1)
                    dve.wait_ge(x_loaded[s], 16 * i + 16)
                    nc.vector.tensor_tensor(x[s][:], x[s][:], norm[:], ALU.add).then_inc(x1_done, 1)
                    cell = rstd(t, s, 1)
                    nc.vector.scalar_tensor_tensor(out=h[:], in0=x[s][:], scalar=cell, in1=w_pre[:],
                                                   op0=ALU.mult, op1=ALU.mult).then_inc(h_done, 1)
                    dve.wait_ge(thi, t + 1)
                    ts = bass.ds(t * P, P)
                    nc.vector.tensor_tensor(hT_lo[:, :, ts], turned[s][:].rearrange("p (k t) -> p k t", k=KT),
                                            hT_hi[:, :, ts].bitcast(F32), ALU.subtract).then_inc(tlo, 1)
            pairs(dve, 0, TT // 2, body)

        @block.tensor
        def _(pe):
            def turn(t):
                pe.wait_ge(h_done, t + 1)
                if t >= 2:
                    pe.wait_ge(tlo, t - 1)
                for k in range(KT):
                    last = pe.transpose(turned[t % 2][:, k * P:(k + 1) * P], h[:, k * P:(k + 1) * P], ident[:])
                last.then_inc(turned_done, 1)

            for t in range(TT):
                ts = slice(t * P, (t + 1) * P)
                if t >= 2:
                    pe.wait_ge(normed, t - 1)
                for k in range(KT):
                    if t == 0:
                        pe.wait_ge(lo_done, k + 1)
                    for n, (m, w) in enumerate(((mixed_hi, w_hi), (mixed_hi, w_lo), (mixed_lo, w_hi))):
                        for half in range(2):
                            hs = slice(half * HALF, (half + 1) * HALF)
                            last = pe.matmul(psum[t % 2][:, hs], m[:, k, ts], w[:, k, hs], start=k == 0 and n == 0,
                                             stop=k == KT - 1 and n == 2)
                last.then_inc(tile_mm, 1)
                if t:
                    turn(t - 1)
            turn(TT - 1)


FG = D_FF // HALF
UPG = HALF // P


def stage_mlp(nc, ap, keep, sem):
    with ExitStack() as ctx:
        def sb(name, shape, dt=F32):
            return ctx.enter_context(nc.sbuf_tensor(name, shape, dt))

        def two(name, shape):
            return [sb(f"{name}{s}", shape, F32R) for s in range(2)]
        hT_hi, hT_lo, out_sum = keep["mixed_hi"], keep["mixed_lo"], keep["out_sum"]
        up_raw, dn_raw = sb("up_raw", [P, KT, P]), sb("down_raw", [P, UPG, 2 * P])
        up_hi, up_lo = two("up_hi", [P, KT, P]), two("up_lo", [P, KT, P])
        dn_hi, dn_lo = two("down_hi", [P, UPG, 2 * P]), two("down_lo", [P, UPG, 2 * P])
        square = sb("relu_squared", [P, SEQ])
        ff_hi, ff_lo = two("ff_hi", [P, UPG, SEQ]), two("ff_lo", [P, UPG, SEQ])
        ps_up = ctx.enter_context(nc.psum_tensor("ps_up", [P, SEQ], F32))
        ps_dn = [ctx.enter_context(nc.psum_tensor(f"ps_down{s}", [P, SEQ], F32)) for s in range(2)]
        up_loaded, dn_loaded = sem("up_loaded"), sem("down_loaded")
        up_hi_done, up_lo_done, dn_hi_done, dn_lo_done = sem("up_hi_done"), sem("up_lo_done"), sem("down_hi_done"), sem("down_lo_done")
        up_mm, dn_mm, relu_done, square_done = sem("up_mm"), sem("down_mm"), sem("relu_done"), sem("square_done")
        ffhi_done, fflo_done, added = sem("ff_hi_done"), sem("ff_lo_done"), sem("down_added")
        block = ctx.enter_context(nc.Block())

        def steps(engine, body):
            for g in range(2):
                for m in range(UPG):
                    body(g, g, m, m % 2)
            with engine.Fori(1, FG // 2 - 1) as i:
                for slot in range(2):
                    with engine.Fori(0, UPG // 2) as r:
                        for v in range(2):
                            body(2 * i + slot, slot, 2 * r + v, v)
            with engine.Fori(0, UPG // 2) as r:
                for v in range(2):
                    body(FG - 2, 0, 2 * r + v, v)
            for g in range(FG - 1, FG + 1):
                for m in range(UPG):
                    body(g, g % 2, m, m % 2)

        def going(g):
            return (not isinstance(g, int) or g < FG), (not isinstance(g, int) or g > 0)

        def after(g, m):
            return g + 1 if isinstance(g, int) and isinstance(m, int) and m == UPG - 1 else g

        def known(q, below):
            return isinstance(q, int) and q < below

        @block.sync
        def _(sp):
            def body(g, slot, m, v):
                up, down = going(g)
                q = g * UPG + m
                if up:
                    if not known(q, 1):
                        sp.wait_ge(up_lo_done, q)
                    sp.dma_start(up_raw[:], ap["w_up"][:, bass.ds(q * P, P)].rearrange("(k p) c -> p k c", p=P)).then_inc(up_loaded, 16)
                if down:
                    if not known(q, UPG + 1):
                        sp.wait_ge(dn_lo_done, q - UPG)
                    sp.dma_start(dn_raw[:], ap["w_down"].rearrange("(g r) c -> g r c", r=HALF)[bass.ds(g - 1, 1), :, bass.ds(m * 2 * P, 2 * P)]
                                 .rearrange("g (k p) c -> p (g k) c", p=P)).then_inc(dn_loaded, 16)
            steps(sp, body)

        @block.scalar
        def _(act):
            def split(q, v, up, down):
                if up:
                    act.wait_ge(up_loaded, 16 * q + 16)
                    if not known(q, 2):
                        act.wait_ge(up_mm, q - 1)
                    nc.scalar.activation(up_hi[v][:], up_raw[:], ACT.Copy).then_inc(up_hi_done, 1)
                if down:
                    act.wait_ge(dn_loaded, 16 * q + 16 - 16 * UPG)
                    if not known(q, UPG + 2):
                        act.wait_ge(dn_mm, 2 * q - 2 * UPG - 2)
                    nc.scalar.activation(dn_hi[v][:], dn_raw[:], ACT.Copy).then_inc(dn_hi_done, 1)

            split(0, 0, True, False)

            def body(g, slot, m, v):
                q = g * UPG + m
                if going(g)[0]:
                    act.wait_ge(up_mm, q + 1)
                    if not known(q, 1):
                        act.wait_ge(fflo_done, q)
                    nc.scalar.activation(square[:], ps_up[:], ACT.Relu).then_inc(relu_done, 1)
                    act.wait_ge(square_done, q + 1)
                    nc.scalar.activation(ff_hi[slot][:, bass.ds(m, 1), :], square[:].unsqueeze(1), ACT.Copy).then_inc(ffhi_done, 1)
                if not (known(g, FG + 1) and g == FG and m == UPG - 1):
                    split(q + 1, 1 - v, *going(after(g, m)))
            steps(act, body)

        @block.vector
        def _(dve):
            def split(q, v, up, down):
                if up:
                    dve.wait_ge(up_hi_done, q + 1)
                    nc.vector.tensor_tensor(up_lo[v][:], up_raw[:], up_hi[v][:].bitcast(F32), ALU.subtract).then_inc(up_lo_done, 1)
                if down:
                    dve.wait_ge(dn_hi_done, q + 1 - UPG)
                    nc.vector.tensor_tensor(dn_lo[v][:], dn_raw[:], dn_hi[v][:].bitcast(F32), ALU.subtract).then_inc(dn_lo_done, 1)

            def add(g, m, s):
                n = 2 * ((g - 1) * UPG + m) + s
                dve.wait_ge(dn_mm, n + 1)
                total = out_sum[:, bass.ds(m * 2 + s, 1), :]
                if isinstance(g, int) and g == 1:
                    nc.vector.tensor_copy(total, ps_dn[s][:].unsqueeze(1)).then_inc(added, 1)
                else:
                    dve.wait_ge(added, n - 2 * UPG + 1)
                    nc.vector.tensor_tensor(total, total, ps_dn[s][:].unsqueeze(1), ALU.add).then_inc(added, 1)

            split(0, 0, True, False)

            def body(g, slot, m, v):
                q = g * UPG + m
                up, down = going(g)
                if up:
                    dve.wait_ge(relu_done, q + 1)
                    nc.vector.tensor_tensor(square[:], square[:], square[:], ALU.mult).then_inc(square_done, 1)
                    dve.wait_ge(ffhi_done, q + 1)
                    nc.vector.tensor_tensor(ff_lo[slot][:, bass.ds(m, 1), :], square[:].unsqueeze(1),
                                            ff_hi[slot][:, bass.ds(m, 1), :].bitcast(F32), ALU.subtract).then_inc(fflo_done, 1)
                if down:
                    add(g, m, 0)
                if not (known(g, FG + 1) and g == FG and m == UPG - 1):
                    split(q + 1, 1 - v, *going(after(g, m)))
                if down:
                    add(g, m, 1)
            steps(dve, body)

        @block.tensor
        def _(pe):
            def body(g, slot, m, v):
                q = g * UPG + m
                up, down = going(g)
                if up:
                    pe.wait_ge(up_lo_done, q + 1)
                    if not known(q, 1):
                        pe.wait_ge(relu_done, q)
                    unit_matmuls(pe, ps_up, up_hi[v], up_lo[v], hT_hi, hT_lo).then_inc(up_mm, 1)
                if down:
                    pe.wait_ge(dn_lo_done, q + 1 - UPG)
                    pe.wait_ge(fflo_done, g * UPG)
                    for s in range(2):
                        if not known(q, UPG + 1):
                            pe.wait_ge(added, 2 * (q - UPG) + s - 1)
                        cs = slice(s * P, (s + 1) * P)
                        unit_matmuls(pe, ps_dn[s], dn_hi[v][:, :, cs], dn_lo[v][:, :, cs], ff_hi[1 - slot], ff_lo[1 - slot],
                                     kt=UPG).then_inc(dn_mm, 1)
            steps(pe, body)


def stage_last(nc, ap, keep, sem):
    with ExitStack() as ctx:
        def sb(name, shape, dt=F32):
            return ctx.enter_context(nc.sbuf_tensor(name, shape, dt))
        out_sum, ident = keep["out_sum"], keep["ident"]
        x = [sb(f"last_x{s}", [P, D_MODEL]) for s in range(TT)]
        junk = sb("last_squares", [P, D_MODEL])
        w_post = sb("last_w", [P, D_MODEL])
        norm = [sb(f"last_norm{s}", [P, D_MODEL]) for s in range(2)]
        stat = sb("last_stats", [P, TT])
        root = sb("last_roots", [P, TT])
        turned = [ctx.enter_context(nc.psum_tensor(f"last_turned{s}", [P, D_MODEL], F32)) for s in range(4)]
        loaded, w_loaded, stored = sem("last_x_loaded"), sem("last_w_loaded"), sem("out_stored")
        turned_done, sum_done, mean_done, root_done, rstd_done = sem("last_turned"), sem("last_sums"), sem("last_means"), sem("last_roots"), sem("last_rstds")
        normed, added = sem("last_normed"), sem("last_added")
        block = ctx.enter_context(nc.Block())

        @block.sync
        def _(sp):
            sp.dma_start(w_post[:], ap["norm_mlp_post"].partition_broadcast(P)).then_inc(w_loaded, 16)
            for t in range(TT):
                sp.dma_start(x[t][:], ap["x1"][t * P:(t + 1) * P, :]).then_inc(loaded, 16)
            for t in range(TT):
                sp.wait_ge(added, t + 1)
                sp.dma_start(ap["out"][t * P:(t + 1) * P, :], x[t][:]).then_inc(stored, 16)
            sp.wait_ge(stored, 16 * TT)

        @block.scalar
        def _(act):
            for t in range(TT):
                act.wait_ge(turned_done, t + 1)
                if t:
                    act.wait_ge(sum_done, t)
                nc.scalar.activation(junk[:], turned[t % 4][:], ACT.Square, accum_out=stat[:, t:t + 1]).then_inc(sum_done, 1)
                act.wait_ge(mean_done, t + 1)
                nc.scalar.activation(root[:, t:t + 1], stat[:, t:t + 1], ACT.Sqrt).then_inc(root_done, 1)

        @block.vector
        def _(dve):
            dve.wait_ge(w_loaded, 16)
            dve.wait_ge(loaded, 16 * TT)
            for t in range(TT):
                cell = stat[:, t:t + 1]
                dve.wait_ge(sum_done, t + 1)
                nc.vector.tensor_scalar(cell, cell, 1.0 / D_MODEL, EPS, ALU.mult, ALU.add).then_inc(mean_done, 1)
                dve.wait_ge(root_done, t + 1)
                nc.vector.reciprocal(root[:, t:t + 1], root[:, t:t + 1]).then_inc(rstd_done, 1)
                dve.wait_ge(rstd_done, t + 1)
                if t >= 2:
                    dve.wait_ge(added, t - 1)
                nc.vector.scalar_tensor_tensor(out=norm[t % 2][:], in0=turned[t % 4][:], scalar=root[:, t:t + 1], in1=w_post[:],
                                               op0=ALU.mult, op1=ALU.mult).then_inc(normed, 1)
                dve.wait_ge(normed, t + 1)
                nc.vector.tensor_tensor(x[t][:], x[t][:], norm[t % 2][:], ALU.add).then_inc(added, 1)

        @block.tensor
        def _(pe):
            for t in range(TT):
                if t >= 4:
                    pe.wait_ge(normed, t - 3)
                for k in range(KT):
                    last = pe.transpose(turned[t % 4][:, k * P:(k + 1) * P], out_sum[:, k, t * P:(t + 1) * P], ident[:])
                last.then_inc(turned_done, 1)


def build(nc, ap):
    with ExitStack() as ctx:
        attended = ctx.enter_context(ExitStack())

        def sb(name, shape, dt=F32, scope=ctx, side=None):
            return scope.enter_context(nc.sbuf_tensor(name, shape, dt, side=side))

        used = []

        def sem(name):
            used.append(nc.alloc_semaphore(name=name))
            return used[-1]

        def clear_semaphores():
            nc.clear_and_free_semaphores(used)
            used.clear()
            nc.all_engine_barrier()

        keep = {"ident": sb("ident", [P, P]), "vec": sb("vec", [P, V_N])}
        with ExitStack() as mid:
            keep |= {
                "trig": sb("trig", [P, SEQ], scope=mid),
                "lat": sb("latents", [P, 4, SEQ], scope=mid),
                "kpe": sb("rope_key", [P, SEQ], scope=mid),
                "dt_tok": sb("dt_tok", [P, TT * 2 * HEADS], scope=mid),
                "la_tok": sb("la_tok", [P, TT * 2 * HEADS], scope=mid),
            }
            with ExitStack() as inner:
                keep["kraw"] = sb("rope_key_raw", [2 * ROPE, SEQ], scope=inner)
                keep["hT_hi"] = sb("hT_hi", [P, KT, SEQ], F32R, scope=inner)
                keep["hT_lo"] = sb("hT_lo", [P, KT, SEQ], F32R, scope=inner)
                stage_norm_in(nc, ap, keep, sem)
                stage_in_proj(nc, ap, keep, sem)
            stage_ssd(nc, ap, keep, sem)
            with ExitStack() as yt:
                keep["yT_hi"] = sb("yT_hi", [P, YT, SEQ], F32R, scope=yt)
                keep["yT_lo"] = sb("yT_lo", [P, YT, SEQ], F32R, scope=yt)
                stage_gate_y(nc, ap, keep, sem)
                stage_ssm_out(nc, ap, keep, sem)
            clear_semaphores()
            keep["attn"] = sb("attn", [P, KT, SEQ], scope=attended, side="right")
            stage_attention(nc, ap, keep, sem)
        with ExitStack() as merged:
            keep["mixed_hi"] = sb("mixed_hi", [P, KT, SEQ], F32R, scope=merged)
            keep["mixed_lo"] = sb("mixed_lo", [P, KT, SEQ], F32R, scope=merged)
            stage_merge(nc, ap, keep, sem)
            attended.close()
            stage_out_proj(nc, ap, keep, sem)
            keep["out_sum"] = sb("out_sum", [P, KT, SEQ], scope=ctx, side="right")
            stage_mlp(nc, ap, keep, sem)
        stage_last(nc, ap, keep, sem)


SCRATCH = {"gates": (2 * D_MODEL, SEQ), "CT": (GROUPS * N_STATE, SEQ), "BT": (GROUPS * N_STATE, SEQ),
           "tok": (SEQ, TOK_W), "la": (2 * HEADS, SEQ), "ends": (2 * HEADS, TT), "y": (SEQ, D_INNER),
           "sums": (A_HEADS, SEQ), "recip": (A_HEADS, SEQ), "mixed": (D_MODEL, SEQ), "x1": (SEQ, D_MODEL)}


def host_layout(inputs):
    a = {k: np.ascontiguousarray(np.asarray(v)[0]) for k, v in inputs.items()}
    w_in = a["w_in"]
    vec = np.zeros((P, V_N), np.float32)
    def cols(at, x):
        x = x.reshape(-1, P).T
        vec[:, at:at + x.shape[1]] = x
    vec[:, V_CONVW:V_CONVB] = a["conv_w"].reshape(TAPS, 32, P).transpose(2, 1, 0).reshape(P, -1)
    cols(V_CONVB, a["conv_b"])
    cols(V_GATEB, a["gate_b"])
    cols(V_QN, a["q_a_norm"])
    cols(V_KVN, a["kv_a_norm"])
    vec[:2 * HEADS, V_DTB] = np.concatenate([a["dt_bias_fwd"], a["dt_bias_bwd"]])
    vec[:2 * HEADS, V_ALOG] = np.concatenate([a["a_log_fwd"], a["a_log_bwd"]])
    freq = (np.float32(10000.0) ** (-np.arange(0, ROPE, 2, dtype=np.float32) / np.float32(ROPE))).astype(np.float32)
    vec[:, V_FREQ] = np.tile(freq, P // len(freq))
    vec[:, V_SIGN] = np.tile(np.repeat(np.float32([-1, 1]), ROPE // 2), P // ROPE)
    rope = w_in[:, COL_ROPE:COL_ROPE + ROPE]
    wq = a["w_q_b"].reshape(QR, A_HEADS, QK)
    out = {
        "x": a["x"], "positions": a["positions"], "norm_mix_pre": a["norm_mix_pre"], "w_in": w_in, "vec": vec,
        "w_rope": np.concatenate([rope, rope[:, ROPE // 2:], rope[:, :ROPE // 2], np.zeros((D_MODEL, 64), np.float32)], 1),
        "w_q": np.concatenate([wq, wq[:, :, QK - ROPE // 2:], wq[:, :, NOPE:NOPE + ROPE // 2]], 2).reshape(QR, A_HEADS * P),
    }
    for n in ("d_skip", "ssm_norm_w", "w_ssm_out", "w_kv_b", "w_mla_out", "w_out", "norm_mix_post", "norm_mlp_pre",
              "w_up", "w_down", "norm_mlp_post"):
        out[n] = a[n]
    return {k: np.ascontiguousarray(v) for k, v in out.items()}


def kernel(**inputs):
    import concourse.bacc as bacc
    from concourse.bass_utils import run_bass_kernel_spmd

    arrays = host_layout(inputs)
    nc = bacc.Bacc("TRN2", target_bir_lowering=False, num_devices=1)
    ap = {k: nc.dram_tensor(f"in_{k}", a.shape, mybir.dt.from_np(a.dtype), kind="ExternalInput").ap() for k, a in arrays.items()}
    ap |= {k: nc.dram_tensor(f"scratch_{k}", s, F32, kind="Internal").ap() for k, s in SCRATCH.items()}
    ap["out"] = nc.dram_tensor("out", (SEQ, D_MODEL), F32, kind="ExternalOutput").ap()
    build(nc, ap)
    got = run_bass_kernel_spmd(nc, [{f"in_{k}": a for k, a in arrays.items()}], core_ids=[0])
    return got.results[0]["out"].reshape(1, SEQ, D_MODEL)
```
